# Optimizing a Trainium2 kernel written in Bass

```python
import math
import jax
import jax.numpy as jnp
from jax import lax
import numpy as np
import jax, jax.numpy as jnp

D_MODEL = 1024
BATCH = 1
SEQ = 256
DEPTH = 1

GRID_W = 64
CTX_LEN = 256
N_MIXERS = 3
MIX_SHORTCONV = 0
MIX_HYENA = 1
MIX_ATTN = 2
CONV_W = 3
EPS = 1e-6
HY_ORDER = 2
HY_EMB = 33
HY_BANDS = (HY_EMB - 1) // 2
HY_FILTER_HIDDEN = 64
HY_FAST_DECAY = 0.3
HY_SLOW_DECAY = 1.5
HY_TARGET = 1e-2
HEAD_DIM = 128
N_Q_HEADS = D_MODEL // HEAD_DIM
N_KV_HEADS = 2
Q_PER_KV = N_Q_HEADS // N_KV_HEADS
AXIS_DIM = HEAD_DIM // 2
ROPE_THETA = 10000.0
Q_BLOCK = 128
N_EXPERTS = 16
EC_CAPACITY_FACTOR = 2
D_EXPERT = D_MODEL


def _layers_of(kind):
    return list(range(kind, DEPTH, N_MIXERS))

def rms_norm(x, g):
    xf = x.astype(jnp.float32)
    y = xf * lax.rsqrt(jnp.mean(xf * xf, axis=-1, keepdims=True) + EPS)
    return (y * g.astype(jnp.float32)).astype(x.dtype)

def modulate(x, shift, scale):
    return x * (1.0 + scale) + shift

def dwconv_centred(x, w):
    L = x.shape[1]
    p = CONV_W // 2
    xp = jnp.pad(x, ((0, 0), (p, p), (0, 0)))
    y = xp[:, 0:L] * w[0]
    for k in range(1, CONV_W):
        y = y + xp[:, k:k + L] * w[k]
    return y

def short_conv_mixer(h, w_in, conv_w, w_out):
    gate_b, gate_c, v = jnp.split(h @ w_in, 3, axis=-1)
    return (gate_b * dwconv_centred(gate_c * v, conv_w)) @ w_out

def hyena_filter_spectrum(L, w1, b1, w2, b2, w3, sin_freq):
    f32 = jnp.float32
    t = jnp.linspace(0.0, 1.0, L, dtype=f32)[:, None]
    bands = jnp.linspace(1e-4, HY_BANDS - 1, HY_BANDS, dtype=f32)[None, :]
    ang = (2.0 * math.pi / L) * jnp.arange(L, dtype=f32)[:, None] * bands
    z = jnp.concatenate([t, jnp.cos(ang), -jnp.sin(ang)], axis=-1)
    freq = sin_freq.astype(f32)
    a = jnp.sin(freq * (z @ w1.astype(f32) + b1.astype(f32)))
    a = jnp.sin(freq * (a @ w2.astype(f32) + b2.astype(f32)))
    h = (a @ w3.astype(f32)).reshape(L, 2, HY_ORDER, D_MODEL)
    deltas = jnp.abs(jnp.linspace(math.log(HY_TARGET) / HY_SLOW_DECAY,
                                  math.log(HY_TARGET) / HY_FAST_DECAY, D_MODEL, dtype=f32))
    h = h * jnp.exp(-t * deltas[None, :])[:, None, None, :]
    fwd = h[:, 0]
    bwd = h[1:, 1][::-1]
    full = jnp.concatenate([fwd, jnp.zeros((1, HY_ORDER, D_MODEL), f32), bwd], axis=0)
    full = full / jnp.sum(jnp.abs(full), axis=0, keepdims=True)
    return jnp.fft.rfft(full, axis=0)

def long_conv(u, filt_f, skip):
    L = u.shape[1]
    uf = u.astype(jnp.float32)
    y = jnp.fft.irfft(jnp.fft.rfft(uf, n=2 * L, axis=1) * filt_f[None], n=2 * L, axis=1)[:, :L]
    return (y + uf * skip.astype(jnp.float32)).astype(u.dtype)

def hyena_mixer(h, w_in, conv_w, f_w1, f_b1, f_w2, f_b2, f_w3, sin_freq, skip, w_out):
    L = h.shape[1]
    parts = jnp.split(dwconv_centred(h @ w_in, conv_w), HY_ORDER + 1, axis=-1)
    z, gates = parts[0], parts[1:]
    filt = hyena_filter_spectrum(L, f_w1, f_b1, f_w2, f_b2, f_w3, sin_freq)
    for o in range(HY_ORDER):
        z = gates[o] * long_conv(z, filt[:, o], skip[o])
    return z @ w_out

def axial_rope_tables(n_tokens, dtype):
    f32 = jnp.float32
    rows = n_tokens // GRID_W
    row = jnp.repeat(jnp.arange(rows, dtype=f32), GRID_W)
    col = jnp.tile(jnp.arange(GRID_W, dtype=f32), rows)
    inv = ROPE_THETA ** (-jnp.arange(0, AXIS_DIM, 2, dtype=f32) / AXIS_DIM)

    def axis_angles(pos):
        a = pos[:, None] * inv[None, :]
        return jnp.concatenate([a, a], axis=-1)

    ang = jnp.concatenate([axis_angles(row), axis_angles(col)], axis=-1)
    return jnp.cos(ang).astype(dtype), jnp.sin(ang).astype(dtype)

def _rotate_axial(x):
    q = AXIS_DIM // 2
    xr, xc = x[..., :AXIS_DIM], x[..., AXIS_DIM:]
    return jnp.concatenate([-xr[..., q:], xr[..., :q], -xc[..., q:], xc[..., :q]], axis=-1)

def apply_rope(x, cos, sin):
    return x * cos + _rotate_axial(x) * sin

def _attend(q, k, v):
    s = jnp.einsum('bqkgd,bskd->bkgqs', q, k, preferred_element_type=jnp.float32) * (HEAD_DIM ** -0.5)
    p = jax.nn.softmax(s, axis=-1)
    return jnp.einsum('bkgqs,bskd->bqkgd', p.astype(v.dtype), v)

def gqa_mixer(h_lat, h_ctx, w_qkv, q_g, k_g, w_o, ctx_out):
    B, L, _ = h_lat.shape
    Lc = h_ctx.shape[1]
    QD = N_Q_HEADS * HEAD_DIM
    KVD = N_KV_HEADS * HEAD_DIM

    def heads_q(t, n):
        return rms_norm(t.reshape(B, n, N_KV_HEADS, Q_PER_KV, HEAD_DIM), q_g)

    def heads_kv(t, n):
        k = rms_norm(t[..., :KVD].reshape(B, n, N_KV_HEADS, HEAD_DIM), k_g)
        v = t[..., KVD:].reshape(B, n, N_KV_HEADS, HEAD_DIM)
        return k, v

    qkv_l = h_lat @ w_qkv
    q_l = heads_q(qkv_l[..., :QD], L)
    k_l, v_l = heads_kv(qkv_l[..., QD:], L)
    cos, sin = axial_rope_tables(L, q_l.dtype)
    q_l = apply_rope(q_l, cos[None, :, None, None], sin[None, :, None, None])
    k_l = apply_rope(k_l, cos[None, :, None], sin[None, :, None])
    if ctx_out:
        qkv_c = h_ctx @ w_qkv
        q_c = heads_q(qkv_c[..., :QD], Lc)
        kv_c = qkv_c[..., QD:]
    else:
        kv_c = h_ctx @ w_qkv[:, QD:]
    k_c, v_c = heads_kv(kv_c, Lc)

    k_all = jnp.concatenate([k_c, k_l], axis=1)
    v_all = jnp.concatenate([v_c, v_l], axis=1)
    n_blk = L // Q_BLOCK
    qb = jnp.moveaxis(q_l.reshape(B, n_blk, Q_BLOCK, N_KV_HEADS, Q_PER_KV, HEAD_DIM), 1, 0)
    o_l = lax.map(lambda qblk: _attend(qblk, k_all, v_all), qb)
    y_l = jnp.moveaxis(o_l, 0, 1).reshape(B, L, QD) @ w_o
    y_c = _attend(q_c, k_c, v_c).reshape(B, Lc, QD) @ w_o if ctx_out else None
    return y_l, y_c

def expert_choice_ffn(h, w_router, w_gate, w_up, w_down):
    B, N, D = h.shape
    cap = EC_CAPACITY_FACTOR * N // N_EXPERTS
    aff = jax.nn.softmax((h @ w_router).astype(jnp.float32), axis=-1)
    g, idx = lax.top_k(jnp.swapaxes(aff, 1, 2), cap)
    xs = jax.vmap(lambda hb, ib: hb[ib])(h, idx)
    hid = jax.nn.silu(jnp.einsum('becd,edf->becf', xs, w_gate)) * jnp.einsum('becd,edf->becf', xs, w_up)
    ys = jnp.einsum('becf,efd->becd', hid, w_down) * g[..., None].astype(h.dtype)
    return jax.vmap(lambda yb, ib: jnp.zeros((N, D), yb.dtype).at[ib.reshape(-1)].add(yb.reshape(-1, D)))(ys, idx)

def first_inputs(seed: int = 0) -> dict:
    key = jax.random.key(seed)
    ks = iter(jax.random.split(key, 40))
    D, F = D_MODEL, D_EXPERT
    nA, nB, nC = (len(_layers_of(k)) for k in range(N_MIXERS))
    QKV = (N_Q_HEADS + 2 * N_KV_HEADS) * HEAD_DIM

    def nrm(shape, s):
        return jax.random.normal(next(ks), shape, jnp.float32) * s

    return {
        "x": nrm((BATCH, SEQ, D), 1.0),
        "c": nrm((BATCH, D), 1.0),
        "ctx": nrm((BATCH, CTX_LEN, D), 1.0),
        "c_ctx": nrm((D,), 1.0),
        "ada_w": nrm((DEPTH, D, 6 * D), 0.5 * D ** -0.5),
        "ada_b": nrm((DEPTH, 6 * D), 0.01),
        "norm_g": 1.0 + nrm((DEPTH, 2, D), 0.02),
        "sc_w_in": nrm((nA, D, 3 * D), D ** -0.5),
        "sc_conv": nrm((nA, CONV_W, D), CONV_W ** -0.5),
        "sc_w_out": nrm((nA, D, D), D ** -0.5),
        "hy_w_in": nrm((nB, D, (HY_ORDER + 1) * D), D ** -0.5),
        "hy_conv": nrm((nB, CONV_W, (HY_ORDER + 1) * D), CONV_W ** -0.5),
        "hy_f_w1": nrm((nB, HY_EMB, HY_FILTER_HIDDEN), HY_EMB ** -0.5),
        "hy_f_b1": nrm((nB, HY_FILTER_HIDDEN), 0.02),
        "hy_f_w2": nrm((nB, HY_FILTER_HIDDEN, HY_FILTER_HIDDEN), HY_FILTER_HIDDEN ** -0.5),
        "hy_f_b2": nrm((nB, HY_FILTER_HIDDEN), 0.02),
        "hy_f_w3": nrm((nB, HY_FILTER_HIDDEN, 2 * HY_ORDER * D), HY_FILTER_HIDDEN ** -0.5),
        "hy_sin_freq": 1.0 + nrm((nB, HY_FILTER_HIDDEN), 0.02),
        "hy_skip": nrm((nB, HY_ORDER, D), 1.0),
        "hy_w_out": nrm((nB, D, D), D ** -0.5),
        "at_w_qkv": nrm((nC, D, QKV), D ** -0.5),
        "at_q_g": 1.0 + nrm((nC, HEAD_DIM), 0.02),
        "at_k_g": 1.0 + nrm((nC, HEAD_DIM), 0.02),
        "at_w_o": nrm((nC, N_Q_HEADS * HEAD_DIM, D), (N_Q_HEADS * HEAD_DIM) ** -0.5),
        "moe_router": nrm((DEPTH, D, N_EXPERTS), D ** -0.5),
        "moe_w_gate": nrm((DEPTH, N_EXPERTS, D, F), D ** -0.5),
        "moe_w_up": nrm((DEPTH, N_EXPERTS, D, F), D ** -0.5),
        "moe_w_down": nrm((DEPTH, N_EXPERTS, F, D), F ** -0.5),
    }

def first_block(x, c, ctx, c_ctx, ada_w, ada_b, norm_g, sc_w_in, sc_conv, sc_w_out,
              hy_w_in, hy_conv, hy_f_w1, hy_f_b1, hy_f_w2, hy_f_b2, hy_f_w3, hy_sin_freq, hy_skip, hy_w_out,
              at_w_qkv, at_q_g, at_k_g, at_w_o, moe_router, moe_w_gate, moe_w_up, moe_w_down):
    last_attn = max(_layers_of(MIX_ATTN), default=-1)
    lat, cx = x, ctx
    silu_c = jax.nn.silu(c)
    silu_cc = jax.nn.silu(c_ctx)
    for i in range(DEPTH):
        kind = i % N_MIXERS
        j = i // N_MIXERS
        need_ctx = i <= last_attn
        upd_ctx = i < last_attn

        m_l = (silu_c @ ada_w[i] + ada_b[i])[:, None, :]
        sh1, sc1, g1, sh2, sc2, g2 = jnp.split(m_l, 6, axis=-1)
        hl = modulate(rms_norm(lat, norm_g[i, 0]), sh1, sc1)
        if need_ctx:
            m_c = silu_cc @ ada_w[i] + ada_b[i]
            csh1, csc1, cg1, csh2, csc2, cg2 = jnp.split(m_c, 6, axis=-1)
            hc = modulate(rms_norm(cx, norm_g[i, 0]), csh1, csc1)

        yc = None
        if kind == MIX_SHORTCONV:
            yl = short_conv_mixer(hl, sc_w_in[j], sc_conv[j], sc_w_out[j])
            if upd_ctx:
                yc = short_conv_mixer(hc, sc_w_in[j], sc_conv[j], sc_w_out[j])
        elif kind == MIX_HYENA:
            hy_args = (hy_w_in[j], hy_conv[j], hy_f_w1[j], hy_f_b1[j], hy_f_w2[j], hy_f_b2[j],
                       hy_f_w3[j], hy_sin_freq[j], hy_skip[j], hy_w_out[j])
            yl = hyena_mixer(hl, *hy_args)
            if upd_ctx:
                yc = hyena_mixer(hc, *hy_args)
        else:
            yl, yc = gqa_mixer(hl, hc, at_w_qkv[j], at_q_g[j], at_k_g[j], at_w_o[j], upd_ctx)

        lat = lat + g1 * yl
        hl2 = modulate(rms_norm(lat, norm_g[i, 1]), sh2, sc2)
        lat = lat + g2 * expert_choice_ffn(hl2, moe_router[i], moe_w_gate[i], moe_w_up[i], moe_w_down[i])
        if upd_ctx:
            cx = cx + cg1 * yc
            hc2 = modulate(rms_norm(cx, norm_g[i, 1]), csh2, csc2)
            cx = cx + cg2 * expert_choice_ffn(hc2, moe_router[i], moe_w_gate[i], moe_w_up[i], moe_w_down[i])
    return lat


POOL_WIDTH = D_MODEL // 2
POOL_WINDOWS = (2, 4, 8, 16)
POOL_GROUPS = len(POOL_WINDOWS)
POOL_GROUP_DIM = POOL_WIDTH // POOL_GROUPS
HEAD_DIM_2 = 64
ATTN_WIDTH = D_MODEL - POOL_WIDTH
ATTN_HEADS = ATTN_WIDTH // HEAD_DIM_2
MIX_WIDTH = POOL_WIDTH + ATTN_WIDTH
MOBA_BLOCK = 256
MOBA_TOPK = 3
Q_CHUNK = 128
MEM_LEN = 256
XATTN_HEADS = 4
XATTN_HEAD_DIM = D_MODEL // XATTN_HEADS
D_FF = 2816
CONV_WIDTH = 3


def _rms_norm(x, g):
    xf = x.astype(jnp.float32)
    y = xf * lax.rsqrt(jnp.mean(xf * xf, axis=-1, keepdims=True) + EPS)
    return (y * g.astype(jnp.float32)).astype(x.dtype)

def _rope(x, pos):
    half = HEAD_DIM_2 // 2
    inv_freq = ROPE_THETA ** (-jnp.arange(half, dtype=jnp.float32) / half)
    ang = pos.astype(jnp.float32)[:, None] * inv_freq[None, :]
    cos = jnp.cos(ang).astype(x.dtype)
    sin = jnp.sin(ang).astype(x.dtype)
    x1, x2 = x[..., :half], x[..., half:]
    return jnp.concatenate([x1 * cos - x2 * sin, x2 * cos + x1 * sin], axis=-1)

def _pool_mixer(u, pool_w, pool_scale):
    B, S, _ = u.shape
    uf = u.astype(jnp.float32)
    cs = jnp.cumsum(uf, axis=1)
    t = jnp.arange(S)
    outs = []
    for g, w in enumerate(POOL_WINDOWS):
        sl = slice(g * POOL_GROUP_DIM, (g + 1) * POOL_GROUP_DIM)
        c = cs[..., sl]
        c_prev = jnp.pad(c, ((0, 0), (w, 0), (0, 0)))[:, :S]
        cnt = jnp.minimum(t + 1, w).astype(jnp.float32)
        outs.append((c - c_prev) / cnt[None, :, None] - uf[..., sl])
    pooled = jnp.stack(outs, axis=2).astype(u.dtype)
    mixed = jnp.einsum('bsgc,gcd->bsgd', pooled, pool_w)
    return mixed.reshape(B, S, POOL_WIDTH) * pool_scale

def _moba_attention(q, k, v):
    B, H, S, Dh = q.shape
    n_blocks = max(-(-S // MOBA_BLOCK), MOBA_TOPK)
    pad = n_blocks * MOBA_BLOCK - S
    kb = jnp.pad(k, ((0, 0), (0, 0), (0, pad), (0, 0))).reshape(B, H, n_blocks, MOBA_BLOCK, Dh)
    vb = jnp.pad(v, ((0, 0), (0, 0), (0, pad), (0, 0))).reshape(B, H, n_blocks, MOBA_BLOCK, Dh)
    k_mean = jnp.mean(kb.astype(jnp.float32), axis=3).astype(k.dtype)
    n_chunks = S // Q_CHUNK
    qc = q.reshape(B, H, n_chunks, Q_CHUNK, Dh).transpose(0, 2, 1, 3, 4)
    scale = HEAD_DIM_2 ** -0.5
    h_idx = jnp.arange(H)[:, None, None]
    blk_ids = jnp.arange(n_blocks)
    slot_ids = jnp.arange(MOBA_TOPK)
    n_sel = MOBA_TOPK * MOBA_BLOCK

    def chunk_fn(q_c, c, kb_b, vb_b, km_b):
        q0 = c * Q_CHUNK
        qblk = q0 // MOBA_BLOCK
        q_pos = q0 + jnp.arange(Q_CHUNK)
        gate = jnp.einsum('hqd,hnd->hqn', q_c, km_b, preferred_element_type=jnp.float32)
        gate = jnp.where(blk_ids[None, None, :] < qblk, gate, -jnp.inf)
        _, sel = lax.top_k(gate, MOBA_TOPK)
        k_sel = kb_b[h_idx, sel]
        v_sel = vb_b[h_idx, sel]
        s_sel = jnp.einsum('hqd,hqkjd->hqkj', q_c, k_sel, preferred_element_type=jnp.float32) * scale
        s_sel = jnp.where((slot_ids < qblk)[None, None, :, None], s_sel, -jnp.inf)
        k_own = lax.dynamic_index_in_dim(kb_b, qblk, axis=1, keepdims=False)
        v_own = lax.dynamic_index_in_dim(vb_b, qblk, axis=1, keepdims=False)
        s_own = jnp.einsum('hqd,hjd->hqj', q_c, k_own, preferred_element_type=jnp.float32) * scale
        k_pos = qblk * MOBA_BLOCK + jnp.arange(MOBA_BLOCK)
        s_own = jnp.where((k_pos[None, :] <= q_pos[:, None])[None], s_own, -jnp.inf)
        scores = jnp.concatenate([s_sel.reshape(H, Q_CHUNK, n_sel), s_own], axis=-1)
        p = jax.nn.softmax(scores, axis=-1).astype(v_sel.dtype)
        p_sel = p[..., :n_sel].reshape(H, Q_CHUNK, MOBA_TOPK, MOBA_BLOCK)
        p_own = p[..., n_sel:]
        return (jnp.einsum('hqkj,hqkjd->hqd', p_sel, v_sel)
                + jnp.einsum('hqj,hjd->hqd', p_own, v_own))

    def batch_fn(args):
        q_b, kb_b, vb_b, km_b = args
        return lax.map(lambda a: chunk_fn(a[0], a[1], kb_b, vb_b, km_b),
                       (q_b, jnp.arange(n_chunks)))

    out = lax.map(batch_fn, (qc, kb, vb, k_mean))
    return out.transpose(0, 2, 1, 3, 4).reshape(B, H, S, Dh)

def _cross_attention(h, m, w_xq, w_xkv, xq_norm_g, xk_norm_g, w_xo):
    B, S, _ = h.shape
    M = m.shape[1]
    q = (h @ w_xq).reshape(B, S, XATTN_HEADS, XATTN_HEAD_DIM)
    kv = (m @ w_xkv).reshape(B, M, 2, XATTN_HEADS, XATTN_HEAD_DIM)
    k, v = kv[:, :, 0], kv[:, :, 1]
    q = _rms_norm(q, xq_norm_g)
    k = _rms_norm(k, xk_norm_g)
    s = jnp.einsum('bshd,bmhd->bhsm', q, k, preferred_element_type=jnp.float32) * (XATTN_HEAD_DIM ** -0.5)
    p = jax.nn.softmax(s, axis=-1).astype(v.dtype)
    o = jnp.einsum('bhsm,bmhd->bshd', p, v).reshape(B, S, D_MODEL)
    return o @ w_xo

def _conv_ffn(h, w_up, conv_w, conv_b, w_down):
    up = h @ w_up
    C = up.shape[-1]
    rhs = conv_w.reshape(CONV_WIDTH, 1, C).astype(up.dtype)
    up = lax.conv_general_dilated(up, rhs, window_strides=(1,), padding=[(CONV_WIDTH - 1, 0)],
                                  dimension_numbers=('NWC', 'WIO', 'NWC'),
                                  feature_group_count=C) + conv_b
    gate, val = up[..., :D_FF], up[..., D_FF:]
    return (jax.nn.silu(gate) * val) @ w_down

def second_inputs(seed: int = 0) -> dict:
    key = jax.random.key(seed)
    ks = jax.random.split(key, 24)
    f32 = jnp.float32

    def nrm(k, shape, scale):
        return jax.random.normal(k, shape, f32) * scale

    def gain(k, shape):
        return 1.0 + 0.1 * jax.random.normal(k, shape, f32)

    L = DEPTH
    return {
        'x': jax.random.normal(ks[0], (BATCH, SEQ, D_MODEL), f32),
        'mem': jax.random.normal(ks[1], (BATCH, MEM_LEN, D_MODEL), f32),
        'norm_mix_g': gain(ks[2], (L, D_MODEL)),
        'w_in': nrm(ks[3], (L, D_MODEL, POOL_WIDTH + 3 * ATTN_WIDTH), D_MODEL ** -0.5),
        'pool_w': nrm(ks[4], (L, POOL_GROUPS, POOL_GROUP_DIM, POOL_GROUP_DIM), POOL_GROUP_DIM ** -0.5),
        'pool_scale': gain(ks[5], (L, POOL_WIDTH)),
        'q_norm_g': gain(ks[6], (L, HEAD_DIM_2)),
        'k_norm_g': gain(ks[7], (L, HEAD_DIM_2)),
        'w_out': nrm(ks[8], (L, MIX_WIDTH, D_MODEL), MIX_WIDTH ** -0.5),
        'norm_xattn_g': gain(ks[9], (L, D_MODEL)),
        'norm_mem_g': gain(ks[10], (L, D_MODEL)),
        'w_xq': nrm(ks[11], (L, D_MODEL, D_MODEL), D_MODEL ** -0.5),
        'w_xkv': nrm(ks[12], (L, D_MODEL, 2 * D_MODEL), D_MODEL ** -0.5),
        'xq_norm_g': gain(ks[13], (L, XATTN_HEAD_DIM)),
        'xk_norm_g': gain(ks[14], (L, XATTN_HEAD_DIM)),
        'w_xo': nrm(ks[15], (L, D_MODEL, D_MODEL), D_MODEL ** -0.5),
        'norm_ffn_g': gain(ks[16], (L, D_MODEL)),
        'w_up': nrm(ks[17], (L, D_MODEL, 2 * D_FF), D_MODEL ** -0.5),
        'conv_w': nrm(ks[18], (L, CONV_WIDTH, 2 * D_FF), CONV_WIDTH ** -0.5),
        'conv_b': nrm(ks[19], (L, 2 * D_FF), 0.01),
        'w_down': nrm(ks[20], (L, D_FF, D_MODEL), D_FF ** -0.5),
    }

def second_block(x, mem, norm_mix_g, w_in, pool_w, pool_scale, q_norm_g, k_norm_g, w_out,
              norm_xattn_g, norm_mem_g, w_xq, w_xkv, xq_norm_g, xk_norm_g, w_xo,
              norm_ffn_g, w_up, conv_w, conv_b, w_down):
    B, S, _ = x.shape
    pos = jnp.arange(S)
    for l in range(DEPTH):
        h = _rms_norm(x, norm_mix_g[l])
        proj = h @ w_in[l]
        u = proj[..., :POOL_WIDTH]
        qkv = proj[..., POOL_WIDTH:].reshape(B, S, 3, ATTN_HEADS, HEAD_DIM_2)
        q = qkv[:, :, 0].transpose(0, 2, 1, 3)
        k = qkv[:, :, 1].transpose(0, 2, 1, 3)
        v = qkv[:, :, 2].transpose(0, 2, 1, 3)
        q = _rope(_rms_norm(q, q_norm_g[l]), pos)
        k = _rope(_rms_norm(k, k_norm_g[l]), pos)
        attn = _moba_attention(q, k, v).transpose(0, 2, 1, 3).reshape(B, S, ATTN_WIDTH)
        pool = _pool_mixer(u, pool_w[l], pool_scale[l])
        x = x + jnp.concatenate([pool, attn], axis=-1) @ w_out[l]
        h = _rms_norm(x, norm_xattn_g[l])
        m = _rms_norm(mem, norm_mem_g[l])
        x = x + _cross_attention(h, m, w_xq[l], w_xkv[l], xq_norm_g[l], xk_norm_g[l], w_xo[l])
        h = _rms_norm(x, norm_ffn_g[l])
        x = x + _conv_ffn(h, w_up[l], conv_w[l], conv_b[l], w_down[l])
    return x


def setup_inputs(seed=0):
    out = dict(first_inputs(seed))
    for name, value in second_inputs(seed + 1).items():
        if name != "x":
            out[name + "_2"] = value
    return out


def reference(
    x, c, ctx, c_ctx, ada_w, ada_b, norm_g, sc_w_in, sc_conv, sc_w_out, hy_w_in, hy_conv,
    hy_f_w1, hy_f_b1, hy_f_w2, hy_f_b2, hy_f_w3, hy_sin_freq, hy_skip, hy_w_out, at_w_qkv,
    at_q_g, at_k_g, at_w_o, moe_router, moe_w_gate, moe_w_up, moe_w_down, mem_2, norm_mix_g_2,
    w_in_2, pool_w_2, pool_scale_2, q_norm_g_2, k_norm_g_2, w_out_2, norm_xattn_g_2,
    norm_mem_g_2, w_xq_2, w_xkv_2, xq_norm_g_2, xk_norm_g_2, w_xo_2, norm_ffn_g_2, w_up_2,
    conv_w_2, conv_b_2, w_down_2,
):
    x = first_block(
        x, c, ctx, c_ctx, ada_w, ada_b, norm_g, sc_w_in, sc_conv, sc_w_out, hy_w_in, hy_conv,
        hy_f_w1, hy_f_b1, hy_f_w2, hy_f_b2, hy_f_w3, hy_sin_freq, hy_skip, hy_w_out, at_w_qkv,
        at_q_g, at_k_g, at_w_o, moe_router, moe_w_gate, moe_w_up, moe_w_down,
    )
    return second_block(
        x, mem_2, norm_mix_g_2, w_in_2, pool_w_2, pool_scale_2, q_norm_g_2, k_norm_g_2, w_out_2,
        norm_xattn_g_2, norm_mem_g_2, w_xq_2, w_xkv_2, xq_norm_g_2, xk_norm_g_2, w_xo_2,
        norm_ffn_g_2, w_up_2, conv_w_2, conv_b_2, w_down_2,
    )


_drawn_inputs = setup_inputs


def setup_inputs(seed=0):
    import zlib

    import numpy as np

    out = dict(_drawn_inputs(seed))
    spreads = {}
    factors = {'ada_b': 3.322,
     'norm_g': 3.599,
     'q_norm_g_2': 5.714,
     'k_norm_g_2': 5.043,
     'norm_xattn_g_2': 5.977,
     'norm_mem_g_2': 4.188,
     'xq_norm_g_2': 5.873,
     'xk_norm_g_2': 6.696,
     'conv_b_2': 64.0,
     'pool_scale_2': 8.0,
     'norm_ffn_g_2': 8.0}
    for name, (base, spread) in spreads.items():
        noise = np.random.default_rng([zlib.crc32(name.encode()), seed]).standard_normal(out[name].shape)
        drawn = base * np.exp(spread * noise) if base else spread * noise
        out[name] = jnp.asarray(drawn.astype(out[name].dtype))
    for name, factor in factors.items():
        out[name] = (out[name] * factor).astype(out[name].dtype)
    return out
```

```python
from contextlib import ExitStack

import concourse.bass as bass
from concourse import mybir

F32 = mybir.dt.float32
ACT = mybir.ActivationFunctionType
ALU = mybir.AluOpType
AX = mybir.AxisListType.X

P = 128
D = 1024
T = 256
KC = D // P
TT = T // P
EPS = 1e-6
RING = 3

N_EXPERTS = 16
CAP = 2 * T // N_EXPERTS
POOL_WINDOWS = (2, 4, 8, 16)
PG = len(POOL_WINDOWS)
PAD = 16
HEADS, HD = 8, 64
XHEADS, XHD = 4, 256
FC = 2816 // P

VEC = {}
_at = 0
for _name, _n in (("c", KC), ("ada_b", 6 * KC), ("norm_g", 2 * KC), ("sc_conv", 3 * KC), ("norm_mem_g", KC),
                  ("router", KC * N_EXPERTS), ("norm_mix_g", KC), ("pool_scale", PG), ("q_norm_g", 1),
                  ("k_norm_g", 1), ("norm_xattn_g", KC), ("xq_norm_g", 2), ("xk_norm_g", 2), ("norm_ffn_g", KC),
                  ("conv_w", 3 * 2 * FC), ("conv_b", 2 * FC)):
    VEC[_name] = (_at, _n)
    _at += _n
VEC_COLS = _at

TAB = {}
_at = 0
for _name, _n in (("ident", P), ("iota", CAP), ("rot", P), ("headmean", P), ("cos", T), ("sin", T),
                  ("causal", 3 * P), ("invcnt", PG * PAD)):
    TAB[_name] = (_at, _n)
    _at += _n
TAB_COLS = _at

BLOCKS = ["shift1", "scale1", "sc_b", "sc_c", "sc_v", "gate1", "sc_out", "shift2", "scale2", "gate2"]
MOE0 = len(BLOCKS)
BLOCK = {n: i for i, n in enumerate(BLOCKS)}
for _i, _name in enumerate(("in_uq", "in_kv", "mix_out", "xq", "xo")):
    BLOCK[_name] = MOE0 + 3 * N_EXPERTS + _i

FILL = {}
_at = 0
for _name, _n in (("x_t", 4), ("mem_t", 4), ("conv_b", 4), ("conv_c", 4), ("conv_v", 4), ("conv_out", 4),
                  ("h2_rows", 4), ("gather", 8), ("q", 2), ("k", 2), ("v", 2), ("u", 2), ("pool", 2),
                  ("mix_out", 4), ("xq", 4), ("xo", 4), ("rows", 4)):
    FILL[_name] = _at
    _at += _n

N1, NMEM, N2, NMIX, NXATT, NFFN = range(6)


def program(nc, io):
    with ExitStack() as ctx:
        def sb(name, shape):
            return ctx.enter_context(nc.sbuf_tensor(name, shape, F32))

        def bank(name):
            return ctx.enter_context(nc.psum_tensor(name, [P, 512], F32))

        def sem(name):
            return ctx.enter_context(nc.semaphore(name))

        ring = sb("ring", [P, RING, KC, D])
        lat = sb("lat", [P, KC, T])
        h = sb("h", [P, KC, T])
        mem_n = sb("mem_n", [P, KC, T])
        k_mem = sb("k_mem", [P, KC, T])
        v_mem = sb("v_mem", [P, TT, D])
        kv_w = sb("kv_w", [P, KC, P])
        region_a = sb("region_a", [P, 4096])
        region_b = sb("region_b", [P, 4352])
        region_c = sb("region_c", [P, 2048])
        region_s = sb("region_s", [P, 2048])
        sq = sb("sq", [P, 2, 512])
        std = sb("std", [P, 2, T])
        rstd = sb("rstd", [P, T])
        eps = sb("eps", [P, 1])
        vec = sb("vec", [P, VEC_COLS])
        tab = sb("tab", [P, TAB_COLS])
        pool_w = sb("pool_w", [P, PG, P])
        ones_d = sb("ones_d", [P, P])
        ones_x = sb("ones_x", [P, P])
        silu_c = sb("silu_c", [P, KC])
        mod = sb("mod", [P, 6 * KC])
        gain1 = sb("gain1", [P, KC])
        gain2 = sb("gain2", [P, KC])
        aff = sb("aff", [P, TT, N_EXPERTS])
        aff_e = sb("aff_e", [P, TT, N_EXPERTS])
        top8 = sb("top8", [N_EXPERTS, 8])
        slot = sb("slot", [P, TT, N_EXPERTS])
        stat = sb("stat", [P, 64])

        def chunks(ap, n):
            return ap.rearrange("p (k t) -> p k t", k=n)

        x_rows = chunks(region_c[:, :], TT)
        mem_rows = chunks(region_b[:, 2304:4352], TT)
        gate_b = chunks(region_a[:, 0:2048], KC)
        gate_c = chunks(region_a[:, 2048:4096], KC)
        cv = chunks(region_b[:, 0:KC * (T + 2)], KC)
        conv = chunks(region_c[:, :], KC)
        sel = region_s[:, 0:1024].rearrange("p (i e s) -> p i e s", i=TT, s=CAP)
        sel_g = region_s[:, 1024:2048].rearrange("p (b i e j s) -> p b i e j s", b=2, i=TT, e=2, j=4)
        h2_rows = chunks(region_c[:, :], TT)
        ada_rows = chunks(region_s[:, 0:512], 2)
        xs = chunks(region_a[:, :], KC)
        scatter = region_b[:, 0:N_EXPERTS * T].rearrange("p (e t) -> p e t", e=N_EXPERTS)
        xs_e = chunks(region_c[:, 0:256], KC)
        silu_g, hid, ys_rows, scat_e = (region_c[:, 256 * i:256 * (i + 1)] for i in range(1, 5))
        hid_t = region_c[:, 1280:1536].rearrange("p (c j s) -> p c j s", c=2, j=4)
        top_work, chosen, count, slot_t, ones_r = (region_b[0:N_EXPERTS, T * i:T * (i + 1)] for i in range(5))
        q_rot = chunks(region_a[:, 0:1024], 4)
        k_rot = chunks(region_a[:, 1024:2048], 4)
        v_rows = chunks(region_a[:, 2048:3072], TT)
        qk_g = region_a[:, 3072:3584]
        qk_t = region_a[:, 3584:4096]
        UP = PAD + T
        u_pad = chunks(region_b[:, 0:PG * UP], PG)
        win_a = chunks(region_b[:, PG * UP:2 * PG * UP], PG)
        win_b = chunks(region_b[:, 2 * PG * UP:3 * PG * UP], PG)
        pooled = chunks(region_b[:, 3 * PG * UP:3 * PG * UP + PG * T], PG)
        mix = chunks(region_c[:, :], KC)
        prob = chunks(region_s[:, 0:1024], 2)
        prob_t = chunks(region_s[:, 1024:2048], 2)
        q_x = chunks(region_a[:, 0:2048], KC)
        o_x = chunks(region_c[:, :], KC)
        up_z = region_a[:, 0:1024].rearrange("p (s g t) -> p s g t", s=2, g=2)
        up_s = chunks(region_a[:, 1024:1536], 2)
        up_h = chunks(region_a[:, 1536:2048], 2)
        out_rows = chunks(region_c[:, :], TT)
        ffn_w = ring[:, 0, 0:6, :].rearrange("p (s a) n -> p s a n", s=2)
        ffn_up = [[ffn_w[:, s, g, :].rearrange("p (k n) -> p k n", k=KC) for g in range(2)] for s in range(2)]
        ffn_down = [ffn_w[:, s, 2, :] for s in range(2)]

        acc = [bank(f"acc{b}") for b in range(4)]
        misc = [bank(f"misc{b}") for b in range(4)]

        def vcol(name, i=0, n=None):
            at, size = VEC[name]
            return vec[:, at + i:at + (size if n is None else i + n)]

        def table(name):
            at, size = TAB[name]
            return tab[:, at:at + size]

        ident = table("ident")
        router = vcol("router").rearrange("p (k e) -> p k e", k=KC)

        s_vec, s_tab, s_x, s_mem, s_poolw = (sem(n) for n in ("vec_in", "tab_in", "x_in", "mem_in", "poolw_in"))
        landed = [sem(f"ring_landed{i}") for i in range(RING)]
        ring_used = sem("ring_used")
        acc_done = [sem(f"acc_done{b}") for b in range(4)]
        acc_free = [sem(f"acc_free{b}") for b in range(4)]
        ones_set = sem("ones_set")
        silu_c_ready = sem("silu_c_ready")
        sq_ready, sq_used = sem("sq_ready"), sem("sq_used")
        mean_ready, mean_free = sem("mean_ready"), sem("mean_free")
        lat_ready = [sem(f"norm_in_ready{n}") for n in range(6)]
        h_scaled = sem("h_scaled")
        h_ready = [sem(f"h_ready{n}") for n in range(6)]
        ada_done, ada_rows_ready, ada_t_done, ada_read = (
            sem(n) for n in ("ada_rows_done", "ada_rows_ready", "ada_t_done", "ada_read"))
        b_ready, c_ready, cv_zeroed, conv_ready = (sem(n) for n in ("gate_b_ready", "gate_c_ready", "cv_zeroed", "conv_ready"))
        dve = sem("vector_chain")
        poolc = sem("gpsimd_chain")

        def block_wait(eng, name):
            m = BLOCK[name]
            eng.wait_ge(landed[m % RING], 16 * (m // RING + 1))

        def block_slot(name):
            return ring[:, BLOCK[name] % RING]

        def fill_done(eng, n):
            eng.wait_ge(acc_done[n % 4], n // 4 + 1)

        def fill_free(eng, n):
            if n >= 4:
                eng.wait_ge(acc_free[n % 4], n // 4)

        logits_done, exp_done, aff_ready, afft_done, slot_t_ready, slot_done = (
            sem(n) for n in ("logits_done", "aff_exp_done", "aff_ready", "aff_t_done", "slot_t_ready", "slot_done"))
        negmax_r = sem("router_negmax")
        sel_ready, selg_ready, rows_ready, xs_ready, scat_t_done, scat_ready = (
            sem(n) for n in ("sel_ready", "sel_g_ready", "h2_rows_ready", "xs_ready", "scatter_t_done", "scatter_ready"))
        logits_read = sem("logits_read")
        slot_read = sem("slot_read")
        y_zeroed = sem("y_zeroed")
        xs_free, xse_ready = sem("xs_e_free"), sem("xs_e_ready")
        gate_done, up_done, silu_ready, hid_ready, hidt_done, hidt_ready, down_done, ysr_ready = (
            sem(n) for n in ("gate_done", "up_done", "silu_ready", "hid_ready", "hid_t_done", "hid_t_ready",
                             "down_done", "ys_rows_ready"))
        scate_ready, scat_free = sem("scatter_e_ready"), sem("scatter_e_free")
        kvw_in, kvw_used, kv_read = sem("kv_w_in"), sem("kv_w_used"), sem("kv_read")
        ksq_ready, kmean_done, kmean_read, k_ready = (sem(n) for n in ("k_sq_ready", "k_mean_done", "k_mean_read", "k_mem_ready"))
        qkg_ready, qk_prep, qk_ready = sem("qk_gained"), sem("qk_mean_rot_done"), sem("qk_ready")
        qk_read, qk_std = sem("qk_rot_read"), sem("qk_std_ready")
        xstd_ready = sem("xq_std_ready")
        v_ready, u_ready, u_zeroed, pooled_ready, pool_ready = (
            sem(n) for n in ("v_rows_ready", "u_ready", "u_zeroed", "pooled_ready", "pool_mix_ready"))
        score_done, masked, negmax, prob_exp, prob_ready, probt_done, probt_ready, pv_done, o_ready = (
            sem(n) for n in ("score_done", "scores_masked", "negmax_ready", "prob_exp", "prob_ready", "prob_t_done",
                             "prob_t_ready", "pv_done", "attn_out_ready"))
        xsq_ready, xmean_done, xq_ready = sem("xq_sq_ready"), sem("xq_mean_done"), sem("xq_ready")
        xscore_done, xnegmax, xexp, xprob_ready, xprobt_done, xprobt_ready, xpv_done, xo_ready = (
            sem(n) for n in ("xscore_done", "xnegmax_ready", "xprob_exp", "xprob_ready", "xprob_t_done",
                             "xprob_t_ready", "xpv_done", "xattn_out_ready"))
        ffn_in = [sem(f"ffn_w_in{s}") for s in range(2)]
        ffn_w_used = sem("ffn_w_used")
        up2_done, z_ready, conv2_done, silu2_ready, act_ready, ffn_zeroed, ffn_done = (
            sem(n) for n in ("ffn_up_done", "ffn_z_ready", "ffn_conv_done", "ffn_silu_ready", "ffn_act_ready",
                             "ffn_acc_zeroed", "ffn_done"))
        lat_final, out_ready, s_out = sem("lat_final"), sem("out_rows_ready"), sem("out_stored")

        def wblock(ap):
            return ap.rearrange("(k p) n -> p k n", p=P)

        ada = io["ada_w"][0]
        stream = {"shift1": ada[:, 0:D], "scale1": ada[:, D:2 * D], "gate1": ada[:, 2 * D:3 * D],
                  "shift2": ada[:, 3 * D:4 * D], "scale2": ada[:, 4 * D:5 * D], "gate2": ada[:, 5 * D:6 * D],
                  "sc_b": io["sc_w_in"][0][:, 0:D], "sc_c": io["sc_w_in"][0][:, D:2 * D],
                  "sc_v": io["sc_w_in"][0][:, 2 * D:3 * D], "sc_out": io["sc_w_out"][0],
                  "in_uq": io["w_in"][0][:, 0:D], "in_kv": io["w_in"][0][:, D:2 * D],
                  "mix_out": io["w_out"][0], "xq": io["w_xq"][0], "xo": io["w_xo"][0]}

        block = ctx.enter_context(nc.Block())

        @block.sync
        def _(sp):
            def load_block(name):
                m = BLOCK[name]
                if m >= RING:
                    sp.wait_ge(ring_used, m - RING + 1)
                src = wblock(stream[name])
                if m == 0:
                    pass
                sp.dma_start(block_slot(name), src).then_inc(landed[m % RING], 16)

            for name in BLOCKS:
                load_block(name)
            with sp.Fori(0, N_EXPERTS) as e:
                for j, w in enumerate((io["moe_w_gate"], io["moe_w_up"], io["moe_w_down"])):
                    m = MOE0 + j
                    sp.wait_ge(ring_used, e * 3 + (m - RING + 1))
                    sp.dma_start(ring[:, m % RING],
                                 w[0, bass.ds(e, 1)].rearrange("o (k p) n -> p (o k) n", p=P)) \
                      .then_inc(landed[m % RING], 16)
            for name in ("in_uq", "in_kv", "mix_out", "xq", "xo"):
                load_block(name)
            w_up, w_down = io["w_up"][0], io["w_down"][0]
            up_v = w_up.rearrange("(k p) (g s n) -> g s p k n", p=P, g=2, n=P)
            down_v = w_down.rearrange("(s p) n -> s p n", p=P)

            def load_ffn(s, par):
                sp.dma_start(ffn_up[par][0], up_v[0, s]).then_inc(ffn_in[par], 16)
                sp.dma_start(ffn_up[par][1], up_v[1, s]).then_inc(ffn_in[par], 16)
                sp.dma_start(ffn_down[par], down_v[s]).then_inc(ffn_in[par], 16)

            sp.wait_ge(ring_used, BLOCK["mix_out"] + 1)
            load_ffn(0, 0)
            load_ffn(1, 1)
            with sp.Fori(1, FC // 2) as i:
                for par in range(2):
                    sp.wait_ge(ffn_w_used, i * 2 + (par - 1))
                    s = i * 2 + par
                    sp.dma_start(ffn_up[par][0], w_up[:, bass.ds(s * P, P)].rearrange("(k p) n -> p k n", p=P)) \
                      .then_inc(ffn_in[par], 16)
                    sp.dma_start(ffn_up[par][1],
                                 w_up[:, bass.ds(s * P + FC * P, P)].rearrange("(k p) n -> p k n", p=P)) \
                      .then_inc(ffn_in[par], 16)
                    sp.dma_start(ffn_down[par], w_down[bass.ds(s * P, P), :]).then_inc(ffn_in[par], 16)
            out_v = io["out"][0].rearrange("(i p) d -> p i d", p=P)
            for f in range(4):
                sp.wait_ge(out_ready, f + 1)
                sp.dma_start(out_v[:, :, f * 256:(f + 1) * 256], out_rows[:, :, f * 256:(f + 1) * 256]) \
                  .then_inc(s_out, 16)
            sp.wait_ge(s_out, 64)

        @block.gpsimd
        def _(pool):
            nc.gpsimd.memset(ones_d[:, :], 1.0 / D).then_inc(ones_set, 1)
            nc.gpsimd.memset(ones_x[:, :], 1.0 / XHD).then_inc(ones_set, 1)
            nc.gpsimd.memset(eps[:, :], EPS).then_inc(ones_set, 1)
            nc.gpsimd.memset(cv[:, :, 0:1], 0.0).then_inc(cv_zeroed, 1)
            nc.gpsimd.memset(cv[:, :, T + 1:T + 2], 0.0).then_inc(cv_zeroed, 1)
            xkv = io["w_xkv"][0]
            pool.dma_start(pool_w[:, :, :], io["pool_w"][0].rearrange("g c n -> c g n")).then_inc(s_poolw, 16)
            pool.dma_start(kv_w[:, :, :], wblock(xkv[:, 0:P])).then_inc(kvw_in, 16)
            with pool.Fori(1, N_EXPERTS) as e:
                pool.wait_ge(kvw_used, e)
                pool.dma_start(kv_w[:, :, :], xkv[:, bass.ds(e * P, P)].rearrange("(k p) n -> p k n", p=P)) \
                    .then_inc(kvw_in, 16)
            pool.wait_ge(scat_free, N_EXPERTS + 1)
            nc.gpsimd.memset(u_pad[:, :, 0:PAD], 0.0).then_inc(u_zeroed, 1)
            pool.wait_ge(u_zeroed, 1)
            pool.wait_ge(u_ready, 2)
            n = 0
            src, dst = u_pad, win_a
            for g in range(PG):
                w = 1 << g
                lo = 2 * w - 1
                nc.gpsimd.tensor_tensor(dst[:, g:PG, lo:UP], src[:, g:PG, lo:UP], src[:, g:PG, lo - w:UP - w],
                                        ALU.add).then_inc(poolc, 1)
                n += 1
                pool.wait_ge(poolc, n)
                nc.gpsimd.tensor_scalar(pooled[:, g, :], dst[:, g, PAD:UP], 1.0 / POOL_WINDOWS[g], None,
                                        ALU.mult).then_inc(poolc, 1)
                n += 1
                pool.wait_ge(poolc, n)
                inv = table("invcnt").rearrange("p (g t) -> p g t", g=PG)
                nc.gpsimd.tensor_tensor(pooled[:, g, 0:PAD], dst[:, g, PAD:2 * PAD], inv[:, g, :],
                                        ALU.mult).then_inc(poolc, 1)
                n += 1
                pool.wait_ge(poolc, n)
                nc.gpsimd.tensor_tensor(pooled[:, g, :], pooled[:, g, :], u_pad[:, g, PAD:UP],
                                        ALU.subtract).then_inc(pooled_ready, 1)
                src = dst
                dst = win_b if dst is win_a else win_a

        @block.tensor
        def _(pe):
            mm = nc.tensor.matmul

            def transpose_rows(rows, first):
                for f in range(4):
                    n = first + f
                    fill_free(pe, n)
                    for c in range(2):
                        for i in range(TT):
                            k = 2 * f + c
                            last = nc.tensor.transpose(acc[n % 4][:, c * T + i * P:c * T + (i + 1) * P],
                                                       rows[:, i, k * P:(k + 1) * P], ident)
                    last.then_inc(acc_done[n % 4], 1)

            def norm_mean(n_norm):
                if n_norm:
                    pe.wait_ge(mean_free, n_norm)
                for f in range(4):
                    pe.wait_ge(sq_ready, 4 * n_norm + f + 1)
                    for c in range(2):
                        last = mm(misc[0][:, 0:T], ones_d[:, :], sq[:, f % 2, c * T:(c + 1) * T],
                                  start=(f == 0 and c == 0), stop=(f == 3 and c == 1))
                    last.then_inc(sq_used, 1)

            def rows_product(out, w, stationary):
                for k in range(KC):
                    for j in range(4):
                        last = mm(out[CAP * j:CAP * (j + 1), 0:256], stationary(k), w[:, k, 256 * j:256 * (j + 1)],
                                  start=(k == 0), stop=(k == KC - 1))
                return last

            def ada_block(name, j):
                block_wait(pe, name)
                if j >= 2:
                    pe.wait_ge(ada_rows_ready, j - 1)
                rows_product(misc[1 + 2 * (j % 2)], block_slot(name),
                             lambda k: silu_c[:, k:k + 1].to_broadcast([P, CAP])).then_inc(ada_done, 1)
                release()

            def ada_columns(j):
                pe.wait_ge(ada_rows_ready, j + 1)
                if j:
                    pe.wait_ge(ada_read, j)
                for c in range(2):
                    last = nc.tensor.transpose(misc[2][:, c * P:(c + 1) * P], ada_rows[:, j % 2, c * P:(c + 1) * P], ident)
                last.then_inc(ada_t_done, 1)

            def dense_fill(slot_ap, src, n, cols, last_of_block):
                fill_free(pe, n)
                for ci, c in enumerate(cols):
                    for k in range(KC):
                        last = mm(acc[n % 4][:, ci * T:(ci + 1) * T], slot_ap[:, k, c * P:(c + 1) * P], src[:, k, :],
                                  start=(k == 0), stop=(k == KC - 1))
                last.then_inc(acc_done[n % 4], 1)
                if last_of_block:
                    release()

            def release():
                nc.tensor.drain().then_inc(ring_used, 1)

            def dense(name, src, first, order=range(4)):
                block_wait(pe, name)
                for j, f in enumerate(order):
                    dense_fill(block_slot(name), src, first + j, (2 * f, 2 * f + 1), j == len(order) - 1)

            pe.wait_ge(s_tab, 16)
            pe.wait_ge(s_x, 16)
            transpose_rows(x_rows, FILL["x_t"])
            pe.wait_ge(s_mem, 16)
            transpose_rows(mem_rows, FILL["mem_t"])
            pe.wait_ge(ones_set, 3)
            norm_mean(N1)
            norm_mean(NMEM)
            pe.wait_ge(silu_c_ready, 1)
            ada_block("shift1", 0)
            ada_block("scale1", 1)
            ada_columns(0)
            ada_columns(1)
            pe.wait_ge(h_ready[N1], KC)
            dense("sc_b", h, FILL["conv_b"])
            dense("sc_c", h, FILL["conv_c"])
            dense("sc_v", h, FILL["conv_v"])
            ada_block("gate1", 2)
            pe.wait_ge(conv_ready, KC)
            ada_columns(2)
            dense("sc_out", conv, FILL["conv_out"])
            ada_block("shift2", 3)
            ada_block("scale2", 4)
            norm_mean(N2)
            ada_columns(3)
            ada_columns(4)
            ada_block("gate2", 5)
            ada_columns(5)
            pe.wait_ge(h_ready[N2], KC)
            pe.wait_ge(ada_read, 6)
            for i in range(TT):
                for k in range(KC):
                    last = mm(misc[3][:, i * N_EXPERTS:(i + 1) * N_EXPERTS], h[:, k, i * P:(i + 1) * P],
                              router[:, k, :], start=(k == 0), stop=(k == KC - 1))
            last.then_inc(logits_done, 1)
            for f in range(4):
                n = FILL["h2_rows"] + f
                fill_free(pe, n)
                i = f // 2
                for c in range(4):
                    k = 4 * (f % 2) + c
                    last = nc.tensor.transpose(acc[n % 4][:, c * P:(c + 1) * P], h[:, k, i * P:(i + 1) * P], ident)
                last.then_inc(acc_done[n % 4], 1)
            pe.wait_ge(aff_ready, 1)
            for i in range(TT):
                last = nc.tensor.transpose(misc[2][0:N_EXPERTS, i * P:(i + 1) * P], aff[:, i, :], ident)
            last.then_inc(afft_done, 1)
            pe.wait_ge(slot_t_ready, 1)
            for i in range(TT):
                last = nc.tensor.transpose(misc[3][:, i * N_EXPERTS:(i + 1) * N_EXPERTS],
                                           slot_t[:, i * P:(i + 1) * P], ident[0:N_EXPERTS, 0:N_EXPERTS])
            last.then_inc(slot_done, 1)
            pe.wait_ge(sel_ready, 1)
            pe.wait_ge(rows_ready, 4)
            for k in range(KC):
                n = FILL["gather"] + k
                fill_free(pe, n)
                for i in range(TT):
                    last = mm(acc[n % 4][:, :], h2_rows[:, i, k * P:(k + 1) * P],
                              sel[:, i, :, :].rearrange("p e s -> p (e s)"), start=(i == 0), stop=(i == TT - 1))
                last.then_inc(acc_done[n % 4], 1)
            for p in range(N_EXPERTS // 2):
                pe.wait_ge(selg_ready, p + 1)
                if p >= 2:
                    pe.wait_ge(scat_ready, p - 1)
                for j in range(2):
                    for i in range(TT):
                        last = nc.tensor.transpose(
                            misc[2 + p % 2][:, j * T + i * P:j * T + (i + 1) * P],
                            sel_g[:, p % 2, i, j, :, :].rearrange("p j s -> p (j s)"), ident)
                last.then_inc(scat_t_done, 1)
            pe.wait_ge(scat_ready, N_EXPERTS // 2)
            nc.tensor.nop().then_inc(scat_free, 1)
            pe.wait_ge(y_zeroed, 4)

            def expert(e, values):
                gate_w, up_w, down_w = (ring[:, (MOE0 + j) % RING] for j in range(3))
                uses = [(MOE0 + j) // RING + 1 for j in range(3)]

                pe.wait_ge(xse_ready, e + 1)
                pe.wait_ge(landed[MOE0 % RING], e * 16 + 16 * uses[0])
                rows_product(misc[0], gate_w, lambda k: xs_e[:, k, :]).then_inc(gate_done, 1)
                release()
                pe.wait_ge(landed[(MOE0 + 1) % RING], e * 16 + 16 * uses[1])
                rows_product(misc[1], up_w, lambda k: xs_e[:, k, :]).then_inc(up_done, 1)
                release()
                pe.wait_ge(kvw_in, e * 16 + 16)
                pe.wait_ge(silu_ready, e + 1)
                if not values:
                    for k in range(KC):
                        last = mm(misc[0][:, 0:T], kv_w[:, k, :], mem_n[:, k, :], start=(k == 0), stop=(k == KC - 1))
                else:
                    for i in range(TT):
                        for k in range(KC):
                            last = mm(misc[0][:, i * P:(i + 1) * P], mem_n[:, k, i * P:(i + 1) * P], kv_w[:, k, :],
                                      start=(k == 0), stop=(k == KC - 1))
                last.then_inc(kvw_used, 1)
                pe.wait_ge(hid_ready, e + 1)
                for c in range(2):
                    last = nc.tensor.transpose(misc[2][:, c * P:(c + 1) * P], hid[:, c * P:(c + 1) * P], ident)
                last.then_inc(hidt_done, 1)
                pe.wait_ge(hidt_ready, e + 1)
                pe.wait_ge(landed[(MOE0 + 2) % RING], e * 16 + 16 * uses[2])
                rows_product(misc[3], down_w, lambda k: hid_t[:, k % 2, k // 2, :]).then_inc(down_done, 1)
                release()
                pe.wait_ge(ysr_ready, e + 1)
                pe.wait_ge(scate_ready, e + 1)
                for c in range(2):
                    for j in range(4):
                        g = slice(CAP * j, CAP * (j + 1))
                        last = mm(acc[j][:, c * T:(c + 1) * T], ys_rows[g, c * P:(c + 1) * P], scat_e[g, :],
                                  start=False, stop=False, skip_group_check=True)
                last.then_inc(scat_free, 1)
                pe.wait_ge(kv_read, e + 1)

            pe.wait_ge(h_ready[NMEM], KC)
            with pe.Fori(0, N_EXPERTS // 2) as e:
                expert(e, False)
            for x in range(XHEADS):
                pe.wait_ge(ksq_ready, x + 1)
                if x:
                    pe.wait_ge(kmean_read, x)
                for c in range(2):
                    last = mm(misc[0][:, 0:T], ones_x[:, :], sq[:, x % 2, c * T:(c + 1) * T], start=(c == 0), stop=(c == 1))
                last.then_inc(kmean_done, 1)
            pe.wait_ge(kmean_read, XHEADS)
            with pe.Fori(N_EXPERTS // 2, N_EXPERTS) as e:
                expert(e, True)

            norm_mean(NMIX)
            pe.wait_ge(h_ready[NMIX], KC)
            rot, headmean = table("rot"), table("headmean")

            def qk_mean_rot(j):
                pe.wait_ge(qkg_ready, j + 1)
                if j:
                    pe.wait_ge(qk_read, j)
                    pe.wait_ge(qk_std, j)
                mm(misc[0][:, :], headmean, sq[:, j % 2, :], start=True, stop=True)
                mm(misc[1][:, :], rot, qk_g, start=True, stop=True).then_inc(qk_prep, 1)

            block_wait(pe, "in_uq")
            dense_fill(block_slot("in_uq"), h, FILL["q"], (4, 5), False)
            dense_fill(block_slot("in_uq"), h, FILL["q"] + 1, (6, 7), False)
            qk_mean_rot(0)
            block_wait(pe, "in_kv")
            dense_fill(block_slot("in_kv"), h, FILL["k"], (0, 1), False)
            qk_mean_rot(1)
            dense_fill(block_slot("in_kv"), h, FILL["k"] + 1, (2, 3), False)
            qk_mean_rot(2)
            for i in range(TT):
                n = FILL["v"] + i
                fill_free(pe, n)
                for k in range(KC):
                    last = mm(acc[n % 4][:, :], h[:, k, i * P:(i + 1) * P], block_slot("in_kv")[:, k, 512:1024],
                              start=(k == 0), stop=(k == KC - 1))
                last.then_inc(acc_done[n % 4], 1)
                if i == 0:
                    qk_mean_rot(3)
            dense_fill(block_slot("in_uq"), h, FILL["u"], (0, 1), False)
            dense_fill(block_slot("in_uq"), h, FILL["u"] + 1, (2, 3), True)
            release()

            def scores(a):
                c, lo = a // 2, HD * (a % 2)
                if a == 0:
                    pe.wait_ge(qk_ready, 4)
                if a >= 2:
                    pe.wait_ge(masked, a - 1)
                b = misc[2 + a % 2]
                mm(b[:, 0:P], q_rot[lo:lo + HD, c, 0:P], k_rot[lo:lo + HD, c, 0:P], start=True, stop=True)
                mm(b[:, P:3 * P], q_rot[lo:lo + HD, c, P:T], k_rot[lo:lo + HD, c, :],
                   start=True, stop=True).then_inc(score_done, 1)

            def weigh(a):
                lo = HD * (a % 2)
                pe.wait_ge(prob_ready, a + 1)
                if a:
                    pe.wait_ge(probt_ready, a)
                for b in range(3):
                    last = nc.tensor.transpose(misc[0][:, b * P:(b + 1) * P], prob[:, a % 2, b * P:(b + 1) * P], ident)
                last.then_inc(probt_done, 1)
                pe.wait_ge(probt_ready, a + 1)
                if a >= 1:
                    pe.wait_ge(o_ready, a)
                o = misc[1][lo:lo + HD, 0:T]
                mm(o, v_rows[:, 0, a * HD:(a + 1) * HD], prob_t[:, a % 2, 0:T], start=True, stop=False)
                mm(misc[1][lo:lo + HD, P:T], v_rows[:, 1, a * HD:(a + 1) * HD], prob_t[:, a % 2, T:T + P],
                   start=False, stop=True).then_inc(pv_done, 1)

            scores(0)
            pe.wait_ge(v_ready, TT)
            pe.wait_ge(s_poolw, 16)
            for a in range(HEADS):
                if a + 1 < HEADS:
                    scores(a + 1)
                weigh(a)
                if a in (3, 5):
                    f = (a - 3) // 2
                    n = FILL["pool"] + f
                    fill_free(pe, n)
                    pe.wait_ge(pooled_ready, 2 * f + 2)
                    for j in range(2):
                        g = 2 * f + j
                        last = mm(acc[n % 4][:, j * T:(j + 1) * T], pool_w[:, g, :], pooled[:, g, :],
                                  start=True, stop=True)
                    last.then_inc(acc_done[n % 4], 1)
            pe.wait_ge(pool_ready, 2)
            pe.wait_ge(o_ready, HEADS)
            dense("mix_out", mix, FILL["mix_out"])

            norm_mean(NXATT)
            pe.wait_ge(h_ready[NXATT], KC)

            def x_mean(x):
                pe.wait_ge(xsq_ready, x + 1)
                if x:
                    pe.wait_ge(xstd_ready, x)
                for c in range(2):
                    last = mm(misc[0][:, 0:T], ones_x[:, :], sq[:, x % 2, c * T:(c + 1) * T], start=(c == 0), stop=(c == 1))
                last.then_inc(xmean_done, 1)

            block_wait(pe, "xq")
            for x in range(XHEADS):
                dense_fill(block_slot("xq"), h, FILL["xq"] + x, (2 * x, 2 * x + 1), x == XHEADS - 1)
                if x:
                    x_mean(x - 1)
            x_mean(XHEADS - 1)

            def x_scores(x):
                pe.wait_ge(xq_ready, x + 1)
                if x >= 2:
                    pe.wait_ge(xexp, x - 1)
                b = misc[2 + x % 2]
                for i in range(TT):
                    for c in range(2):
                        last = mm(b[:, i * T:(i + 1) * T], q_x[:, 2 * x + c, i * P:(i + 1) * P], k_mem[:, 2 * x + c, :],
                                  start=(c == 0), stop=(c == 1))
                last.then_inc(xscore_done, 1)

            def x_weigh(x):
                pe.wait_ge(xprob_ready, x + 1)
                if x:
                    pe.wait_ge(xprobt_ready, x)
                for j in range(TT):
                    for i in range(TT):
                        last = nc.tensor.transpose(misc[0][:, j * T + i * P:j * T + (i + 1) * P],
                                                   prob[:, x % 2, i * T + j * P:i * T + (j + 1) * P], ident)
                last.then_inc(xprobt_done, 1)
                pe.wait_ge(xprobt_ready, x + 1)
                if x:
                    pe.wait_ge(xo_ready, x)
                for c in range(2):
                    for j in range(TT):
                        at = x * XHD + c * P
                        last = mm(misc[1][:, c * T:(c + 1) * T], v_mem[:, j, at:at + P], prob_t[:, x % 2, j * T:(j + 1) * T],
                                  start=(j == 0), stop=(j == TT - 1))
                last.then_inc(xpv_done, 1)

            pe.wait_ge(xq_ready, XHEADS)
            x_scores(0)
            for x in range(XHEADS):
                if x + 1 < XHEADS:
                    x_scores(x + 1)
                x_weigh(x)
            pe.wait_ge(xo_ready, XHEADS)
            dense("xo", o_x, FILL["xo"])

            norm_mean(NFFN)
            pe.wait_ge(h_ready[NFFN], KC)
            pe.wait_ge(ffn_zeroed, 4)

            def ffn_up_step(s, par, loads, first=False):
                pe.wait_ge(ffn_in[par], loads * 48)
                if not first:
                    pe.wait_ge(conv2_done, s - 1)
                for g in range(2):
                    for k in range(KC):
                        last = mm(misc[par][:, g * T:(g + 1) * T], ffn_up[par][g][:, k, :], h[:, k, :],
                                  start=(k == 0), stop=(k == KC - 1))
                last.then_inc(up2_done, 1)

            def ffn_down_step(s, par, done=None):
                pe.wait_ge(act_ready, s + 1)
                for c in range(KC):
                    last = mm(acc[c // 2][:, (c % 2) * T:(c % 2 + 1) * T], ffn_down[par][:, c * P:(c + 1) * P],
                              up_h[:, par, :], start=False, stop=False, skip_group_check=True)
                last.then_inc(ffn_w_used, 1)

            ffn_up_step(0, 0, 1, first=True)
            ffn_up_step(1, 1, 1, first=True)
            ffn_down_step(0, 0)
            with pe.Fori(1, FC // 2) as i:
                ffn_up_step(i * 2, 0, i + 1)
                ffn_down_step(i * 2 - 1, 1)
                ffn_up_step(i * 2 + 1, 1, i + 1)
                ffn_down_step(i * 2, 0)
            ffn_down_step(FC - 1, 1)

            for f in range(4):
                n = FILL["rows"] + f
                pe.wait_ge(lat_final, max(f, n % 4) + 1)
                fill_free(pe, n)
                for i in range(TT):
                    for c in range(2):
                        last = nc.tensor.transpose(acc[n % 4][:, i * T + c * P:i * T + (c + 1) * P],
                                                   lat[:, 2 * f + c, i * P:(i + 1) * P], ident)
                last.then_inc(acc_done[n % 4], 1)

        @block.scalar
        def _(act):
            A = nc.scalar.activation
            act.dma_start(vec[:, :], io["vectors"]).then_inc(s_vec, 16)
            act.dma_start(x_rows, io["x"][0].rearrange("(i p) d -> p i d", p=P)).then_inc(s_x, 16)
            act.dma_start(tab[:, :], io["tables"]).then_inc(s_tab, 16)
            act.dma_start(mem_rows, io["mem"][0].rearrange("(i p) d -> p i d", p=P)).then_inc(s_mem, 16)

            def squares(n_norm, src):
                for f in range(4):
                    act.wait_ge(lat_ready[n_norm], f + 1)
                    m = 4 * n_norm + f
                    if m >= 2:
                        act.wait_ge(sq_used, m - 1)
                    A(sq[:, f % 2, :], src[:, 2 * f:2 * f + 2, :], ACT.Square).then_inc(sq_ready, 1)

            def deviation(n_norm):
                act.wait_ge(sq_used, 4 * (n_norm + 1))
                A(std[:, n_norm % 2, :], misc[0][:, 0:T], ACT.Sqrt, bias=eps[:, :]).then_inc(mean_free, 1)

            act.wait_ge(ones_set, 3)
            act.wait_ge(s_vec, 16)
            A(silu_c[:, :], vcol("c"), ACT.Silu).then_inc(silu_c_ready, 1)
            squares(N1, lat)
            deviation(N1)
            for f in range(4):
                n = FILL["mem_t"] + f
                fill_done(act, n)
                A(mem_n[:, 2 * f:2 * f + 2, :], acc[n % 4][:, :], ACT.Copy).then_inc(acc_free[n % 4], 1)
            for f in range(4):
                n = FILL["mem_t"] + f
                act.wait_ge(acc_free[n % 4], n // 4 + 1)
                act.wait_ge(sq_used, 4 + f - 1)
                A(sq[:, f % 2, :], mem_n[:, 2 * f:2 * f + 2, :], ACT.Square).then_inc(sq_ready, 1)
            deviation(NMEM)
            def ada_copy(j):
                act.wait_ge(ada_done, j + 1)
                if j >= 2:
                    act.wait_ge(ada_t_done, j - 1)
                A(ada_rows[:, j % 2, :], misc[1 + 2 * (j % 2)][:, 0:256], ACT.Copy).then_inc(ada_rows_ready, 1)

            ada_copy(0)
            ada_copy(1)
            for k in range(KC):
                act.wait_ge(h_scaled, k + 1)
                A(h[:, k, :], h[:, k, :], ACT.Identity, bias=mod[:, k:k + 1]).then_inc(h_ready[N1], 1)
            for name, dst, ready in (("conv_b", gate_b, b_ready), ("conv_c", gate_c, c_ready)):
                for f in range(4):
                    n = FILL[name] + f
                    fill_done(act, n)
                    A(dst[:, 2 * f:2 * f + 2, :], acc[n % 4][:, :], ACT.Copy).then_inc(acc_free[n % 4], 1)
            ada_copy(2)
            squares(N2, lat)
            ada_copy(3)
            ada_copy(4)
            deviation(N2)
            for k in range(KC):
                act.wait_ge(h_scaled, KC + k + 1)
                A(h[:, k, :], h[:, k, :], ACT.Identity, bias=mod[:, 3 * KC + k:3 * KC + k + 1]).then_inc(h_ready[N2], 1)
            ada_copy(5)
            act.wait_ge(negmax_r, 1)
            for i in range(TT):
                A(aff_e[:, i, :], misc[3][:, i * N_EXPERTS:(i + 1) * N_EXPERTS], ACT.Exp, bias=stat[:, i:i + 1],
                  accum_out=stat[:, 2 + i:3 + i]).then_inc(exp_done, 1)
            for f in range(4):
                n = FILL["h2_rows"] + f
                fill_done(act, n)
                A(h2_rows[:, f // 2, (f % 2) * 512:(f % 2 + 1) * 512], acc[n % 4][:, :], ACT.Copy) \
                    .then_inc(acc_free[n % 4], 1)
            for f in range(4):
                n = FILL["h2_rows"] + f
                act.wait_ge(acc_free[n % 4], n // 4 + 1)
            nc.scalar.nop().then_inc(rows_ready, 4)
            for k in range(0, KC, 2):
                n = FILL["gather"] + k
                fill_done(act, n)
                A(xs[:, k, :], acc[n % 4][:, :], ACT.Copy).then_inc(acc_free[n % 4], 1)
            for p in range(N_EXPERTS // 2):
                act.wait_ge(scat_t_done, p + 1)
                A(scatter[:, 2 * p:2 * p + 2, :], misc[2 + p % 2][:, :], ACT.Copy).then_inc(scat_ready, 1)

            def expert(e):
                act.wait_ge(gate_done, e + 1)
                A(silu_g, misc[0][:, 0:256], ACT.Silu).then_inc(silu_ready, 1)
                act.wait_ge(hidt_done, e + 1)
                A(hid_t, misc[2][:, 0:256].rearrange("p (c j s) -> p c j s", c=2, j=4), ACT.Copy).then_inc(hidt_ready, 1)
                act.wait_ge(down_done, e + 1)
                A(ys_rows, misc[3][:, 0:256], ACT.Copy).then_inc(ysr_ready, 1)

            with act.Fori(0, N_EXPERTS // 2) as e:
                expert(e)
            for x in range(XHEADS):
                act.wait_ge(kv_read, 2 * x + 2)
                if x >= 2:
                    act.wait_ge(kmean_done, x - 1)
                A(sq[:, x % 2, :], k_mem[:, 2 * x:2 * x + 2, :], ACT.Square).then_inc(ksq_ready, 1)
                act.wait_ge(kmean_done, x + 1)
                if x >= 2:
                    act.wait_ge(k_ready, 2 * (x - 1))
                A(std[:, x % 2, :], misc[0][:, 0:T], ACT.Sqrt, bias=eps[:, :]).then_inc(kmean_read, 1)
            with act.Fori(N_EXPERTS // 2, N_EXPERTS) as e:
                expert(e)

            squares(NMIX, lat)
            deviation(NMIX)
            for j in range(4):
                n = (FILL["q"], FILL["k"])[j // 2] + j % 2
                fill_done(act, n)
                if j:
                    act.wait_ge(qk_ready, j)
                else:
                    act.wait_ge(sq_used, 4 * (NMIX + 1))
                A(sq[:, j % 2, :], acc[n % 4][:, :], ACT.Square)
                A(qk_g, acc[n % 4][:, :], ACT.Copy, scale=vcol(("q_norm_g", "k_norm_g")[j // 2])) \
                    .then_inc(acc_free[n % 4], 1)
                act.wait_ge(acc_free[n % 4], n // 4 + 1)
                nc.scalar.nop().then_inc(qkg_ready, 1)
                act.wait_ge(qk_prep, j + 1)
                A(region_s[:, 0:512], misc[0][:, :], ACT.Sqrt, bias=eps[:, :]).then_inc(qk_std, 1)
            for i in range(TT):
                n = FILL["v"] + i
                fill_done(act, n)
                A(v_rows[:, i, :], acc[n % 4][:, :], ACT.Copy).then_inc(acc_free[n % 4], 1)
                act.wait_ge(acc_free[n % 4], n // 4 + 1)
                nc.scalar.nop().then_inc(v_ready, 1)
            act.wait_ge(scat_free, N_EXPERTS + 1)
            for f in range(2):
                n = FILL["u"] + f
                fill_done(act, n)
                A(u_pad[:, 2 * f:2 * f + 2, PAD:UP], acc[n % 4][:, :].rearrange("p (g t) -> p g t", g=2), ACT.Copy) \
                    .then_inc(acc_free[n % 4], 1)
                act.wait_ge(acc_free[n % 4], n // 4 + 1)
                nc.scalar.nop().then_inc(u_ready, 1)
            for a in range(HEADS):
                act.wait_ge(negmax, a + 1)
                at = 4 * (a % 2)
                for i, (lo, hi) in enumerate(((0, P), (P, 3 * P))):
                    A(prob[:, a % 2, lo:hi], prob[:, a % 2, lo:hi], ACT.Exp, scale=HD ** -0.5,
                      bias=stat[:, at + i:at + i + 1], accum_out=stat[:, at + 2 + i:at + 3 + i]).then_inc(prob_exp, 1)
                act.wait_ge(pv_done, a + 1)
                lo = HD * (a % 2)
                A(mix[lo:lo + HD, PG + a // 2, :], misc[1][lo:lo + HD, 0:T], ACT.Copy).then_inc(o_ready, 1)
                if a in (4, 6):
                    f = (a - 4) // 2
                    n = FILL["pool"] + f
                    fill_done(act, n)
                    for j in range(2):
                        g = 2 * f + j
                        last = A(mix[:, g, :], acc[n % 4][:, j * T:(j + 1) * T], ACT.Copy, scale=vcol("pool_scale", g, 1))
                    last.then_inc(acc_free[n % 4], 1)
                    act.wait_ge(acc_free[n % 4], n // 4 + 1)
                    nc.scalar.nop().then_inc(pool_ready, 1)
            squares(NXATT, lat)
            deviation(NXATT)
            for x in range(XHEADS):
                n = FILL["xq"] + x
                fill_done(act, n)
                if x >= 2:
                    act.wait_ge(xmean_done, x - 1)
                else:
                    act.wait_ge(sq_used, 4 * (NXATT + 1))
                A(sq[:, x % 2, :], acc[n % 4][:, :], ACT.Square).then_inc(xsq_ready, 1)
                act.wait_ge(xmean_done, x + 1)
                if x >= 2:
                    act.wait_ge(xq_ready, x - 1)
                A(std[:, x % 2, :], misc[0][:, 0:T], ACT.Sqrt, bias=eps[:, :]).then_inc(xstd_ready, 1)
            for x in range(XHEADS):
                act.wait_ge(xnegmax, x + 1)
                at = 4 * (x % 2)
                for i in range(TT):
                    A(prob[:, x % 2, i * T:(i + 1) * T], misc[2 + x % 2][:, i * T:(i + 1) * T], ACT.Exp, scale=XHD ** -0.5,
                      bias=stat[:, at + i:at + i + 1], accum_out=stat[:, at + 2 + i:at + 3 + i])
                act.drain().then_inc(xexp, 1)
                act.wait_ge(xpv_done, x + 1)
                A(o_x[:, 2 * x:2 * x + 2, :], misc[1][:, :], ACT.Copy).then_inc(xo_ready, 1)
            squares(NFFN, lat)
            deviation(NFFN)

            def ffn_step(s, par, first=False):
                act.wait_ge(up2_done, s + 1)
                for g in range(2):
                    w = vec[:, bass.ds(s + (VEC["conv_w"][0] + 2 * 2 * FC + g * FC), 1)]
                    b = vec[:, bass.ds(s + (VEC["conv_b"][0] + g * FC), 1)]
                    last = A(up_z[:, par, g, :], misc[par][:, g * T:(g + 1) * T], ACT.Identity, scale=w, bias=b)
                last.then_inc(z_ready, 1)
                act.wait_ge(conv2_done, s + 1)
                A(up_s[:, par, :], up_z[:, par, 0, :], ACT.Silu).then_inc(silu2_ready, 1)

            with act.Fori(0, FC // 2) as i:
                ffn_step(i * 2, 0)
                ffn_step(i * 2 + 1, 1)

        @block.vector
        def _(ve):
            V = nc.vector
            n_chain = [0]

            def then(ins):
                ins.then_inc(dve, 1)
                n_chain[0] += 1
                ve.wait_ge(dve, n_chain[0])

            def norm(n_norm, src, dst, gain, scaled, base=0):
                ve.wait_ge(mean_free, n_norm + 1)
                then(V.reciprocal(rstd[:, :], std[:, n_norm % 2, :]))
                for k in range(KC):
                    V.scalar_tensor_tensor(out=dst[:, k, :], in0=src[:, k, :], scalar=gain[:, k:k + 1], in1=rstd[:, :],
                                           op0=ALU.mult, op1=ALU.mult).then_inc(scaled, 1)

            def ada_read_block(j):
                ve.wait_ge(ada_t_done, j + 1)
                first_copy = misc[2][:, 0:256].rearrange("p (c j s) -> p j c s", c=2, j=4)[:, :, :, 0]
                V.tensor_tensor(mod[:, j * KC:(j + 1) * KC].rearrange("p (j c) -> p j c", c=2), first_copy,
                                vcol("ada_b", j * KC, KC).rearrange("p (j c) -> p j c", c=2), ALU.add) \
                    .then_inc(ada_read, 1)
                ve.wait_ge(ada_read, j + 1)

            ve.wait_ge(s_vec, 16)
            for f in range(4):
                n = FILL["x_t"] + f
                fill_done(ve, n)
                V.tensor_copy(lat[:, 2 * f:2 * f + 2, :], acc[n % 4][:, :].rearrange("p (c t) -> p c t", c=2)) \
                    .then_inc(acc_free[n % 4], 1)
                ve.wait_ge(acc_free[n % 4], n // 4 + 1)
                V.engine_nop().then_inc(lat_ready[N1], 1)
            ve.wait_ge(mean_free, 1)
            then(V.reciprocal(rstd[:, :], std[:, 0, :]))
            ada_read_block(0)
            ada_read_block(1)
            then(V.scalar_tensor_tensor(out=gain1[:, :], in0=mod[:, KC:2 * KC], scalar=1.0, in1=vcol("norm_g", 0, KC),
                                        op0=ALU.add, op1=ALU.mult))
            for k in range(KC):
                V.scalar_tensor_tensor(out=h[:, k, :], in0=lat[:, k, :], scalar=gain1[:, k:k + 1], in1=rstd[:, :],
                                       op0=ALU.mult, op1=ALU.mult).then_inc(h_scaled, 1)
            ve.wait_ge(h_scaled, KC)
            norm(NMEM, mem_n, mem_n, vcol("norm_mem_g"), h_ready[NMEM])
            ve.wait_ge(cv_zeroed, 2)
            cw = vcol("sc_conv").rearrange("p (w k) -> p w k", w=3)
            ve.wait_ge(s_mem, 16)
            for f in range(4):
                n = FILL["conv_v"] + f
                pair = slice(2 * f, 2 * f + 2)
                ve.wait_ge(acc_free[(FILL["conv_c"] + f) % 4], (FILL["conv_c"] + f) // 4 + 1)
                fill_done(ve, n)
                V.tensor_tensor(cv[:, pair, 1:T + 1], acc[n % 4][:, :].rearrange("p (c t) -> p c t", c=2),
                                gate_c[:, pair, :], ALU.mult).then_inc(acc_free[n % 4], 1)
                ve.wait_ge(acc_free[n % 4], n // 4 + 1)
                for k in range(2 * f, 2 * f + 2):
                    ins = V.tensor_scalar(conv[:, k, :], cv[:, k, 0:T], cw[:, 0, k:k + 1], None, ALU.mult)
                    if k % 2:
                        then(ins)
                for w in (1, 2):
                    for k in range(2 * f, 2 * f + 2):
                        ins = V.scalar_tensor_tensor(out=conv[:, k, :], in0=cv[:, k, w:w + T], scalar=cw[:, w, k:k + 1],
                                                     in1=conv[:, k, :], op0=ALU.mult, op1=ALU.add)
                        if k % 2:
                            then(ins)
                V.tensor_tensor(conv[:, pair, :], conv[:, pair, :], gate_b[:, pair, :], ALU.mult).then_inc(conv_ready, 2)
            ada_read_block(2)
            for f in range(4):
                n = FILL["conv_out"] + f
                fill_done(ve, n)
                for c in range(2):
                    k = 2 * f + c
                    last = V.scalar_tensor_tensor(out=lat[:, k, :], in0=acc[n % 4][:, c * T:(c + 1) * T],
                                                  scalar=mod[:, 2 * KC + k:2 * KC + k + 1], in1=lat[:, k, :],
                                                  op0=ALU.mult, op1=ALU.add)
                last.then_inc(acc_free[n % 4], 1)
                ve.wait_ge(acc_free[n % 4], n // 4 + 1)
                V.engine_nop().then_inc(lat_ready[N2], 1)
            ada_read_block(3)
            ada_read_block(4)
            then(V.scalar_tensor_tensor(out=gain2[:, :], in0=mod[:, 4 * KC:5 * KC], scalar=1.0, in1=vcol("norm_g", KC, KC),
                                        op0=ALU.add, op1=ALU.mult))
            norm(N2, lat, h, gain2, h_scaled)
            ada_read_block(5)
            ve.wait_ge(logits_done, 1)
            then(V.tensor_reduce(stat[:, 4:6], misc[3][:, 0:TT * N_EXPERTS].rearrange("p (i e) -> p i e", i=TT), AX, ALU.max))
            V.tensor_scalar(stat[:, 0:2], stat[:, 4:6], -1.0, None, ALU.mult).then_inc(negmax_r, 1)
            ve.wait_ge(exp_done, 2)
            then(V.reciprocal(stat[:, 6:8], stat[:, 2:4]))
            for i in range(TT):
                last = V.tensor_scalar(aff[:, i, :], aff_e[:, i, :], stat[:, 6 + i:7 + i], None, ALU.mult)
            last.then_inc(aff_ready, 1)
            V.memset(ones_r, 1.0)
            ve.wait_ge(afft_done, 1)
            then(V.tensor_copy(top_work[:, :], misc[2][0:N_EXPERTS, 0:T]))
            for r in range(CAP // 8):
                then(V.max(top8[:, :], top_work[:, :]))
                then(V.match_replace(top_work[:, :], top8[:, :], top_work[:, :], -1.0))
            then(V.tensor_scalar(chosen[:, :], top_work[:, :], 0.0, None, ALU.is_lt))
            then(V.tensor_tensor_scan(count[:, :], ones_r[:, :], chosen[:, :], 0.0, ALU.mult, ALU.add))
            then(V.tensor_tensor(slot_t[:, :], count[:, :], chosen[:, :], ALU.mult))
            V.tensor_scalar(slot_t[:, :], slot_t[:, :], -1.0, None, ALU.add).then_inc(slot_t_ready, 1)
            ve.wait_ge(slot_done, 1)
            then(V.tensor_copy(slot[:, :, :], misc[3][:, 0:TT * N_EXPERTS].rearrange("p (i e) -> p i e", i=TT)))
            iota = table("iota")[:, None, :].to_broadcast([P, N_EXPERTS, CAP])
            for i in range(TT):
                last = V.tensor_tensor(sel[:, i, :, :], iota, slot[:, i, :, None].to_broadcast([P, N_EXPERTS, CAP]),
                                       ALU.is_equal)
            last.then_inc(sel_ready, 1)
            ve.wait_ge(sel_ready, 1)

            def gate_pair(p):
                if p >= 2:
                    ve.wait_ge(scat_t_done, p - 1)
                for i in range(TT):
                    for j in range(2):
                        e = 2 * p + j
                        last = V.tensor_scalar(sel_g[:, p % 2, i, j, :, :],
                                               sel[:, i, e, None, :].to_broadcast([P, 4, CAP]),
                                               aff[:, i, e:e + 1], None, ALU.mult)
                last.then_inc(selg_ready, 1)

            gate_pair(0)
            gate_pair(1)
            for k in range(1, KC, 2):
                n = FILL["gather"] + k
                fill_done(ve, n)
                V.tensor_copy(xs[:, k, :], acc[n % 4][:, :]).then_inc(acc_free[n % 4], 1)
            for p in range(2, N_EXPERTS // 2):
                gate_pair(p)
            for b in range(4):
                n = FILL["gather"] + 4 + b
                ve.wait_ge(acc_free[n % 4], n // 4 + 1)
            for b in range(4):
                V.memset(acc[b][:, :], 0.0).then_inc(y_zeroed, 1)

            def expert(e, values):
                V.tensor_copy(xs_e[:, :, :], xs[:, :, bass.ds(e * CAP, CAP)]).then_inc(xse_ready, 1)
                ve.wait_ge(silu_ready, e + 1)
                ve.wait_ge(up_done, e + 1)
                V.tensor_tensor(hid, silu_g, misc[1][:, 0:256], ALU.mult).then_inc(hid_ready, 1)
                ve.wait_ge(kvw_used, e + 1)
                if not values:
                    V.tensor_copy(k_mem[:, bass.ds(e, 1), :], misc[0][:, None, 0:T]).then_inc(kv_read, 1)
                else:
                    V.tensor_copy(v_mem[:, :, bass.ds((e - N_EXPERTS // 2) * P, P)],
                                  misc[0][:, 0:T].rearrange("p (i n) -> p i n", i=TT)).then_inc(kv_read, 1)
                ve.wait_ge(scat_free, e + 1)
                V.tensor_copy(scat_e[:, None, :], scatter[:, bass.ds(e, 1), :]).then_inc(scate_ready, 1)

            with ve.Fori(0, N_EXPERTS // 2) as e:
                expert(e, False)
            for x in range(XHEADS):
                ve.wait_ge(kmean_read, x + 1)
                then(V.reciprocal(rstd[:, :], std[:, x % 2, :]))
                for c in range(2):
                    k = 2 * x + c
                    V.scalar_tensor_tensor(out=k_mem[:, k, :], in0=k_mem[:, k, :], scalar=vcol("xk_norm_g", c, 1),
                                           in1=rstd[:, :], op0=ALU.mult, op1=ALU.mult).then_inc(k_ready, 1)
                ve.wait_ge(k_ready, 2 * x + 2)
            with ve.Fori(N_EXPERTS // 2, N_EXPERTS) as e:
                expert(e, True)
            ve.wait_ge(scat_free, N_EXPERTS + 1)
            for k in range(KC):
                ins = V.scalar_tensor_tensor(out=lat[:, k, :], in0=acc[k // 2][:, (k % 2) * T:(k % 2 + 1) * T],
                                             scalar=mod[:, 5 * KC + k:5 * KC + k + 1], in1=lat[:, k, :],
                                             op0=ALU.mult, op1=ALU.add)
                if k % 2:
                    ins.then_inc(lat_ready[NMIX], 1)
            norm(NMIX, lat, h, vcol("norm_mix_g"), h_ready[NMIX])

            def two(ap):
                return ap[:, None, :].to_broadcast([P, 2, T])

            for j in range(4):
                dst = (q_rot, k_rot)[j // 2][:, 2 * (j % 2):2 * (j % 2) + 2, :]
                t3 = qk_t.rearrange("p (c t) -> p c t", c=2)
                ve.wait_ge(qkg_ready, j + 1)
                ve.wait_ge(qk_prep, j + 1)
                V.tensor_tensor(dst, misc[1][:, :].rearrange("p (c t) -> p c t", c=2), two(table("sin")), ALU.mult) \
                    .then_inc(qk_read, 1)
                then(V.tensor_tensor(t3, qk_g.rearrange("p (c t) -> p c t", c=2), two(table("cos")), ALU.mult))
                ve.wait_ge(qk_read, j + 1)
                V.tensor_tensor(dst, dst, t3, ALU.add)
                ve.wait_ge(qk_std, j + 1)
                then(V.reciprocal(region_s[:, 512:1024], region_s[:, 0:512]))
                V.tensor_tensor(dst, dst, region_s[:, 512:1024].rearrange("p (c t) -> p c t", c=2), ALU.mult) \
                    .then_inc(qk_ready, 1)
                ve.wait_ge(qk_ready, j + 1)
            for a in range(HEADS):
                s = prob[:, a % 2, 0:3 * P]
                at = 4 * (a % 2)
                ve.wait_ge(score_done, a + 1)
                if a >= 2:
                    ve.wait_ge(probt_done, a - 1)
                V.tensor_tensor(s, misc[2 + a % 2][:, 0:3 * P], table("causal"), ALU.add).then_inc(masked, 1)
                ve.wait_ge(masked, a + 1)
                V.tensor_reduce(stat[:, 16:17], s[:, 0:P], AX, ALU.max)
                then(V.tensor_reduce(stat[:, 17:18], s[:, P:3 * P], AX, ALU.max))
                V.tensor_scalar(stat[:, at:at + 2], stat[:, 16:18], -HD ** -0.5, None, ALU.mult).then_inc(negmax, 1)
                ve.wait_ge(prob_exp, 2 * a + 2)
                then(V.reciprocal(stat[:, 18:20], stat[:, at + 2:at + 4]))
                V.tensor_scalar(s[:, 0:P], s[:, 0:P], stat[:, 18:19], None, ALU.mult)
                V.tensor_scalar(s[:, P:3 * P], s[:, P:3 * P], stat[:, 19:20], None, ALU.mult).then_inc(prob_ready, 1)
                ve.wait_ge(probt_done, a + 1)
                V.tensor_copy(prob_t[:, a % 2, 0:3 * P], misc[0][:, 0:3 * P]).then_inc(probt_ready, 1)

            def add_to_lat(name, ready):
                for f in range(4):
                    n = FILL[name] + f
                    fill_done(ve, n)
                    V.tensor_tensor(lat[:, 2 * f:2 * f + 2, :], acc[n % 4][:, :].rearrange("p (c t) -> p c t", c=2),
                                    lat[:, 2 * f:2 * f + 2, :], ALU.add).then_inc(acc_free[n % 4], 1)
                    ve.wait_ge(acc_free[n % 4], n // 4 + 1)
                    V.engine_nop().then_inc(ready, 1)

            add_to_lat("mix_out", lat_ready[NXATT])
            norm(NXATT, lat, h, vcol("norm_xattn_g"), h_ready[NXATT])
            for x in range(XHEADS):
                n = FILL["xq"] + x
                ve.wait_ge(xstd_ready, x + 1)
                if x == 0:
                    ve.wait_ge(h_ready[NXATT], KC)
                then(V.reciprocal(rstd[:, :], std[:, x % 2, :]))
                for c in range(2):
                    last = V.scalar_tensor_tensor(out=q_x[:, 2 * x + c, :], in0=acc[n % 4][:, c * T:(c + 1) * T],
                                                  scalar=vcol("xq_norm_g", c, 1), in1=rstd[:, :],
                                                  op0=ALU.mult, op1=ALU.mult)
                last.then_inc(acc_free[n % 4], 1)
                ve.wait_ge(acc_free[n % 4], n // 4 + 1)
                V.engine_nop().then_inc(xq_ready, 1)
            for x in range(XHEADS):
                s = prob[:, x % 2, :].rearrange("p (i m) -> p i m", i=TT)
                at = 4 * (x % 2)
                ve.wait_ge(xscore_done, x + 1)
                then(V.tensor_reduce(stat[:, 16:18], misc[2 + x % 2][:, :].rearrange("p (i m) -> p i m", i=TT), AX, ALU.max))
                if x >= 2:
                    ve.wait_ge(xprobt_done, x - 1)
                V.tensor_scalar(stat[:, at:at + 2], stat[:, 16:18], -XHD ** -0.5, None, ALU.mult).then_inc(xnegmax, 1)
                ve.wait_ge(xexp, x + 1)
                then(V.reciprocal(stat[:, 18:20], stat[:, at + 2:at + 4]))
                for i in range(TT):
                    last = V.tensor_scalar(s[:, i, :], s[:, i, :], stat[:, 18 + i:19 + i], None, ALU.mult)
                last.then_inc(xprob_ready, 1)
                ve.wait_ge(xprobt_done, x + 1)
                V.tensor_copy(prob_t[:, x % 2, :], misc[0][:, :]).then_inc(xprobt_ready, 1)
            add_to_lat("xo", lat_ready[NFFN])
            for b in range(4):
                V.memset(acc[b][:, :], 0.0).then_inc(ffn_zeroed, 1)
            norm(NFFN, lat, h, vcol("norm_ffn_g"), h_ready[NFFN])

            def ffn_step(s, par, base):
                ve.wait_ge(z_ready, s + 1)
                for w in (1, 0):
                    d = 2 - w
                    for g in range(2):
                        tap = vec[:, bass.ds(s + (VEC["conv_w"][0] + w * 2 * FC + g * FC), 1)]
                        ins = V.scalar_tensor_tensor(out=up_z[:, par, g, d:T], in0=misc[par][:, g * T:(g + 1) * T - d],
                                                     scalar=tap, in1=up_z[:, par, g, d:T], op0=ALU.mult, op1=ALU.add)
                    if w:
                        ins.then_inc(dve, 1)
                        ve.wait_ge(dve, s + base)
                ins.then_inc(conv2_done, 1)
                ve.wait_ge(conv2_done, s + 1)
                ve.wait_ge(silu2_ready, s + 1)
                V.tensor_tensor(up_h[:, par, :], up_s[:, par, :], up_z[:, par, 1, :], ALU.mult).then_inc(act_ready, 1)

            base = n_chain[0] + 1
            with ve.Fori(0, FC // 2) as i:
                ffn_step(i * 2, 0, base)
                ffn_step(i * 2 + 1, 1, base)
            ve.wait_ge(ffn_w_used, FC)
            for f in range(4):
                V.tensor_tensor(lat[:, 2 * f:2 * f + 2, :], acc[f][:, :].rearrange("p (c t) -> p c t", c=2),
                                lat[:, 2 * f:2 * f + 2, :], ALU.add).then_inc(lat_final, 1)
            for f in range(4):
                n = FILL["rows"] + f
                fill_done(ve, n)
                V.tensor_copy(out_rows[:, :, f * 256:(f + 1) * 256],
                              acc[n % 4][:, :].rearrange("p (i d) -> p i d", i=TT)).then_inc(out_ready, 1)


def _tables(np):
    tab = np.zeros((P, TAB_COLS), np.float32)

    def put(name, value):
        at, n = TAB[name]
        tab[:, at:at + n] = value

    put("ident", np.eye(P))
    put("iota", np.arange(CAP)[None])
    half = HD // 2
    rot = np.zeros((P, P))
    head = np.zeros((P, P))
    for m in range(P):
        base, j = m // HD * HD, m % HD
        if j < half:
            rot[base + j + half, m] = -1.0
        else:
            rot[base + j - half, m] = 1.0
        head[base:base + HD, m] = 1.0 / HD
    put("rot", rot)
    put("headmean", head)
    inv_freq = (np.float32(10000.0) ** (-np.arange(half, dtype=np.float32) / np.float32(half))).astype(np.float32)
    ang = (np.arange(T, dtype=np.float32)[None, :] * inv_freq[np.arange(P) % half][:, None]).astype(np.float32)
    put("cos", np.cos(ang.astype(np.float64)))
    put("sin", np.sin(ang.astype(np.float64)))
    q, k = np.arange(P)[:, None], np.arange(P)[None, :]
    diag = np.where(k <= q, 0.0, -1e30)
    put("causal", np.concatenate([diag, np.zeros((P, P)), diag], 1))
    put("invcnt", np.concatenate([1.0 / np.minimum(np.arange(PAD) + 1, w) for w in POOL_WINDOWS])[None])
    return tab


def kernel(**inputs):
    import numpy as np
    import concourse.bacc as bacc
    from concourse.bass_utils import run_bass_kernel_spmd

    a = {n: np.asarray(v) for n, v in inputs.items()}

    def cols(v):
        return v.reshape(-1, P).T

    vectors = np.concatenate([
        cols(a["c"]), cols(a["ada_b"]), cols(a["norm_g"]), cols(a["sc_conv"]), cols(a["norm_mem_g_2"]),
        a["moe_router"][0].reshape(KC, P, N_EXPERTS).transpose(1, 0, 2).reshape(P, -1),
        cols(a["norm_mix_g_2"]), cols(a["pool_scale_2"]),
        np.concatenate([a["q_norm_g_2"][0]] * 2)[:, None], np.concatenate([a["k_norm_g_2"][0]] * 2)[:, None],
        cols(a["norm_xattn_g_2"]), cols(a["xq_norm_g_2"]), cols(a["xk_norm_g_2"]), cols(a["norm_ffn_g_2"]),
        cols(a["conv_w_2"]), cols(a["conv_b_2"])], axis=1)
    arrays = {"vectors": vectors, "tables": _tables(np), "x": a["x"], "mem": a["mem_2"], "pool_w": a["pool_w_2"],
              "ada_w": a["ada_w"], "sc_w_in": a["sc_w_in"], "sc_w_out": a["sc_w_out"], "moe_w_gate": a["moe_w_gate"],
              "moe_w_up": a["moe_w_up"], "moe_w_down": a["moe_w_down"], "w_in": a["w_in_2"], "w_out": a["w_out_2"],
              "w_xq": a["w_xq_2"], "w_xkv": a["w_xkv_2"], "w_xo": a["w_xo_2"], "w_up": a["w_up_2"],
              "w_down": a["w_down_2"]}
    nc = bacc.Bacc("TRN2", target_bir_lowering=False, num_devices=1)
    feeds, io = {}, {}
    for name, v in arrays.items():
        v = np.ascontiguousarray(v)
        feeds[f"in_{name}"] = v
        io[name] = nc.dram_tensor(f"in_{name}", v.shape, F32, kind="ExternalInput").ap()
    io["out"] = nc.dram_tensor("out", (1, T, D), F32, kind="ExternalOutput").ap()
    program(nc, io)
    r = run_bass_kernel_spmd(nc, [feeds], core_ids=[0])
    return r.results[0]["out"]
```

```python
from contextlib import ExitStack

import concourse.bass as bass
from concourse import mybir

F32 = mybir.dt.float32
F32R = mybir.dt.float32r
ACT = mybir.ActivationFunctionType
ALU = mybir.AluOpType
AX = mybir.AxisListType.X

P = 128
D = 1024
T = 256
KC = D // P
TT = T // P
EPS = 1e-6
RING = 3

N_EXPERTS = 16
CAP = 2 * T // N_EXPERTS
POOL_WINDOWS = (2, 4, 8, 16)
PG = len(POOL_WINDOWS)
PAD = 16
HEADS, HD = 8, 64
XHEADS, XHD = 4, 256
FC = 2816 // P
FFN_SLOTS = 2

VEC = {}
_at = 0
for _name, _n in (("c", KC), ("ada_b", 6 * KC), ("norm_g", 2 * KC), ("sc_conv", 3 * KC), ("norm_mem_g", KC),
                  ("router", KC * N_EXPERTS), ("norm_mix_g", KC), ("pool_scale", PG), ("q_norm_g", 1),
                  ("k_norm_g", 1), ("norm_xattn_g", KC), ("xq_norm_g", 2), ("xk_norm_g", 2), ("norm_ffn_g", KC),
                  ("conv_w", 3 * 2 * FC), ("conv_b", 2 * FC)):
    VEC[_name] = (_at, _n)
    _at += _n
VEC_COLS = _at

TAB = {}
_at = 0
for _name, _n in (("ident", P), ("iota", CAP), ("rot", P), ("headmean", P), ("cos", T), ("sin", T),
                  ("causal", 3 * P), ("invcnt", PG * PAD)):
    TAB[_name] = (_at, _n)
    _at += _n
TAB_COLS = _at

BLOCKS = ["shift1", "scale1", "sc_b", "sc_c", "sc_v", "gate1", "sc_out", "shift2", "scale2", "gate2"]
MOE0 = len(BLOCKS)
BLOCK = {n: i for i, n in enumerate(BLOCKS)}
for _i, _name in enumerate(("in_uq", "in_kv", "mix_out", "xq", "xo")):
    BLOCK[_name] = MOE0 + 3 * N_EXPERTS + _i

FILL = {}
_at = 0
for _name, _n in (("x_t", 4), ("mem_t", 4), ("conv_b", 4), ("conv_c", 4), ("conv_v", 4), ("conv_out", 4),
                  ("h2_rows", 4), ("gather", 8), ("q", 2), ("k", 2), ("v", 2), ("u", 2), ("pool", 2),
                  ("mix_out", 4), ("xq", 4), ("xo", 4), ("rows", 4)):
    FILL[_name] = _at
    _at += _n

ADA = ["shift1", "scale1", "gate1", "shift2", "scale2", "gate2"]
LAST_FILL = {"sc_b": FILL["conv_b"] + 3, "sc_c": FILL["conv_c"] + 3, "sc_v": FILL["conv_v"] + 3,
             "sc_out": FILL["conv_out"] + 3, "in_uq": FILL["u"] + 1, "in_kv": FILL["v"] + 1,
             "mix_out": FILL["mix_out"] + 3, "xq": FILL["xq"] + 3, "xo": FILL["xo"] + 3}

N1, NMEM, N2, NMIX, NXATT, NFFN = range(6)


def program(nc, io):
    with ExitStack() as ctx:
        def sb(name, shape):
            return ctx.enter_context(nc.sbuf_tensor(name, shape, F32))

        def bank(name):
            return ctx.enter_context(nc.psum_tensor(name, [P, 512], F32))

        def sem(name):
            return ctx.enter_context(nc.semaphore(name))

        def overlay(*specs):
            with ExitStack() as place:
                return [place.enter_context(nc.sbuf_tensor(name, shape, F32R)) for name, shape in specs]

        ring, ffn_hi, ffn_lo = [], [], []
        for i in range(RING):
            if i:
                for part, tensor in zip((ffn_hi, ffn_lo), overlay((f"ffn_w_hi{i}", [P, 3, D]), (f"ffn_w_lo{i}", [P, 3, D]))):
                    part.append(tensor)
            ring.append(sb(f"ring{i}", [P, KC, D]))
        lat = sb("lat", [P, KC, T])
        h = sb("h", [P, KC, T])
        (x_hi,) = overlay(("x_hi", [P, KC, T]))
        mem_n = sb("mem_n", [P, KC, T])
        (x_lo,) = overlay(("x_lo", [P, KC, T]))
        k_mem = sb("k_mem", [P, KC, T])
        v_mem = sb("v_mem", [P, TT, D])
        act_hi, act_lo = overlay(("act_hi", [P, 2, T]), ("act_lo", [P, 2, T]))
        kv_w = sb("kv_w", [P, KC, P])
        region_a = sb("region_a", [P, 4096])
        region_b = sb("region_b", [P, 4352])
        region_c = sb("region_c", [P, 2048])
        region_s = sb("region_s", [P, 2048])
        sq = sb("sq", [P, 2, 512])
        std = sb("std", [P, 2, T])
        rstd = sb("rstd", [P, T])
        eps = sb("eps", [P, 1])
        vec = sb("vec", [P, VEC_COLS])
        tab = sb("tab", [P, TAB_COLS])
        pool_w = sb("pool_w", [P, PG, P])
        ones_d = sb("ones_d", [P, P])
        ones_x = sb("ones_x", [P, P])
        silu_c = sb("silu_c", [P, KC])
        mod = sb("mod", [P, 6 * KC])
        gain1 = sb("gain1", [P, KC])
        gain2 = sb("gain2", [P, KC])
        aff = sb("aff", [P, TT, N_EXPERTS])
        aff_e = sb("aff_e", [P, TT, N_EXPERTS])
        top8 = sb("top8", [N_EXPERTS, 8])
        slot = sb("slot", [P, TT, N_EXPERTS])
        stat = sb("stat", [P, 64])

        def chunks(ap, n):
            return ap.rearrange("p (k t) -> p k t", k=n)

        x_rows = chunks(region_c[:, :], TT)
        mem_rows = chunks(region_b[:, 2304:4352], TT)
        gate_b = chunks(region_a[:, 0:2048], KC)
        gate_c = chunks(region_a[:, 2048:4096], KC)
        cv = chunks(region_b[:, 0:KC * (T + 2)], KC)
        conv = chunks(region_c[:, :], KC)
        sel = region_s[:, 0:1024].rearrange("p (i e s) -> p i e s", i=TT, s=CAP)
        sel_g = region_s[:, 1024:2048].rearrange("p (b i e j s) -> p b i e j s", b=2, i=TT, e=2, j=4)
        h2_rows = chunks(region_c[:, :], TT)
        ada_rows = chunks(region_s[:, 0:512], 2)
        xs = chunks(region_a[:, :], KC)
        scatter = region_b[:, 0:N_EXPERTS * T].rearrange("p (e t) -> p e t", e=N_EXPERTS)
        xs_e = chunks(region_c[:, 0:256], KC)
        silu_g, hid, ys_rows, scat_e = (region_c[:, 256 * i:256 * (i + 1)] for i in range(1, 5))
        hid_t = region_c[:, 1280:1536].rearrange("p (c j s) -> p c j s", c=2, j=4)
        top_work, chosen, count, slot_t, ones_r = (region_b[0:N_EXPERTS, T * i:T * (i + 1)] for i in range(5))
        q_rot = chunks(region_a[:, 0:1024], 4)
        k_rot = chunks(region_a[:, 1024:2048], 4)
        v_rows = chunks(region_a[:, 2048:3072], TT)
        qk_g = region_a[:, 3072:3584]
        qk_t = region_a[:, 3584:4096]
        UP = PAD + T
        u_pad = chunks(region_b[:, 0:PG * UP], PG)
        win_a = chunks(region_b[:, PG * UP:2 * PG * UP], PG)
        win_b = chunks(region_b[:, 2 * PG * UP:3 * PG * UP], PG)
        pooled = chunks(region_b[:, 3 * PG * UP:3 * PG * UP + PG * T], PG)
        mix = chunks(region_c[:, :], KC)
        prob = chunks(region_s[:, 0:1024], 2)
        prob_t = chunks(region_s[:, 1024:2048], 2)
        q_x = chunks(region_a[:, 0:2048], KC)
        o_x = chunks(region_c[:, :], KC)
        up_z = region_a[:, 0:1024].rearrange("p (s g t) -> p s g t", s=2, g=2)
        up_s = chunks(region_a[:, 1024:1536], 2)
        up_h = chunks(region_a[:, 1536:2048], 2)
        out_rows = chunks(region_c[:, :], TT)
        ffn_up = [[ring[0][:, 2 * s + g, :].rearrange("p (k n) -> p k n", k=KC) for g in range(2)]
                  for s in range(FFN_SLOTS)]
        ffn_down = [ring[0][:, 2 * FFN_SLOTS + s, :] for s in range(FFN_SLOTS)]

        def ffn_raw(slot, part):
            return ffn_down[slot] if part == 2 else ring[0][:, 2 * slot + part, :]

        acc = [bank(f"acc{b}") for b in range(4)]
        misc = [bank(f"misc{b}") for b in range(4)]

        def vcol(name, i=0, n=None):
            at, size = VEC[name]
            return vec[:, at + i:at + (size if n is None else i + n)]

        def table(name):
            at, size = TAB[name]
            return tab[:, at:at + size]

        ident = table("ident")
        router = vcol("router").rearrange("p (k e) -> p k e", k=KC)

        s_vec, s_tab, s_x, s_mem, s_poolw = (sem(n) for n in ("vec_in", "tab_in", "x_in", "mem_in", "poolw_in"))
        landed = [sem(f"ring_landed{i}") for i in range(RING)]
        acc_done = [sem(f"acc_done{b}") for b in range(4)]
        acc_free = [sem(f"acc_free{b}") for b in range(4)]
        ones_set = sem("ones_set")
        silu_c_ready = sem("silu_c_ready")
        sq_ready, sq_used = sem("sq_ready"), sem("sq_used")
        mean_ready, mean_free = sem("mean_ready"), sem("mean_free")
        lat_ready = [sem(f"norm_in_ready{n}") for n in range(6)]
        h_scaled = sem("h_scaled")
        h_ready = [sem(f"h_ready{n}") for n in range(6)]
        ada_done, ada_rows_ready, ada_t_done, ada_read = (
            sem(n) for n in ("ada_rows_done", "ada_rows_ready", "ada_t_done", "ada_read"))
        cv_zeroed, conv_ready = (sem(n) for n in ("cv_zeroed", "conv_ready"))
        dve = sem("vector_chain")
        poolc = sem("gpsimd_chain")

        def block_wait(eng, name):
            m = BLOCK[name]
            eng.wait_ge(landed[m % RING], 16 * (m // RING + 1))

        def block_done(eng, m):
            if m >= MOE0 and m < MOE0 + 3 * N_EXPERTS:
                e, j = divmod(m - MOE0, 3)
                eng.wait_ge((gate_done, up_done, down_done)[j], e + 1)
                return
            name = next(n for n, i in BLOCK.items() if i == m)
            if name in ADA:
                eng.wait_ge(ada_done, ADA.index(name) + 1)
            else:
                n = LAST_FILL[name]
                eng.wait_ge(acc_done[n % 4], n // 4 + 1)

        def block_slot(name):
            return ring[BLOCK[name] % RING][:, :, :]

        def fill_done(eng, n):
            eng.wait_ge(acc_done[n % 4], n // 4 + 1)

        def fill_free(eng, n):
            if n >= 4:
                eng.wait_ge(acc_free[n % 4], n // 4)

        logits_done, exp_done, aff_ready, afft_done, slot_t_ready, slot_done = (
            sem(n) for n in ("logits_done", "aff_exp_done", "aff_ready", "aff_t_done", "slot_t_ready", "slot_done"))
        negmax_r = sem("router_negmax")
        sel_ready, selg_ready, rows_ready, xs_ready, scat_t_done, scat_ready = (
            sem(n) for n in ("sel_ready", "sel_g_ready", "h2_rows_ready", "xs_ready", "scatter_t_done", "scatter_ready"))
        logits_read = sem("logits_read")
        slot_read = sem("slot_read")
        y_zeroed = sem("y_zeroed")
        xs_free, xse_ready = sem("xs_e_free"), sem("xs_e_ready")
        gate_done, up_done, silu_ready, hid_ready, hidt_done, hidt_ready, down_done, ysr_ready = (
            sem(n) for n in ("gate_done", "up_done", "silu_ready", "hid_ready", "hid_t_done", "hid_t_ready",
                             "down_done", "ys_rows_ready"))
        scate_ready, scat_free = sem("scatter_e_ready"), sem("scatter_e_free")
        kvw_in, kvw_used, kv_read = sem("kv_w_in"), sem("kv_w_used"), sem("kv_read")
        ksq_ready, kmean_done, kmean_read, k_ready = (sem(n) for n in ("k_sq_ready", "k_mean_done", "k_mean_read", "k_mem_ready"))
        qkg_ready, qk_prep, qk_ready = sem("qk_gained"), sem("qk_mean_rot_done"), sem("qk_ready")
        qk_read, qk_std = sem("qk_rot_read"), sem("qk_std_ready")
        xstd_ready = sem("xq_std_ready")
        v_ready, u_ready, u_zeroed, pooled_ready, pool_ready = (
            sem(n) for n in ("v_rows_ready", "u_ready", "u_zeroed", "pooled_ready", "pool_mix_ready"))
        score_done, masked, negmax, prob_exp, prob_ready, probt_done, probt_ready, pv_done, o_ready = (
            sem(n) for n in ("score_done", "scores_masked", "negmax_ready", "prob_exp", "prob_ready", "prob_t_done",
                             "prob_t_ready", "pv_done", "attn_out_ready"))
        xsq_ready, xmean_done, xq_ready = sem("xq_sq_ready"), sem("xq_mean_done"), sem("xq_ready")
        xscore_done, xnegmax, xexp, xprob_ready, xprobt_done, xprobt_ready, xpv_done, xo_ready = (
            sem(n) for n in ("xscore_done", "xnegmax_ready", "xprob_exp", "xprob_ready", "xprob_t_done",
                             "xprob_t_ready", "xpv_done", "xattn_out_ready"))
        ffn_up_in = [sem(f"ffn_up_w_in{s}") for s in range(FFN_SLOTS)]
        ffn_down_in = [sem(f"ffn_down_w_in{s}") for s in range(FFN_SLOTS)]
        w_hi, w_lo = ([sem(f"ffn_{n}_{part}_ready") for n in ("gate", "value", "down")] for part in ("hi", "lo"))
        x_hi_ready, x_lo_ready = sem("x_hi_ready"), sem("x_lo_ready")
        hid_f, act_hi_ready = sem("ffn_hidden_ready"), sem("ffn_act_hi_ready")
        up2_done, z_ready, conv2_done, silu2_ready, act_ready, ffn_zeroed, down2_done = (
            sem(n) for n in ("ffn_up_done", "ffn_z_ready", "ffn_conv_done", "ffn_silu_ready", "ffn_act_ready",
                             "ffn_acc_zeroed", "ffn_down_done"))
        lat_final, out_ready, s_out = sem("lat_final"), sem("out_rows_ready"), sem("out_stored")

        def wblock(ap):
            return ap.rearrange("(k p) n -> p k n", p=P)

        ada = io["ada_w"][0]
        stream = {"shift1": ada[:, 0:D], "scale1": ada[:, D:2 * D], "gate1": ada[:, 2 * D:3 * D],
                  "shift2": ada[:, 3 * D:4 * D], "scale2": ada[:, 4 * D:5 * D], "gate2": ada[:, 5 * D:6 * D],
                  "sc_b": io["sc_w_in"][0][:, 0:D], "sc_c": io["sc_w_in"][0][:, D:2 * D],
                  "sc_v": io["sc_w_in"][0][:, 2 * D:3 * D], "sc_out": io["sc_w_out"][0],
                  "in_uq": io["w_in"][0][:, 0:D], "in_kv": io["w_in"][0][:, D:2 * D],
                  "mix_out": io["w_out"][0], "xq": io["w_xq"][0], "xo": io["w_xo"][0]}

        block = ctx.enter_context(nc.Block())

        @block.sync
        def _(sp):
            def load_block(name):
                m = BLOCK[name]
                if m >= RING:
                    block_done(sp, m - RING)
                sp.dma_start(block_slot(name), wblock(stream[name])).then_inc(landed[m % RING], 16)

            sp.dma_start(x_rows, io["x"][0].rearrange("(i p) d -> p i d", p=P)).then_inc(s_x, 16)
            sp.dma_start(vec[:, :], io["vectors"]).then_inc(s_vec, 16)
            for name in BLOCKS[:2]:
                load_block(name)
            sp.dma_start(mem_rows, io["mem"][0].rearrange("(i p) d -> p i d", p=P)).then_inc(s_mem, 16)
            for name in BLOCKS[2:]:
                load_block(name)
            experts = (io["moe_w_gate"], io["moe_w_up"], io["moe_w_down"])
            for j, w in enumerate(experts):
                block_done(sp, MOE0 + j - RING)
                sp.dma_start(ring[(MOE0 + j) % RING][:, :, :], wblock(w[0, 0])).then_inc(landed[(MOE0 + j) % RING], 16)
            with sp.Fori(1, N_EXPERTS) as e:
                for j, (w, done) in enumerate(zip(experts, (gate_done, up_done, down_done))):
                    m = MOE0 + j
                    sp.wait_ge(done, e)
                    sp.dma_start(ring[m % RING][:, :, :],
                                 w[0, bass.ds(e, 1)].rearrange("o (k p) n -> p (o k) n", p=P)) \
                      .then_inc(landed[m % RING], 16)
            for name in ("in_uq", "in_kv", "mix_out", "xq", "xo"):
                load_block(name)
            w_up, w_down = io["w_up"][0], io["w_down"][0]

            def load_up(s, slot):
                for g in range(2):
                    sp.dma_start(ffn_up[slot][g],
                                 w_up[:, bass.ds(s * P + g * FC * P, P)].rearrange("(k p) n -> p k n", p=P)) \
                      .then_inc(ffn_up_in[slot], 16)

            def load_down(s, slot):
                sp.dma_start(ffn_down[slot], w_down[bass.ds(s * P, P), :]).then_inc(ffn_down_in[slot], 16)

            block_done(sp, BLOCK["mix_out"])
            for s in range(FFN_SLOTS):
                load_up(s, s)
                load_down(s, s)
            with sp.Fori(1, FC // FFN_SLOTS) as i:
                for slot in range(FFN_SLOTS):
                    sp.wait_ge(w_lo[1], i * FFN_SLOTS + (slot - FFN_SLOTS + 1))
                    load_up(i * FFN_SLOTS + slot, slot)
                    sp.wait_ge(w_lo[2], i * FFN_SLOTS + (slot - FFN_SLOTS + 1))
                    load_down(i * FFN_SLOTS + slot, slot)
            out_v = io["out"][0].rearrange("(i p) d -> p i d", p=P)
            for f in range(4):
                sp.wait_ge(out_ready, f + 1)
                sp.dma_start(out_v[:, :, f * 256:(f + 1) * 256], out_rows[:, :, f * 256:(f + 1) * 256]) \
                  .then_inc(s_out, 16)
            sp.wait_ge(s_out, 64)

        @block.gpsimd
        def _(pool):
            nc.gpsimd.memset(ones_d[:, :], 1.0 / D).then_inc(ones_set, 1)
            nc.gpsimd.memset(ones_x[:, :], 1.0 / XHD).then_inc(ones_set, 1)
            nc.gpsimd.memset(eps[:, :], EPS).then_inc(ones_set, 1)
            nc.gpsimd.memset(cv[:, :, 0:1], 0.0).then_inc(cv_zeroed, 1)
            nc.gpsimd.memset(cv[:, :, T + 1:T + 2], 0.0).then_inc(cv_zeroed, 1)
            xkv = io["w_xkv"][0]
            pool.dma_start(pool_w[:, :, :], io["pool_w"][0].rearrange("g c n -> c g n")).then_inc(s_poolw, 16)
            pool.dma_start(kv_w[:, :, :], wblock(xkv[:, 0:P])).then_inc(kvw_in, 16)
            with pool.Fori(1, N_EXPERTS) as e:
                pool.wait_ge(kvw_used, e)
                pool.dma_start(kv_w[:, :, :], xkv[:, bass.ds(e * P, P)].rearrange("(k p) n -> p k n", p=P)) \
                    .then_inc(kvw_in, 16)
            pool.wait_ge(scat_free, N_EXPERTS + 1)
            nc.gpsimd.memset(u_pad[:, :, 0:PAD], 0.0).then_inc(u_zeroed, 1)
            pool.wait_ge(u_zeroed, 1)
            pool.wait_ge(u_ready, 2)
            n = 0
            src, dst = u_pad, win_a
            for g in range(PG):
                w = 1 << g
                lo = 2 * w - 1
                nc.gpsimd.tensor_tensor(dst[:, g:PG, lo:UP], src[:, g:PG, lo:UP], src[:, g:PG, lo - w:UP - w],
                                        ALU.add).then_inc(poolc, 1)
                n += 1
                pool.wait_ge(poolc, n)
                nc.gpsimd.tensor_scalar(pooled[:, g, :], dst[:, g, PAD:UP], 1.0 / POOL_WINDOWS[g], None,
                                        ALU.mult).then_inc(poolc, 1)
                n += 1
                pool.wait_ge(poolc, n)
                inv = table("invcnt").rearrange("p (g t) -> p g t", g=PG)
                nc.gpsimd.tensor_tensor(pooled[:, g, 0:PAD], dst[:, g, PAD:2 * PAD], inv[:, g, :],
                                        ALU.mult).then_inc(poolc, 1)
                n += 1
                pool.wait_ge(poolc, n)
                nc.gpsimd.tensor_tensor(pooled[:, g, :], pooled[:, g, :], u_pad[:, g, PAD:UP],
                                        ALU.subtract).then_inc(pooled_ready, 1)
                src = dst
                dst = win_b if dst is win_a else win_a

        @block.tensor
        def _(pe):
            mm = nc.tensor.matmul

            def transpose_rows(rows, first):
                for f in range(4):
                    n = first + f
                    fill_free(pe, n)
                    for c in range(2):
                        for i in range(TT):
                            k = 2 * f + c
                            last = nc.tensor.transpose(acc[n % 4][:, c * T + i * P:c * T + (i + 1) * P],
                                                       rows[:, i, k * P:(k + 1) * P], ident)
                    last.then_inc(acc_done[n % 4], 1)

            def norm_mean(n_norm):
                if n_norm:
                    pe.wait_ge(mean_free, n_norm)
                for f in range(4):
                    pe.wait_ge(sq_ready, 4 * n_norm + f + 1)
                    for c in range(2):
                        last = mm(misc[0][:, 0:T], ones_d[:, :], sq[:, f % 2, c * T:(c + 1) * T],
                                  start=(f == 0 and c == 0), stop=(f == 3 and c == 1))
                    last.then_inc(sq_used, 1)

            def rows_product(out, w, stationary):
                for k in range(KC):
                    for j in range(4):
                        last = mm(out[CAP * j:CAP * (j + 1), 0:256], stationary(k), w[:, k, 256 * j:256 * (j + 1)],
                                  start=(k == 0), stop=(k == KC - 1))
                return last

            def ada_block(name, j):
                block_wait(pe, name)
                if j >= 2:
                    pe.wait_ge(ada_rows_ready, j - 1)
                rows_product(misc[1 + 2 * (j % 2)], block_slot(name),
                             lambda k: silu_c[:, k:k + 1].to_broadcast([P, CAP])).then_inc(ada_done, 1)

            def ada_columns(j):
                pe.wait_ge(ada_rows_ready, j + 1)
                if j:
                    pe.wait_ge(ada_read, j)
                for c in range(2):
                    last = nc.tensor.transpose(misc[2][:, c * P:(c + 1) * P], ada_rows[:, j % 2, c * P:(c + 1) * P], ident)
                last.then_inc(ada_t_done, 1)

            def dense_fill(slot_ap, src, n, cols):
                fill_free(pe, n)
                for ci, c in enumerate(cols):
                    for k in range(KC):
                        last = mm(acc[n % 4][:, ci * T:(ci + 1) * T], slot_ap[:, k, c * P:(c + 1) * P], src[:, k, :],
                                  start=(k == 0), stop=(k == KC - 1))
                last.then_inc(acc_done[n % 4], 1)
    
            def dense(name, src, first, order=range(4)):
                block_wait(pe, name)
                for j, f in enumerate(order):
                    dense_fill(block_slot(name), src, first + j, (2 * f, 2 * f + 1))

            pe.wait_ge(s_tab, 16)
            pe.wait_ge(s_x, 16)
            transpose_rows(x_rows, FILL["x_t"])
            pe.wait_ge(ones_set, 3)
            norm_mean(N1)
            pe.wait_ge(silu_c_ready, 1)
            ada_block("shift1", 0)
            ada_block("scale1", 1)
            ada_columns(0)
            ada_columns(1)
            pe.wait_ge(s_mem, 16)
            transpose_rows(mem_rows, FILL["mem_t"])
            pe.wait_ge(h_ready[N1], KC)
            dense("sc_b", h, FILL["conv_b"])
            norm_mean(NMEM)
            dense("sc_c", h, FILL["conv_c"])
            dense("sc_v", h, FILL["conv_v"])
            ada_block("gate1", 2)
            pe.wait_ge(conv_ready, KC)
            ada_columns(2)
            dense("sc_out", conv, FILL["conv_out"])
            ada_block("shift2", 3)
            ada_block("scale2", 4)
            norm_mean(N2)
            ada_columns(3)
            ada_columns(4)
            ada_block("gate2", 5)
            ada_columns(5)
            pe.wait_ge(h_ready[N2], KC)
            pe.wait_ge(ada_read, 6)
            for i in range(TT):
                for k in range(KC):
                    last = mm(misc[3][:, i * N_EXPERTS:(i + 1) * N_EXPERTS], h[:, k, i * P:(i + 1) * P],
                              router[:, k, :], start=(k == 0), stop=(k == KC - 1))
            last.then_inc(logits_done, 1)
            for f in range(4):
                n = FILL["h2_rows"] + f
                fill_free(pe, n)
                i = f // 2
                for c in range(4):
                    k = 4 * (f % 2) + c
                    last = nc.tensor.transpose(acc[n % 4][:, c * P:(c + 1) * P], h[:, k, i * P:(i + 1) * P], ident)
                last.then_inc(acc_done[n % 4], 1)
            pe.wait_ge(aff_ready, 1)
            for i in range(TT):
                last = nc.tensor.transpose(misc[2][0:N_EXPERTS, i * P:(i + 1) * P], aff[:, i, :], ident)
            last.then_inc(afft_done, 1)
            pe.wait_ge(slot_t_ready, 1)
            for i in range(TT):
                last = nc.tensor.transpose(misc[3][:, i * N_EXPERTS:(i + 1) * N_EXPERTS],
                                           slot_t[:, i * P:(i + 1) * P], ident[0:N_EXPERTS, 0:N_EXPERTS])
            last.then_inc(slot_done, 1)
            pe.wait_ge(sel_ready, 1)
            pe.wait_ge(rows_ready, 4)
            for k in range(KC):
                n = FILL["gather"] + k
                fill_free(pe, n)
                for i in range(TT):
                    last = mm(acc[n % 4][:, :], h2_rows[:, i, k * P:(k + 1) * P],
                              sel[:, i, :, :].rearrange("p e s -> p (e s)"), start=(i == 0), stop=(i == TT - 1))
                last.then_inc(acc_done[n % 4], 1)
            for p in range(N_EXPERTS // 2):
                pe.wait_ge(selg_ready, p + 1)
                if p >= 2:
                    pe.wait_ge(scat_ready, p - 1)
                for j in range(2):
                    for i in range(TT):
                        last = nc.tensor.transpose(
                            misc[2 + p % 2][:, j * T + i * P:j * T + (i + 1) * P],
                            sel_g[:, p % 2, i, j, :, :].rearrange("p j s -> p (j s)"), ident)
                last.then_inc(scat_t_done, 1)
            pe.wait_ge(scat_ready, N_EXPERTS // 2)
            nc.tensor.nop().then_inc(scat_free, 1)
            pe.wait_ge(y_zeroed, 4)

            def expert(e, values):
                gate_w, up_w, down_w = (ring[(MOE0 + j) % RING] for j in range(3))
                uses = [(MOE0 + j) // RING + 1 for j in range(3)]

                pe.wait_ge(xse_ready, e + 1)
                pe.wait_ge(landed[MOE0 % RING], e * 16 + 16 * uses[0])
                rows_product(misc[0], gate_w, lambda k: xs_e[:, k, :]).then_inc(gate_done, 1)
                pe.wait_ge(landed[(MOE0 + 1) % RING], e * 16 + 16 * uses[1])
                rows_product(misc[1], up_w, lambda k: xs_e[:, k, :]).then_inc(up_done, 1)
                pe.wait_ge(kvw_in, e * 16 + 16)
                pe.wait_ge(silu_ready, e + 1)
                if not values:
                    for k in range(KC):
                        last = mm(misc[0][:, 0:T], kv_w[:, k, :], mem_n[:, k, :], start=(k == 0), stop=(k == KC - 1))
                else:
                    for i in range(TT):
                        for k in range(KC):
                            last = mm(misc[0][:, i * P:(i + 1) * P], mem_n[:, k, i * P:(i + 1) * P], kv_w[:, k, :],
                                      start=(k == 0), stop=(k == KC - 1))
                last.then_inc(kvw_used, 1)
                pe.wait_ge(hid_ready, e + 1)
                for c in range(2):
                    last = nc.tensor.transpose(misc[2][:, c * P:(c + 1) * P], hid[:, c * P:(c + 1) * P], ident)
                last.then_inc(hidt_done, 1)
                pe.wait_ge(hidt_ready, e + 1)
                pe.wait_ge(landed[(MOE0 + 2) % RING], e * 16 + 16 * uses[2])
                rows_product(misc[3], down_w, lambda k: hid_t[:, k % 2, k // 2, :]).then_inc(down_done, 1)
                pe.wait_ge(ysr_ready, e + 1)
                pe.wait_ge(scate_ready, e + 1)
                for c in range(2):
                    for j in range(4):
                        g = slice(CAP * j, CAP * (j + 1))
                        last = mm(acc[j][:, c * T:(c + 1) * T], ys_rows[g, c * P:(c + 1) * P], scat_e[g, :],
                                  start=False, stop=False, skip_group_check=True)
                last.then_inc(scat_free, 1)
                pe.wait_ge(kv_read, e + 1)

            pe.wait_ge(h_ready[NMEM], KC)
            with pe.Fori(0, N_EXPERTS // 2) as e:
                expert(e, False)
            for x in range(XHEADS):
                pe.wait_ge(ksq_ready, x + 1)
                if x:
                    pe.wait_ge(kmean_read, x)
                for c in range(2):
                    last = mm(misc[0][:, 0:T], ones_x[:, :], sq[:, x % 2, c * T:(c + 1) * T], start=(c == 0), stop=(c == 1))
                last.then_inc(kmean_done, 1)
            pe.wait_ge(kmean_read, XHEADS)
            with pe.Fori(N_EXPERTS // 2, N_EXPERTS) as e:
                expert(e, True)

            norm_mean(NMIX)
            pe.wait_ge(h_ready[NMIX], KC)
            rot, headmean = table("rot"), table("headmean")

            def qk_mean_rot(j):
                pe.wait_ge(qkg_ready, j + 1)
                if j:
                    pe.wait_ge(qk_read, j)
                    pe.wait_ge(qk_std, j)
                mm(misc[0][:, :], headmean, sq[:, j % 2, :], start=True, stop=True)
                mm(misc[1][:, :], rot, qk_g, start=True, stop=True).then_inc(qk_prep, 1)

            block_wait(pe, "in_uq")
            dense_fill(block_slot("in_uq"), h, FILL["q"], (4, 5))
            dense_fill(block_slot("in_uq"), h, FILL["q"] + 1, (6, 7))
            qk_mean_rot(0)
            block_wait(pe, "in_kv")
            dense_fill(block_slot("in_kv"), h, FILL["k"], (0, 1))
            qk_mean_rot(1)
            dense_fill(block_slot("in_kv"), h, FILL["k"] + 1, (2, 3))
            qk_mean_rot(2)
            for i in range(TT):
                n = FILL["v"] + i
                fill_free(pe, n)
                for k in range(KC):
                    last = mm(acc[n % 4][:, :], h[:, k, i * P:(i + 1) * P], block_slot("in_kv")[:, k, 512:1024],
                              start=(k == 0), stop=(k == KC - 1))
                last.then_inc(acc_done[n % 4], 1)
                if i == 0:
                    qk_mean_rot(3)
            dense_fill(block_slot("in_uq"), h, FILL["u"], (0, 1))
            dense_fill(block_slot("in_uq"), h, FILL["u"] + 1, (2, 3))

            def scores(a):
                c, lo = a // 2, HD * (a % 2)
                if a == 0:
                    pe.wait_ge(qk_ready, 4)
                if a >= 2:
                    pe.wait_ge(masked, a - 1)
                b = misc[2 + a % 2]
                mm(b[:, 0:P], q_rot[lo:lo + HD, c, 0:P], k_rot[lo:lo + HD, c, 0:P], start=True, stop=True)
                mm(b[:, P:3 * P], q_rot[lo:lo + HD, c, P:T], k_rot[lo:lo + HD, c, :],
                   start=True, stop=True).then_inc(score_done, 1)

            def weigh(a):
                lo = HD * (a % 2)
                pe.wait_ge(prob_ready, a + 1)
                if a:
                    pe.wait_ge(probt_ready, a)
                for b in range(3):
                    last = nc.tensor.transpose(misc[0][:, b * P:(b + 1) * P], prob[:, a % 2, b * P:(b + 1) * P], ident)
                last.then_inc(probt_done, 1)
                pe.wait_ge(probt_ready, a + 1)
                if a >= 1:
                    pe.wait_ge(o_ready, a)
                o = misc[1][lo:lo + HD, 0:T]
                mm(o, v_rows[:, 0, a * HD:(a + 1) * HD], prob_t[:, a % 2, 0:T], start=True, stop=False)
                mm(misc[1][lo:lo + HD, P:T], v_rows[:, 1, a * HD:(a + 1) * HD], prob_t[:, a % 2, T:T + P],
                   start=False, stop=True).then_inc(pv_done, 1)

            scores(0)
            pe.wait_ge(v_ready, TT)
            pe.wait_ge(s_poolw, 16)
            for a in range(HEADS):
                if a + 1 < HEADS:
                    scores(a + 1)
                weigh(a)
                if a in (3, 5):
                    f = (a - 3) // 2
                    n = FILL["pool"] + f
                    fill_free(pe, n)
                    pe.wait_ge(pooled_ready, 2 * f + 2)
                    for j in range(2):
                        g = 2 * f + j
                        last = mm(acc[n % 4][:, j * T:(j + 1) * T], pool_w[:, g, :], pooled[:, g, :],
                                  start=True, stop=True)
                    last.then_inc(acc_done[n % 4], 1)
            pe.wait_ge(pool_ready, 2)
            pe.wait_ge(o_ready, HEADS)
            dense("mix_out", mix, FILL["mix_out"])

            norm_mean(NXATT)
            pe.wait_ge(h_ready[NXATT], KC)

            def x_mean(x):
                pe.wait_ge(xsq_ready, x + 1)
                if x:
                    pe.wait_ge(xstd_ready, x)
                for c in range(2):
                    last = mm(misc[0][:, 0:T], ones_x[:, :], sq[:, x % 2, c * T:(c + 1) * T], start=(c == 0), stop=(c == 1))
                last.then_inc(xmean_done, 1)

            block_wait(pe, "xq")
            for x in range(XHEADS):
                dense_fill(block_slot("xq"), h, FILL["xq"] + x, (2 * x, 2 * x + 1))
                if x:
                    x_mean(x - 1)
            x_mean(XHEADS - 1)

            def x_scores(x):
                pe.wait_ge(xq_ready, x + 1)
                if x >= 2:
                    pe.wait_ge(xexp, x - 1)
                b = misc[2 + x % 2]
                for i in range(TT):
                    for c in range(2):
                        last = mm(b[:, i * T:(i + 1) * T], q_x[:, 2 * x + c, i * P:(i + 1) * P], k_mem[:, 2 * x + c, :],
                                  start=(c == 0), stop=(c == 1))
                last.then_inc(xscore_done, 1)

            def x_weigh(x):
                pe.wait_ge(xprob_ready, x + 1)
                if x:
                    pe.wait_ge(xprobt_ready, x)
                for j in range(TT):
                    for i in range(TT):
                        last = nc.tensor.transpose(misc[0][:, j * T + i * P:j * T + (i + 1) * P],
                                                   prob[:, x % 2, i * T + j * P:i * T + (j + 1) * P], ident)
                last.then_inc(xprobt_done, 1)
                pe.wait_ge(xprobt_ready, x + 1)
                if x:
                    pe.wait_ge(xo_ready, x)
                for c in range(2):
                    for j in range(TT):
                        at = x * XHD + c * P
                        last = mm(misc[1][:, c * T:(c + 1) * T], v_mem[:, j, at:at + P], prob_t[:, x % 2, j * T:(j + 1) * T],
                                  start=(j == 0), stop=(j == TT - 1))
                last.then_inc(xpv_done, 1)

            pe.wait_ge(xq_ready, XHEADS)
            x_scores(0)
            for x in range(XHEADS):
                if x + 1 < XHEADS:
                    x_scores(x + 1)
                x_weigh(x)
            pe.wait_ge(xo_ready, XHEADS)
            dense("xo", o_x, FILL["xo"])

            norm_mean(NFFN)
            pe.wait_ge(ffn_zeroed, 4)

            def split_mm(out, hi, lo, x_hi, x_lo, start, stop):
                mm(out, hi, x_hi, start=start, stop=False, skip_group_check=True)
                mm(out, hi, x_lo, start=False, stop=False, skip_group_check=True)
                return mm(out, lo, x_hi, start=False, stop=stop, skip_group_check=True)

            def ffn_up_step(s, par):
                first = isinstance(s, int) and s == 0
                if not isinstance(s, int) or s >= 2:
                    pe.wait_ge(conv2_done, s - 1)
                for g in range(2):
                    pe.wait_ge(w_lo[g], s + 1)
                    for k in range(KC):
                        if first and g == 0:
                            pe.wait_ge(x_lo_ready, k + 1)
                        n = slice(k * P, (k + 1) * P)
                        last = split_mm(misc[par][:, g * T:(g + 1) * T], ffn_hi[par][:, g, n], ffn_lo[par][:, g, n],
                                        x_hi[:, k, :], x_lo[:, k, :], k == 0, k == KC - 1)
                last.then_inc(up2_done, 1)

            def ffn_down_step(s, par):
                pe.wait_ge(w_lo[2], s + 1)
                pe.wait_ge(act_ready, s + 1)
                for c in range(KC):
                    n = slice(c * P, (c + 1) * P)
                    last = split_mm(acc[c // 2][:, (c % 2) * T:(c % 2 + 1) * T], ffn_hi[par][:, 2, n],
                                    ffn_lo[par][:, 2, n], act_hi[:, par, :], act_lo[:, par, :], False, False)
                last.then_inc(down2_done, 1)

            ffn_up_step(0, 0)
            ffn_up_step(1, 1)
            ffn_down_step(0, 0)
            with pe.Fori(1, FC // 2) as i:
                for par in range(2):
                    ffn_up_step(i * 2 + par, par)
                    ffn_down_step(i * 2 + (par - 1), 1 - par)
            ffn_down_step(FC - 1, 1)

            for f in range(4):
                n = FILL["rows"] + f
                pe.wait_ge(lat_final, max(f, n % 4) + 1)
                fill_free(pe, n)
                for i in range(TT):
                    for c in range(2):
                        last = nc.tensor.transpose(acc[n % 4][:, i * T + c * P:i * T + (c + 1) * P],
                                                   lat[:, 2 * f + c, i * P:(i + 1) * P], ident)
                last.then_inc(acc_done[n % 4], 1)

        @block.scalar
        def _(act):
            A = nc.scalar.activation
            act.dma_start(tab[:, :], io["tables"]).then_inc(s_tab, 16)

            def squares(n_norm, src):
                for f in range(4):
                    act.wait_ge(lat_ready[n_norm], f + 1)
                    m = 4 * n_norm + f
                    if m >= 2:
                        act.wait_ge(sq_used, m - 1)
                    A(sq[:, f % 2, :], src[:, 2 * f:2 * f + 2, :], ACT.Square).then_inc(sq_ready, 1)

            def deviation(n_norm):
                act.wait_ge(sq_used, 4 * (n_norm + 1))
                A(std[:, n_norm % 2, :], misc[0][:, 0:T], ACT.Sqrt, bias=eps[:, :]).then_inc(mean_free, 1)

            act.wait_ge(ones_set, 3)
            act.wait_ge(s_vec, 16)
            A(silu_c[:, :], vcol("c"), ACT.Silu).then_inc(silu_c_ready, 1)
            squares(N1, lat)
            deviation(N1)
            def ada_copy(j):
                act.wait_ge(ada_done, j + 1)
                if j >= 2:
                    act.wait_ge(ada_t_done, j - 1)
                A(ada_rows[:, j % 2, :], misc[1 + 2 * (j % 2)][:, 0:256], ACT.Copy).then_inc(ada_rows_ready, 1)

            ada_copy(0)
            ada_copy(1)
            for k in range(KC):
                act.wait_ge(h_scaled, k + 1)
                A(h[:, k, :], h[:, k, :], ACT.Identity, bias=mod[:, k:k + 1]).then_inc(h_ready[N1], 1)
            for f in range(4):
                n = FILL["mem_t"] + f
                fill_done(act, n)
                A(mem_n[:, 2 * f:2 * f + 2, :], acc[n % 4][:, :], ACT.Copy).then_inc(acc_free[n % 4], 1)
            for name, dst in (("conv_b", gate_b), ("conv_c", gate_c)):
                for f in range(4):
                    n = FILL[name] + f
                    fill_done(act, n)
                    A(dst[:, 2 * f:2 * f + 2, :], acc[n % 4][:, :], ACT.Copy).then_inc(acc_free[n % 4], 1)
                    if name == "conv_b":
                        act.wait_ge(acc_free[(FILL["mem_t"] + f) % 4], (FILL["mem_t"] + f) // 4 + 1)
                        if f >= 2:
                            act.wait_ge(sq_used, 4 * NMEM + f - 1)
                        A(sq[:, f % 2, :], mem_n[:, 2 * f:2 * f + 2, :], ACT.Square).then_inc(sq_ready, 1)
                if name == "conv_b":
                    deviation(NMEM)
            ada_copy(2)
            squares(N2, lat)
            ada_copy(3)
            ada_copy(4)
            deviation(N2)
            for k in range(KC):
                act.wait_ge(h_scaled, KC + k + 1)
                A(h[:, k, :], h[:, k, :], ACT.Identity, bias=mod[:, 3 * KC + k:3 * KC + k + 1]).then_inc(h_ready[N2], 1)
            ada_copy(5)
            act.wait_ge(negmax_r, 1)
            for i in range(TT):
                A(aff_e[:, i, :], misc[3][:, i * N_EXPERTS:(i + 1) * N_EXPERTS], ACT.Exp, bias=stat[:, i:i + 1],
                  accum_out=stat[:, 2 + i:3 + i]).then_inc(exp_done, 1)
            for f in range(4):
                n = FILL["h2_rows"] + f
                fill_done(act, n)
                A(h2_rows[:, f // 2, (f % 2) * 512:(f % 2 + 1) * 512], acc[n % 4][:, :], ACT.Copy) \
                    .then_inc(acc_free[n % 4], 1)
            for f in range(4):
                n = FILL["h2_rows"] + f
                act.wait_ge(acc_free[n % 4], n // 4 + 1)
            nc.scalar.nop().then_inc(rows_ready, 4)
            for k in range(0, KC, 2):
                n = FILL["gather"] + k
                fill_done(act, n)
                A(xs[:, k, :], acc[n % 4][:, :], ACT.Copy).then_inc(acc_free[n % 4], 1)
            for p in range(N_EXPERTS // 2):
                act.wait_ge(scat_t_done, p + 1)
                A(scatter[:, 2 * p:2 * p + 2, :], misc[2 + p % 2][:, :], ACT.Copy).then_inc(scat_ready, 1)

            def expert(e):
                act.wait_ge(gate_done, e + 1)
                A(silu_g, misc[0][:, 0:256], ACT.Silu).then_inc(silu_ready, 1)
                act.wait_ge(hidt_done, e + 1)
                A(hid_t, misc[2][:, 0:256].rearrange("p (c j s) -> p c j s", c=2, j=4), ACT.Copy).then_inc(hidt_ready, 1)
                act.wait_ge(down_done, e + 1)
                A(ys_rows, misc[3][:, 0:256], ACT.Copy).then_inc(ysr_ready, 1)

            with act.Fori(0, N_EXPERTS // 2) as e:
                expert(e)
            for x in range(XHEADS):
                act.wait_ge(kv_read, 2 * x + 2)
                if x >= 2:
                    act.wait_ge(kmean_done, x - 1)
                A(sq[:, x % 2, :], k_mem[:, 2 * x:2 * x + 2, :], ACT.Square).then_inc(ksq_ready, 1)
                act.wait_ge(kmean_done, x + 1)
                if x >= 2:
                    act.wait_ge(k_ready, 2 * (x - 1))
                A(std[:, x % 2, :], misc[0][:, 0:T], ACT.Sqrt, bias=eps[:, :]).then_inc(kmean_read, 1)
            with act.Fori(N_EXPERTS // 2, N_EXPERTS) as e:
                expert(e)

            squares(NMIX, lat)
            deviation(NMIX)
            for j in range(4):
                n = (FILL["q"], FILL["k"])[j // 2] + j % 2
                fill_done(act, n)
                if j:
                    act.wait_ge(qk_ready, j)
                else:
                    act.wait_ge(sq_used, 4 * (NMIX + 1))
                A(sq[:, j % 2, :], acc[n % 4][:, :], ACT.Square)
                A(qk_g, acc[n % 4][:, :], ACT.Copy, scale=vcol(("q_norm_g", "k_norm_g")[j // 2])) \
                    .then_inc(acc_free[n % 4], 1)
                act.wait_ge(acc_free[n % 4], n // 4 + 1)
                nc.scalar.nop().then_inc(qkg_ready, 1)
                act.wait_ge(qk_prep, j + 1)
                A(region_s[:, 0:512], misc[0][:, :], ACT.Sqrt, bias=eps[:, :]).then_inc(qk_std, 1)
            for i in range(TT):
                n = FILL["v"] + i
                fill_done(act, n)
                A(v_rows[:, i, :], acc[n % 4][:, :], ACT.Copy).then_inc(acc_free[n % 4], 1)
                act.wait_ge(acc_free[n % 4], n // 4 + 1)
                nc.scalar.nop().then_inc(v_ready, 1)
            act.wait_ge(scat_free, N_EXPERTS + 1)
            for f in range(2):
                n = FILL["u"] + f
                fill_done(act, n)
                A(u_pad[:, 2 * f:2 * f + 2, PAD:UP], acc[n % 4][:, :].rearrange("p (g t) -> p g t", g=2), ACT.Copy) \
                    .then_inc(acc_free[n % 4], 1)
                act.wait_ge(acc_free[n % 4], n // 4 + 1)
                nc.scalar.nop().then_inc(u_ready, 1)
            for a in range(HEADS):
                act.wait_ge(negmax, a + 1)
                at = 4 * (a % 2)
                for i, (lo, hi) in enumerate(((0, P), (P, 3 * P))):
                    A(prob[:, a % 2, lo:hi], prob[:, a % 2, lo:hi], ACT.Exp, scale=HD ** -0.5,
                      bias=stat[:, at + i:at + i + 1], accum_out=stat[:, at + 2 + i:at + 3 + i]).then_inc(prob_exp, 1)
                act.wait_ge(pv_done, a + 1)
                lo = HD * (a % 2)
                A(mix[lo:lo + HD, PG + a // 2, :], misc[1][lo:lo + HD, 0:T], ACT.Copy).then_inc(o_ready, 1)
                if a in (4, 6):
                    f = (a - 4) // 2
                    n = FILL["pool"] + f
                    fill_done(act, n)
                    for j in range(2):
                        g = 2 * f + j
                        last = A(mix[:, g, :], acc[n % 4][:, j * T:(j + 1) * T], ACT.Copy, scale=vcol("pool_scale", g, 1))
                    last.then_inc(acc_free[n % 4], 1)
                    act.wait_ge(acc_free[n % 4], n // 4 + 1)
                    nc.scalar.nop().then_inc(pool_ready, 1)
            squares(NXATT, lat)
            deviation(NXATT)
            for x in range(XHEADS):
                n = FILL["xq"] + x
                fill_done(act, n)
                if x >= 2:
                    act.wait_ge(xmean_done, x - 1)
                else:
                    act.wait_ge(sq_used, 4 * (NXATT + 1))
                A(sq[:, x % 2, :], acc[n % 4][:, :], ACT.Square).then_inc(xsq_ready, 1)
                act.wait_ge(xmean_done, x + 1)
                if x >= 2:
                    act.wait_ge(xq_ready, x - 1)
                A(std[:, x % 2, :], misc[0][:, 0:T], ACT.Sqrt, bias=eps[:, :]).then_inc(xstd_ready, 1)
            for x in range(XHEADS):
                act.wait_ge(xnegmax, x + 1)
                at = 4 * (x % 2)
                for i in range(TT):
                    A(prob[:, x % 2, i * T:(i + 1) * T], misc[2 + x % 2][:, i * T:(i + 1) * T], ACT.Exp, scale=XHD ** -0.5,
                      bias=stat[:, at + i:at + i + 1], accum_out=stat[:, at + 2 + i:at + 3 + i])
                act.drain().then_inc(xexp, 1)
                act.wait_ge(xpv_done, x + 1)
                A(o_x[:, 2 * x:2 * x + 2, :], misc[1][:, :], ACT.Copy).then_inc(xo_ready, 1)

            def ffn_high(par, part, loads):
                if part < 2:
                    act.wait_ge(ffn_up_in[par], loads * 32)
                else:
                    act.wait_ge(ffn_down_in[par], loads * 16)
                A(ffn_hi[par][:, part, :], ffn_raw(par, part), ACT.Copy).then_inc(w_hi[part], 1)

            block_done(act, BLOCK["xq"])
            for part in range(3):
                ffn_high(0, part, 1)
            squares(NFFN, lat)
            deviation(NFFN)
            for k in range(KC):
                act.wait_ge(h_ready[NFFN], k + 1)
                A(x_hi[:, k, :], h[:, k, :], ACT.Copy).then_inc(x_hi_ready, 1)
            ffn_high(1, 0, 1)
            ffn_high(1, 1, 1)

            def ffn_step(s, par, loads, last=0):
                act.wait_ge(up2_done, s + 1)
                for g in range(2):
                    w = vec[:, bass.ds(s + (VEC["conv_w"][0] + 2 * 2 * FC + g * FC), 1)]
                    b = vec[:, bass.ds(s + (VEC["conv_b"][0] + g * FC), 1)]
                    z = A(up_z[:, par, g, :], misc[par][:, g * T:(g + 1) * T], ACT.Identity, scale=w, bias=b)
                z.then_inc(z_ready, 1)
                if last < 1:
                    ffn_high(par, 0, loads + 1)
                act.wait_ge(conv2_done, s + 1)
                A(up_s[:, par, :], up_z[:, par, 0, :], ACT.Silu).then_inc(silu2_ready, 1)
                if last < 1:
                    ffn_high(par, 1, loads + 1)
                if last < 2:
                    if not isinstance(s, int) or s:
                        act.wait_ge(down2_done, s)
                    ffn_high(1 - par, 2, loads + par)

            ffn_step(0, 0, 1)
            ffn_step(1, 1, 1)
            with act.Fori(1, FC // 2 - 1) as i:
                ffn_step(i * 2, 0, i + 1)
                ffn_step(i * 2 + 1, 1, i + 1)
            ffn_step(FC - 2, 0, FC // 2, last=1)
            ffn_step(FC - 1, 1, FC // 2, last=2)

        @block.vector
        def _(ve):
            V = nc.vector
            n_chain = [0]

            def then(ins):
                ins.then_inc(dve, 1)
                n_chain[0] += 1
                ve.wait_ge(dve, n_chain[0])

            def norm(n_norm, src, dst, gain, scaled, base=0):
                ve.wait_ge(mean_free, n_norm + 1)
                then(V.reciprocal(rstd[:, :], std[:, n_norm % 2, :]))
                for k in range(KC):
                    V.scalar_tensor_tensor(out=dst[:, k, :], in0=src[:, k, :], scalar=gain[:, k:k + 1], in1=rstd[:, :],
                                           op0=ALU.mult, op1=ALU.mult).then_inc(scaled, 1)

            def ada_read_block(j):
                ve.wait_ge(ada_t_done, j + 1)
                first_copy = misc[2][:, 0:256].rearrange("p (c j s) -> p j c s", c=2, j=4)[:, :, :, 0]
                V.tensor_tensor(mod[:, j * KC:(j + 1) * KC].rearrange("p (j c) -> p j c", c=2), first_copy,
                                vcol("ada_b", j * KC, KC).rearrange("p (j c) -> p j c", c=2), ALU.add) \
                    .then_inc(ada_read, 1)
                ve.wait_ge(ada_read, j + 1)

            ve.wait_ge(s_vec, 16)
            for f in range(4):
                n = FILL["x_t"] + f
                fill_done(ve, n)
                V.tensor_copy(lat[:, 2 * f:2 * f + 2, :], acc[n % 4][:, :].rearrange("p (c t) -> p c t", c=2)) \
                    .then_inc(acc_free[n % 4], 1)
                ve.wait_ge(acc_free[n % 4], n // 4 + 1)
                V.engine_nop().then_inc(lat_ready[N1], 1)
            ve.wait_ge(mean_free, 1)
            then(V.reciprocal(rstd[:, :], std[:, 0, :]))
            ada_read_block(0)
            ada_read_block(1)
            then(V.scalar_tensor_tensor(out=gain1[:, :], in0=mod[:, KC:2 * KC], scalar=1.0, in1=vcol("norm_g", 0, KC),
                                        op0=ALU.add, op1=ALU.mult))
            for k in range(KC):
                V.scalar_tensor_tensor(out=h[:, k, :], in0=lat[:, k, :], scalar=gain1[:, k:k + 1], in1=rstd[:, :],
                                       op0=ALU.mult, op1=ALU.mult).then_inc(h_scaled, 1)
            ve.wait_ge(h_scaled, KC)
            norm(NMEM, mem_n, mem_n, vcol("norm_mem_g"), h_ready[NMEM])
            ve.wait_ge(cv_zeroed, 2)
            cw = vcol("sc_conv").rearrange("p (w k) -> p w k", w=3)
            ve.wait_ge(s_mem, 16)
            for f in range(4):
                n = FILL["conv_v"] + f
                pair = slice(2 * f, 2 * f + 2)
                ve.wait_ge(acc_free[(FILL["conv_c"] + f) % 4], (FILL["conv_c"] + f) // 4 + 1)
                fill_done(ve, n)
                V.tensor_tensor(cv[:, pair, 1:T + 1], acc[n % 4][:, :].rearrange("p (c t) -> p c t", c=2),
                                gate_c[:, pair, :], ALU.mult).then_inc(acc_free[n % 4], 1)
                ve.wait_ge(acc_free[n % 4], n // 4 + 1)
                for k in range(2 * f, 2 * f + 2):
                    ins = V.tensor_scalar(conv[:, k, :], cv[:, k, 0:T], cw[:, 0, k:k + 1], None, ALU.mult)
                    if k % 2:
                        then(ins)
                for w in (1, 2):
                    for k in range(2 * f, 2 * f + 2):
                        ins = V.scalar_tensor_tensor(out=conv[:, k, :], in0=cv[:, k, w:w + T], scalar=cw[:, w, k:k + 1],
                                                     in1=conv[:, k, :], op0=ALU.mult, op1=ALU.add)
                        if k % 2:
                            then(ins)
                V.tensor_tensor(conv[:, pair, :], conv[:, pair, :], gate_b[:, pair, :], ALU.mult).then_inc(conv_ready, 2)
            ada_read_block(2)
            for f in range(4):
                n = FILL["conv_out"] + f
                fill_done(ve, n)
                for c in range(2):
                    k = 2 * f + c
                    last = V.scalar_tensor_tensor(out=lat[:, k, :], in0=acc[n % 4][:, c * T:(c + 1) * T],
                                                  scalar=mod[:, 2 * KC + k:2 * KC + k + 1], in1=lat[:, k, :],
                                                  op0=ALU.mult, op1=ALU.add)
                last.then_inc(acc_free[n % 4], 1)
                ve.wait_ge(acc_free[n % 4], n // 4 + 1)
                V.engine_nop().then_inc(lat_ready[N2], 1)
            ada_read_block(3)
            ada_read_block(4)
            then(V.scalar_tensor_tensor(out=gain2[:, :], in0=mod[:, 4 * KC:5 * KC], scalar=1.0, in1=vcol("norm_g", KC, KC),
                                        op0=ALU.add, op1=ALU.mult))
            norm(N2, lat, h, gain2, h_scaled)
            ada_read_block(5)
            ve.wait_ge(logits_done, 1)
            then(V.tensor_reduce(stat[:, 4:6], misc[3][:, 0:TT * N_EXPERTS].rearrange("p (i e) -> p i e", i=TT), AX, ALU.max))
            V.tensor_scalar(stat[:, 0:2], stat[:, 4:6], -1.0, None, ALU.mult).then_inc(negmax_r, 1)
            ve.wait_ge(exp_done, 2)
            then(V.reciprocal(stat[:, 6:8], stat[:, 2:4]))
            for i in range(TT):
                last = V.tensor_scalar(aff[:, i, :], aff_e[:, i, :], stat[:, 6 + i:7 + i], None, ALU.mult)
            last.then_inc(aff_ready, 1)
            V.memset(ones_r, 1.0)
            ve.wait_ge(afft_done, 1)
            then(V.tensor_copy(top_work[:, :], misc[2][0:N_EXPERTS, 0:T]))
            for r in range(CAP // 8):
                then(V.max(top8[:, :], top_work[:, :]))
                then(V.match_replace(top_work[:, :], top8[:, :], top_work[:, :], -1.0))
            then(V.tensor_scalar(chosen[:, :], top_work[:, :], 0.0, None, ALU.is_lt))
            then(V.tensor_tensor_scan(count[:, :], ones_r[:, :], chosen[:, :], 0.0, ALU.mult, ALU.add))
            then(V.tensor_tensor(slot_t[:, :], count[:, :], chosen[:, :], ALU.mult))
            V.tensor_scalar(slot_t[:, :], slot_t[:, :], -1.0, None, ALU.add).then_inc(slot_t_ready, 1)
            ve.wait_ge(slot_done, 1)
            then(V.tensor_copy(slot[:, :, :], misc[3][:, 0:TT * N_EXPERTS].rearrange("p (i e) -> p i e", i=TT)))
            iota = table("iota")[:, None, :].to_broadcast([P, N_EXPERTS, CAP])
            for i in range(TT):
                last = V.tensor_tensor(sel[:, i, :, :], iota, slot[:, i, :, None].to_broadcast([P, N_EXPERTS, CAP]),
                                       ALU.is_equal)
            last.then_inc(sel_ready, 1)
            ve.wait_ge(sel_ready, 1)

            def gate_pair(p):
                if p >= 2:
                    ve.wait_ge(scat_t_done, p - 1)
                for i in range(TT):
                    for j in range(2):
                        e = 2 * p + j
                        last = V.tensor_scalar(sel_g[:, p % 2, i, j, :, :],
                                               sel[:, i, e, None, :].to_broadcast([P, 4, CAP]),
                                               aff[:, i, e:e + 1], None, ALU.mult)
                last.then_inc(selg_ready, 1)

            gate_pair(0)
            gate_pair(1)
            for k in range(1, KC, 2):
                n = FILL["gather"] + k
                fill_done(ve, n)
                V.tensor_copy(xs[:, k, :], acc[n % 4][:, :]).then_inc(acc_free[n % 4], 1)
            for p in range(2, N_EXPERTS // 2):
                gate_pair(p)
            for b in range(4):
                n = FILL["gather"] + 4 + b
                ve.wait_ge(acc_free[n % 4], n // 4 + 1)
            for b in range(4):
                V.memset(acc[b][:, :], 0.0).then_inc(y_zeroed, 1)

            def expert(e, values):
                V.tensor_copy(xs_e[:, :, :], xs[:, :, bass.ds(e * CAP, CAP)]).then_inc(xse_ready, 1)
                ve.wait_ge(silu_ready, e + 1)
                ve.wait_ge(up_done, e + 1)
                V.tensor_tensor(hid, silu_g, misc[1][:, 0:256], ALU.mult).then_inc(hid_ready, 1)
                ve.wait_ge(kvw_used, e + 1)
                if not values:
                    V.tensor_copy(k_mem[:, bass.ds(e, 1), :], misc[0][:, None, 0:T]).then_inc(kv_read, 1)
                else:
                    V.tensor_copy(v_mem[:, :, bass.ds((e - N_EXPERTS // 2) * P, P)],
                                  misc[0][:, 0:T].rearrange("p (i n) -> p i n", i=TT)).then_inc(kv_read, 1)
                ve.wait_ge(scat_free, e + 1)
                V.tensor_copy(scat_e[:, None, :], scatter[:, bass.ds(e, 1), :]).then_inc(scate_ready, 1)

            with ve.Fori(0, N_EXPERTS // 2) as e:
                expert(e, False)
            for x in range(XHEADS):
                ve.wait_ge(kmean_read, x + 1)
                then(V.reciprocal(rstd[:, :], std[:, x % 2, :]))
                for c in range(2):
                    k = 2 * x + c
                    V.scalar_tensor_tensor(out=k_mem[:, k, :], in0=k_mem[:, k, :], scalar=vcol("xk_norm_g", c, 1),
                                           in1=rstd[:, :], op0=ALU.mult, op1=ALU.mult).then_inc(k_ready, 1)
                ve.wait_ge(k_ready, 2 * x + 2)
            with ve.Fori(N_EXPERTS // 2, N_EXPERTS) as e:
                expert(e, True)
            ve.wait_ge(scat_free, N_EXPERTS + 1)
            for k in range(KC):
                ins = V.scalar_tensor_tensor(out=lat[:, k, :], in0=acc[k // 2][:, (k % 2) * T:(k % 2 + 1) * T],
                                             scalar=mod[:, 5 * KC + k:5 * KC + k + 1], in1=lat[:, k, :],
                                             op0=ALU.mult, op1=ALU.add)
                if k % 2:
                    ins.then_inc(lat_ready[NMIX], 1)
            norm(NMIX, lat, h, vcol("norm_mix_g"), h_ready[NMIX])

            def two(ap):
                return ap[:, None, :].to_broadcast([P, 2, T])

            for j in range(4):
                dst = (q_rot, k_rot)[j // 2][:, 2 * (j % 2):2 * (j % 2) + 2, :]
                t3 = qk_t.rearrange("p (c t) -> p c t", c=2)
                ve.wait_ge(qkg_ready, j + 1)
                ve.wait_ge(qk_prep, j + 1)
                V.tensor_tensor(dst, misc[1][:, :].rearrange("p (c t) -> p c t", c=2), two(table("sin")), ALU.mult) \
                    .then_inc(qk_read, 1)
                then(V.tensor_tensor(t3, qk_g.rearrange("p (c t) -> p c t", c=2), two(table("cos")), ALU.mult))
                ve.wait_ge(qk_read, j + 1)
                V.tensor_tensor(dst, dst, t3, ALU.add)
                ve.wait_ge(qk_std, j + 1)
                then(V.reciprocal(region_s[:, 512:1024], region_s[:, 0:512]))
                V.tensor_tensor(dst, dst, region_s[:, 512:1024].rearrange("p (c t) -> p c t", c=2), ALU.mult) \
                    .then_inc(qk_ready, 1)
                ve.wait_ge(qk_ready, j + 1)
            for a in range(HEADS):
                s = prob[:, a % 2, 0:3 * P]
                at = 4 * (a % 2)
                ve.wait_ge(score_done, a + 1)
                if a >= 2:
                    ve.wait_ge(probt_done, a - 1)
                V.tensor_tensor(s, misc[2 + a % 2][:, 0:3 * P], table("causal"), ALU.add).then_inc(masked, 1)
                ve.wait_ge(masked, a + 1)
                V.tensor_reduce(stat[:, 16:17], s[:, 0:P], AX, ALU.max)
                then(V.tensor_reduce(stat[:, 17:18], s[:, P:3 * P], AX, ALU.max))
                V.tensor_scalar(stat[:, at:at + 2], stat[:, 16:18], -HD ** -0.5, None, ALU.mult).then_inc(negmax, 1)
                ve.wait_ge(prob_exp, 2 * a + 2)
                then(V.reciprocal(stat[:, 18:20], stat[:, at + 2:at + 4]))
                V.tensor_scalar(s[:, 0:P], s[:, 0:P], stat[:, 18:19], None, ALU.mult)
                V.tensor_scalar(s[:, P:3 * P], s[:, P:3 * P], stat[:, 19:20], None, ALU.mult).then_inc(prob_ready, 1)
                ve.wait_ge(probt_done, a + 1)
                V.tensor_copy(prob_t[:, a % 2, 0:3 * P], misc[0][:, 0:3 * P]).then_inc(probt_ready, 1)

            def add_to_lat(name, ready):
                for f in range(4):
                    n = FILL[name] + f
                    fill_done(ve, n)
                    V.tensor_tensor(lat[:, 2 * f:2 * f + 2, :], acc[n % 4][:, :].rearrange("p (c t) -> p c t", c=2),
                                    lat[:, 2 * f:2 * f + 2, :], ALU.add).then_inc(acc_free[n % 4], 1)
                    ve.wait_ge(acc_free[n % 4], n // 4 + 1)
                    V.engine_nop().then_inc(ready, 1)

            add_to_lat("mix_out", lat_ready[NXATT])
            norm(NXATT, lat, h, vcol("norm_xattn_g"), h_ready[NXATT])
            for x in range(XHEADS):
                n = FILL["xq"] + x
                ve.wait_ge(xstd_ready, x + 1)
                if x == 0:
                    ve.wait_ge(h_ready[NXATT], KC)
                then(V.reciprocal(rstd[:, :], std[:, x % 2, :]))
                for c in range(2):
                    last = V.scalar_tensor_tensor(out=q_x[:, 2 * x + c, :], in0=acc[n % 4][:, c * T:(c + 1) * T],
                                                  scalar=vcol("xq_norm_g", c, 1), in1=rstd[:, :],
                                                  op0=ALU.mult, op1=ALU.mult)
                last.then_inc(acc_free[n % 4], 1)
                ve.wait_ge(acc_free[n % 4], n // 4 + 1)
                V.engine_nop().then_inc(xq_ready, 1)
            for x in range(XHEADS):
                s = prob[:, x % 2, :].rearrange("p (i m) -> p i m", i=TT)
                at = 4 * (x % 2)
                ve.wait_ge(xscore_done, x + 1)
                then(V.tensor_reduce(stat[:, 16:18], misc[2 + x % 2][:, :].rearrange("p (i m) -> p i m", i=TT), AX, ALU.max))
                if x >= 2:
                    ve.wait_ge(xprobt_done, x - 1)
                V.tensor_scalar(stat[:, at:at + 2], stat[:, 16:18], -XHD ** -0.5, None, ALU.mult).then_inc(xnegmax, 1)
                ve.wait_ge(xexp, x + 1)
                then(V.reciprocal(stat[:, 18:20], stat[:, at + 2:at + 4]))
                for i in range(TT):
                    last = V.tensor_scalar(s[:, i, :], s[:, i, :], stat[:, 18 + i:19 + i], None, ALU.mult)
                last.then_inc(xprob_ready, 1)
                ve.wait_ge(xprobt_done, x + 1)
                V.tensor_copy(prob_t[:, x % 2, :], misc[0][:, :]).then_inc(xprobt_ready, 1)
            def ffn_low(s, par, part):
                ve.wait_ge(w_hi[part], s + 1)
                V.tensor_tensor(ffn_lo[par][:, part, :], ffn_raw(par, part), ffn_hi[par][:, part, :], ALU.subtract) \
                    .then_inc(w_lo[part], 1)

            for part in range(3):
                ffn_low(0, 0, part)
            add_to_lat("xo", lat_ready[NFFN])
            for b in range(4):
                V.memset(acc[b][:, :], 0.0).then_inc(ffn_zeroed, 1)

            def x_low(k):
                ve.wait_ge(x_hi_ready, k + 1)
                V.tensor_tensor(x_lo[:, k, :], h[:, k, :], x_hi[:, k, :], ALU.subtract).then_inc(x_lo_ready, 1)

            ve.wait_ge(mean_free, NFFN + 1)
            then(V.reciprocal(rstd[:, :], std[:, NFFN % 2, :]))
            for k in range(KC):
                V.scalar_tensor_tensor(out=h[:, k, :], in0=lat[:, k, :], scalar=vcol("norm_ffn_g", k, 1), in1=rstd[:, :],
                                       op0=ALU.mult, op1=ALU.mult).then_inc(h_ready[NFFN], 1)
                if k:
                    x_low(k - 1)
            x_low(KC - 1)
            ffn_low(1, 1, 0)
            ffn_low(1, 1, 1)

            def ffn_step(s, par, base, last=0):
                ve.wait_ge(z_ready, s + 1)
                for w in (1, 0):
                    d = 2 - w
                    for g in range(2):
                        tap = vec[:, bass.ds(s + (VEC["conv_w"][0] + w * 2 * FC + g * FC), 1)]
                        ins = V.scalar_tensor_tensor(out=up_z[:, par, g, d:T], in0=misc[par][:, g * T:(g + 1) * T - d],
                                                     scalar=tap, in1=up_z[:, par, g, d:T], op0=ALU.mult, op1=ALU.add)
                    if w:
                        ins.then_inc(dve, 1)
                        ve.wait_ge(dve, s + base)
                ins.then_inc(conv2_done, 1)
                if last < 1:
                    ffn_low(s + 2, par, 0)
                ve.wait_ge(conv2_done, s + 1)
                ve.wait_ge(silu2_ready, s + 1)
                V.tensor_tensor(up_h[:, par, :], up_s[:, par, :], up_z[:, par, 1, :], ALU.mult).then_inc(hid_f, 1)
                if not isinstance(s, int) or s >= 2:
                    ve.wait_ge(down2_done, s - 1)
                V.tensor_tensor(act_hi[:, par, :], up_s[:, par, :], up_z[:, par, 1, :], ALU.mult).then_inc(act_hi_ready, 1)
                ve.wait_ge(hid_f, s + 1)
                ve.wait_ge(act_hi_ready, s + 1)
                V.tensor_tensor(act_lo[:, par, :], up_h[:, par, :], act_hi[:, par, :], ALU.subtract).then_inc(act_ready, 1)
                if last < 1:
                    ffn_low(s + 2, par, 1)
                if last < 2:
                    ffn_low(s + 1, 1 - par, 2)

            base = n_chain[0] + 1
            ffn_step(0, 0, base)
            ffn_step(1, 1, base)
            with ve.Fori(1, FC // 2 - 1) as i:
                ffn_step(i * 2, 0, base)
                ffn_step(i * 2 + 1, 1, base)
            ffn_step(FC - 2, 0, base, last=1)
            ffn_step(FC - 1, 1, base, last=2)
            ve.wait_ge(down2_done, FC)
            for f in range(4):
                V.tensor_tensor(lat[:, 2 * f:2 * f + 2, :], acc[f][:, :].rearrange("p (c t) -> p c t", c=2),
                                lat[:, 2 * f:2 * f + 2, :], ALU.add).then_inc(lat_final, 1)
            for f in range(4):
                n = FILL["rows"] + f
                fill_done(ve, n)
                V.tensor_copy(out_rows[:, :, f * 256:(f + 1) * 256],
                              acc[n % 4][:, :].rearrange("p (i d) -> p i d", i=TT)).then_inc(out_ready, 1)


def _tables(np):
    tab = np.zeros((P, TAB_COLS), np.float32)

    def put(name, value):
        at, n = TAB[name]
        tab[:, at:at + n] = value

    put("ident", np.eye(P))
    put("iota", np.arange(CAP)[None])
    half = HD // 2
    rot = np.zeros((P, P))
    head = np.zeros((P, P))
    for m in range(P):
        base, j = m // HD * HD, m % HD
        if j < half:
            rot[base + j + half, m] = -1.0
        else:
            rot[base + j - half, m] = 1.0
        head[base:base + HD, m] = 1.0 / HD
    put("rot", rot)
    put("headmean", head)
    inv_freq = (np.float32(10000.0) ** (-np.arange(half, dtype=np.float32) / np.float32(half))).astype(np.float32)
    ang = (np.arange(T, dtype=np.float32)[None, :] * inv_freq[np.arange(P) % half][:, None]).astype(np.float32)
    put("cos", np.cos(ang.astype(np.float64)))
    put("sin", np.sin(ang.astype(np.float64)))
    q, k = np.arange(P)[:, None], np.arange(P)[None, :]
    diag = np.where(k <= q, 0.0, -1e30)
    put("causal", np.concatenate([diag, np.zeros((P, P)), diag], 1))
    put("invcnt", np.concatenate([1.0 / np.minimum(np.arange(PAD) + 1, w) for w in POOL_WINDOWS])[None])
    return tab


def kernel(**inputs):
    import numpy as np
    import concourse.bacc as bacc
    from concourse.bass_utils import run_bass_kernel_spmd

    a = {n: np.asarray(v) for n, v in inputs.items()}

    def cols(v):
        return v.reshape(-1, P).T

    vectors = np.concatenate([
        cols(a["c"]), cols(a["ada_b"]), cols(a["norm_g"]), cols(a["sc_conv"]), cols(a["norm_mem_g_2"]),
        a["moe_router"][0].reshape(KC, P, N_EXPERTS).transpose(1, 0, 2).reshape(P, -1),
        cols(a["norm_mix_g_2"]), cols(a["pool_scale_2"]),
        np.concatenate([a["q_norm_g_2"][0]] * 2)[:, None], np.concatenate([a["k_norm_g_2"][0]] * 2)[:, None],
        cols(a["norm_xattn_g_2"]), cols(a["xq_norm_g_2"]), cols(a["xk_norm_g_2"]), cols(a["norm_ffn_g_2"]),
        cols(a["conv_w_2"]), cols(a["conv_b_2"])], axis=1)
    arrays = {"vectors": vectors, "tables": _tables(np), "x": a["x"], "mem": a["mem_2"], "pool_w": a["pool_w_2"],
              "ada_w": a["ada_w"], "sc_w_in": a["sc_w_in"], "sc_w_out": a["sc_w_out"], "moe_w_gate": a["moe_w_gate"],
              "moe_w_up": a["moe_w_up"], "moe_w_down": a["moe_w_down"], "w_in": a["w_in_2"], "w_out": a["w_out_2"],
              "w_xq": a["w_xq_2"], "w_xkv": a["w_xkv_2"], "w_xo": a["w_xo_2"], "w_up": a["w_up_2"],
              "w_down": a["w_down_2"]}
    nc = bacc.Bacc("TRN2", target_bir_lowering=False, num_devices=1)
    feeds, io = {}, {}
    for name, v in arrays.items():
        v = np.ascontiguousarray(v)
        feeds[f"in_{name}"] = v
        io[name] = nc.dram_tensor(f"in_{name}", v.shape, F32, kind="ExternalInput").ap()
    io["out"] = nc.dram_tensor("out", (1, T, D), F32, kind="ExternalOutput").ap()
    program(nc, io)
    r = run_bass_kernel_spmd(nc, [feeds], core_ids=[0])
    return r.results[0]["out"]
```

```python
from contextlib import ExitStack

import concourse.bass as bass
from concourse import mybir

F32 = mybir.dt.float32
F32R = mybir.dt.float32r
ACT = mybir.ActivationFunctionType
ALU = mybir.AluOpType
AX = mybir.AxisListType.X

P = 128
D = 1024
T = 256
KC = D // P
TT = T // P
EPS = 1e-6
RING = 3

N_EXPERTS = 16
CAP = 2 * T // N_EXPERTS
POOL_WINDOWS = (2, 4, 8, 16)
PG = len(POOL_WINDOWS)
PAD = 16
HEADS, HD = 8, 64
XHEADS, XHD = 4, 256
FC = 2816 // P
FFN_SLOTS = 2

VEC = {}
_at = 0
for _name, _n in (("c", KC), ("ada_b", 6 * KC), ("norm_g", 2 * KC), ("sc_conv", 3 * KC), ("norm_mem_g", KC),
                  ("router", KC * N_EXPERTS), ("norm_mix_g", KC), ("pool_scale", PG), ("q_norm_g", 1),
                  ("k_norm_g", 1), ("norm_xattn_g", KC), ("xq_norm_g", 2), ("xk_norm_g", 2), ("norm_ffn_g", KC),
                  ("conv_w", 3 * 2 * FC), ("conv_b", 2 * FC)):
    VEC[_name] = (_at, _n)
    _at += _n
VEC_COLS = _at

TAB = {}
_at = 0
for _name, _n in (("ident", P), ("iota", CAP), ("rot", P), ("headmean", P), ("cos", T), ("sin", T),
                  ("causal", 3 * P), ("invcnt", PG * PAD)):
    TAB[_name] = (_at, _n)
    _at += _n
TAB_COLS = _at

BLOCKS = ["shift1", "scale1", "sc_b", "sc_c", "gate1", "sc_v", "sc_out", "shift2", "scale2", "gate2"]
MOE0 = len(BLOCKS)
POST = ("in_uq", "in_kv", "mix_out", "xq", "xo")
SLOT = dict(zip(BLOCKS, (1, 0, 2, 1, 0, 2, 0, 1, 2, 1)))
BEFORE = {n: [b for b in BLOCKS[:i] if SLOT[b] == SLOT[n]] for i, n in enumerate(BLOCKS)}
LOADS = {n: len(BEFORE[n]) + 1 for n in BLOCKS}
for _i, _name in enumerate(POST):
    SLOT[_name] = 1 + _i % 2
    LOADS[_name] = sum(SLOT[b] == SLOT[_name] for b in BLOCKS) + N_EXPERTS + _i // 2 + 1

FILL = {}
_at = 0
for _name, _n in (("x_t", 4), ("conv_b", 4), ("conv_c", 4), ("conv_v", 4), ("conv_out", 4), ("mem_t", 4),
                  ("h2_rows", 4), ("gather", 8), ("q", 2), ("k", 2), ("u", 2), ("v", 2), ("pool", 2),
                  ("mix_out", 4), ("xq", 4), ("xo", 4), ("rows", 4)):
    FILL[_name] = _at
    _at += _n

ADA = ["shift1", "scale1", "gate1", "shift2", "scale2", "gate2"]
LAST_FILL = {"sc_b": FILL["conv_b"] + 3, "sc_c": FILL["conv_c"] + 3, "sc_v": FILL["conv_v"] + 3,
             "sc_out": FILL["conv_out"] + 3, "in_uq": FILL["u"] + 1, "in_kv": FILL["v"] + 1,
             "mix_out": FILL["mix_out"] + 3, "xq": FILL["xq"] + 3, "xo": FILL["xo"] + 3}

STAGES = 4
MIX_STEP = (1, 2, 3, 4, 5, 7, 9, 11)
PIECES, PIECE = [], {}
for _name, _f in ([(_n, _f) for _n in ("conv_b", "conv_c", "conv_v", "conv_out") for _f in range(4)] +
                  [("q", 0), ("q", 1), ("k", 0), ("u", 0), ("u", 1), ("k", 1), ("v", 0), ("v", 1)] +
                  [("mix_out", _k) for _k in range(KC)] + [("xq", _f) for _f in range(4)] +
                  [("xo", _k) for _k in range(KC)]):
    PIECE[_name, _f] = len(PIECES)
    if _name in ("mix_out", "xo"):
        for _i in range(2):
            PIECES.append((_name, _f, 1, 512 * _i, 512, FILL[_name] + 2 * _i + 1 if _f == KC - 1 else None))
        continue
    _block, _c0 = {"conv_b": ("sc_b", 0), "conv_c": ("sc_c", 0), "conv_v": ("sc_v", 0), "conv_out": ("sc_out", 0),
                   "u": ("in_uq", 0), "q": ("in_uq", 4), "k": ("in_kv", 0), "v": ("in_kv", 4), "xq": ("xq", 0)}[_name]
    for _i in range(4):
        _done = FILL[_name] + _f if _i == 3 else None
        if _name == "v":
            PIECES.append((_block, 2 * _i, 2, P * _c0 + 256 * _f, 256, _done))
        else:
            PIECES.append((_block, 4 * (_i % 2), 4, P * (_c0 + 2 * _f + _i // 2), P, _done))
POST_PIECES = PIECE["q", 0]

N1, N2, NMEM, NMIX, NXATT, NFFN = range(6)


def program(nc, io):
    with ExitStack() as ctx:
        def sb(name, shape):
            return ctx.enter_context(nc.sbuf_tensor(name, shape, F32))

        def bank(name):
            return ctx.enter_context(nc.psum_tensor(name, [P, 512], F32))

        def sem(name):
            return ctx.enter_context(nc.semaphore(name))

        def overlay(*specs):
            with ExitStack() as place:
                return [place.enter_context(nc.sbuf_tensor(name, shape, F32R)) for name, shape in specs]

        ring, ffn_hi, ffn_lo = [], [], []
        y_hi, piece_hi, piece_lo, x_lo = overlay(("y_hi", [P, KC, T]), ("piece_hi", [P, STAGES, 512]),
                                                 ("piece_lo", [P, STAGES, 512]), ("x_lo", [P, KC, T]))
        for i in range(RING):
            if i < 2:
                hi, lo = overlay((f"ffn_w_hi{i}", [P, 3, D]), (f"ffn_w_lo{i}", [P, 3, D]))
                ffn_hi.insert(0, hi)
                ffn_lo.insert(0, lo)
            ring.append(sb(f"ring{i}", [P, KC, D]))
        lat = sb("lat", [P, KC, T])
        h = sb("h", [P, KC, T])
        (x_hi,) = overlay(("x_hi", [P, KC, T]))
        mem_n = sb("mem_n", [P, KC, T])
        (early_hi,) = overlay(("early_piece_hi", [P, STAGES, 512]))
        (gather_lo,) = overlay(("h2_rows_lo", [P, TT, D]))
        k_mem = sb("k_mem", [P, KC, T])
        (early_lo,) = overlay(("early_piece_lo", [P, STAGES, 512]))
        v_mem = sb("v_mem", [P, TT, D])
        act_hi, act_lo = overlay(("act_hi", [P, 2, T]), ("act_lo", [P, 2, T]))
        kv_w = sb("kv_w", [P, KC, P])
        region_a = sb("region_a", [P, 4096])
        region_b = sb("region_b", [P, 4352])
        (y_lo,) = overlay(("y_lo", [P, KC, T]))
        (gather_hi,) = overlay(("h2_rows_hi", [P, TT, D]))
        region_c = sb("region_c", [P, 2048])
        (sel_r,) = overlay(("sel", [P, 1024]))
        region_s = sb("region_s", [P, 2048])
        sq = sb("sq", [P, 2, 512])
        std = sb("std", [P, 2, T])
        rstd = sb("rstd", [P, T])
        eps = sb("eps", [P, 1])
        spare = sb("spare", [P, 1])
        vec = sb("vec", [P, VEC_COLS])
        tab = sb("tab", [P, TAB_COLS])
        pool_w = sb("pool_w", [P, PG, P])
        ones_d = sb("ones_d", [P, P])
        ones_x = sb("ones_x", [P, P])
        silu_c = sb("silu_c", [P, KC])
        mod = sb("mod", [P, 6 * KC])
        gain1 = sb("gain1", [P, KC])
        gain2 = sb("gain2", [P, KC])
        aff = sb("aff", [P, TT, N_EXPERTS])
        aff_e = sb("aff_e", [P, TT, N_EXPERTS])
        top8 = sb("top8", [N_EXPERTS, 8])
        slot = sb("slot", [P, TT, N_EXPERTS])
        stat = sb("stat", [P, 64])

        def chunks(ap, n):
            return ap.rearrange("p (k t) -> p k t", k=n)

        x_rows = chunks(region_c[:, :], TT)
        mem_rows = chunks(region_b[:, 2304:4352], TT)
        gate_b = chunks(region_a[:, 0:2048], KC)
        gate_c = chunks(region_a[:, 2048:4096], KC)
        cv = chunks(region_b[:, 0:KC * (T + 2)], KC)
        conv = h
        sel = sel_r[:, :].rearrange("p (i e s) -> p i e s", i=TT, s=CAP)
        h2_rows = v_mem
        sel_g = region_s[:, 1024:2048].rearrange("p (b i e j s) -> p b i e j s", b=2, i=TT, e=2, j=4)
        ada_rows = chunks(region_s[:, 0:512], 2)
        xs = chunks(region_a[:, :], KC)
        scatter = region_b[:, 0:N_EXPERTS * T].rearrange("p (e t) -> p e t", e=N_EXPERTS)
        xs_e = chunks(region_c[:, 0:256], KC)
        silu_g, hid, ys_rows, scat_e = (region_c[:, 256 * i:256 * (i + 1)] for i in range(1, 5))
        hid_t = region_c[:, 1280:1536].rearrange("p (c j s) -> p c j s", c=2, j=4)
        top_work, chosen, count, slot_t, ones_r = (region_b[0:N_EXPERTS, T * i:T * (i + 1)] for i in range(5))
        q_rot = chunks(region_a[:, 0:1024], 4)
        k_rot = chunks(region_a[:, 1024:2048], 4)
        v_rows = chunks(region_a[:, 2048:3072], TT)
        qk_g = region_a[:, 3072:3584]
        qk_t = region_a[:, 3584:4096]
        UP = PAD + T
        u_pad = chunks(region_b[:, 0:PG * UP], PG)
        win_a = chunks(region_b[:, PG * UP:2 * PG * UP], PG)
        win_b = chunks(region_b[:, 2 * PG * UP:3 * PG * UP], PG)
        pooled = chunks(region_b[:, 3 * PG * UP:3 * PG * UP + PG * T], PG)
        qk_gs = (qk_g, kv_w[:, 0:4, :].rearrange("p k n -> p (k n)"))
        qk_stds = (region_s[:, 0:512], region_s[:, 1024:1536])
        prob = chunks(region_s[:, 0:3 * 384], 3)
        prob_t = chunks(region_s[:, 3 * 384:5 * 384], 2)
        xprob = chunks(region_s[:, 0:1024], 2)
        xprob_t = chunks(region_s[:, 1024:2048], 2)
        q_x = chunks(region_a[:, 0:2048], KC)
        up_z = region_a[:, 0:1024].rearrange("p (s g t) -> p s g t", s=2, g=2)
        up_s = chunks(region_a[:, 1024:1536], 2)
        up_h = chunks(region_a[:, 1536:2048], 2)
        out_rows = chunks(region_c[:, :], TT)
        ffn_up = [[ring[2][:, 2 * s + g, :].rearrange("p (k n) -> p k n", k=KC) for g in range(2)]
                  for s in range(FFN_SLOTS)]
        ffn_down = [ring[2][:, 2 * FFN_SLOTS + s, :] for s in range(FFN_SLOTS)]

        def square_slot(n_norm, f):
            if n_norm == NMEM or f < 2:
                return sq[:, f % 2, :]
            return region_s[:, 512 * f:512 * (f + 1)]

        def ffn_raw(slot, part):
            return ffn_down[slot] if part == 2 else ring[2][:, 2 * slot + part, :]

        acc = [bank(f"acc{b}") for b in range(4)]
        misc = [bank(f"misc{b}") for b in range(4)]

        logits = (misc[1][:, 0:N_EXPERTS], misc[3][:, 0:N_EXPERTS])

        def vcol(name, i=0, n=None):
            at, size = VEC[name]
            return vec[:, at + i:at + (size if n is None else i + n)]

        def table(name):
            at, size = TAB[name]
            return tab[:, at:at + size]

        ident = table("ident")
        router = vcol("router").rearrange("p (k e) -> p k e", k=KC)

        s_vec, s_tab, s_x, s_mem, s_poolw = (sem(n) for n in ("vec_in", "tab_in", "x_in", "mem_in", "poolw_in"))
        landed = [sem(f"ring_landed{i}") for i in range(RING)]
        acc_done = [sem(f"acc_done{b}") for b in range(4)]
        acc_free = [sem(f"acc_free{b}") for b in range(4)]
        ones_set = sem("ones_set")
        silu_c_ready = sem("silu_c_ready")
        sq_ready, sq_used = sem("sq_ready"), sem("sq_used")
        mean_free = sem("mean_free")
        lat_ready = [sem(f"norm_in_ready{n}") for n in range(6)]
        h_scaled = sem("h_scaled")
        h_ready = [sem(f"h_ready{n}") for n in range(6)]
        ada_done, ada_rows_ready, ada_t_done, ada_read = (
            sem(n) for n in ("ada_rows_done", "ada_rows_ready", "ada_t_done", "ada_read"))
        cv_zeroed, conv_summed, conv_ready = (sem(n) for n in ("cv_zeroed", "conv_summed", "conv_ready"))
        piece_hi_ready, piece_lo_ready, pieces_used = sem("piece_hi_ready"), sem("piece_lo_ready"), sem("pieces_used")
        y_hi_ready, y_lo_ready = sem("y_hi_ready"), sem("y_lo_ready")
        mix_zeroed, xo_zeroed = sem("mix_acc_zeroed"), sem("xo_acc_zeroed")
        dve = sem("vector_chain")
        poolc = sem("gpsimd_chain")

        def block_wait(eng, name):
            eng.wait_ge(landed[SLOT[name]], 16 * LOADS[name])

        def block_done(eng, name):
            if name in ADA:
                eng.wait_ge(ada_done, ADA.index(name) + 1)
            else:
                n = LAST_FILL[name]
                eng.wait_ge(acc_done[n % 4], n // 4 + 1)

        def block_slot(name):
            return ring[SLOT[name]][:, :, :]

        def piece_used(eng, q):
            if PIECES[q][5] is None:
                eng.wait_ge(pieces_used, sum(p[5] is None for p in PIECES[:q + 1]))
            else:
                fill_done(eng, PIECES[q][5])

        def piece_raw(q):
            name, k, nk, n, cols, _ = PIECES[q]
            return block_slot(name)[:, k:k + nk, n:n + cols]

        def piece_part(part, q):
            parts = ((early_hi, early_lo), (piece_hi, piece_lo))[q >= POST_PIECES][part]
            return parts[:, q % STAGES, :].rearrange("p (k n) -> p k n", k=PIECES[q][2])

        def fill_done(eng, n):
            eng.wait_ge(acc_done[n % 4], n // 4 + 1)

        def fill_free(eng, n):
            if n >= 4:
                eng.wait_ge(acc_free[n % 4], n // 4)

        logits_done, exp_done, aff_ready, afft_done, slot_t_ready, slot_done = (
            sem(n) for n in ("logits_done", "aff_exp_done", "aff_ready", "aff_t_done", "slot_t_ready", "slot_done"))
        negmax_r = sem("router_negmax")
        sel_ready, selg_ready, rows_ready, scat_t_done, scat_ready = (
            sem(n) for n in ("sel_ready", "sel_g_ready", "h2_rows_ready", "scatter_t_done", "scatter_ready"))
        rows_hi = sem("h2_rows_hi_ready")
        y_zeroed = sem("y_zeroed")
        xse_ready = sem("xs_e_ready")
        gate_done, up_done, silu_ready, hid_ready, hidt_done, hidt_ready, down_done, ysr_ready = (
            sem(n) for n in ("gate_done", "up_done", "silu_ready", "hid_ready", "hid_t_done", "hid_t_ready",
                             "down_done", "ys_rows_ready"))
        scate_ready, scat_free = sem("scatter_e_ready"), sem("scatter_e_free")
        kvw_in, kvw_used, kv_read = sem("kv_w_in"), sem("kv_w_used"), sem("kv_read")
        ksq_ready, kmean_done, kmean_read, k_ready = (
            sem(n) for n in ("k_sq_ready", "k_mean_done", "k_mean_read", "k_mem_ready"))
        qkg_ready, qk_prep, qk_ready = sem("qk_gained"), sem("qk_mean_rot_done"), sem("qk_ready")
        qk_read, qk_std = sem("qk_rot_read"), sem("qk_std_ready")
        xstd_ready = sem("xq_std_ready")
        v_ready, u_ready, u_zeroed, pooled_ready = (
            sem(n) for n in ("v_rows_ready", "u_ready", "u_zeroed", "pooled_ready"))
        score_done, masked, negmax, prob_exp, prob_ready, probt_done, probt_ready, pv_done = (
            sem(n) for n in ("score_done", "scores_masked", "negmax_ready", "prob_exp", "prob_ready", "prob_t_done",
                             "prob_t_ready", "pv_done"))
        xsq_ready, xmean_done, xq_ready = sem("xq_sq_ready"), sem("xq_mean_done"), sem("xq_ready")
        xscore_done, xnegmax, xexp, xprob_ready, xprobt_done, xprobt_ready, xpv_done = (
            sem(n) for n in ("xscore_done", "xnegmax_ready", "xprob_exp", "xprob_ready", "xprob_t_done",
                             "xprob_t_ready", "xpv_done"))
        ffn_up_in = [sem(f"ffn_up_w_in{s}") for s in range(FFN_SLOTS)]
        ffn_down_in = [sem(f"ffn_down_w_in{s}") for s in range(FFN_SLOTS)]
        w_hi, w_lo = ([sem(f"ffn_{n}_{part}_ready") for n in ("gate", "value", "down")] for part in ("hi", "lo"))
        x_hi_ready, x_lo_ready = sem("x_hi_ready"), sem("x_lo_ready")
        hid_f, act_hi_ready = sem("ffn_hidden_ready"), sem("ffn_act_hi_ready")
        up2_done, z_ready, conv2_done, silu2_ready, act_ready, ffn_zeroed, down2_done, ffn_done = (
            sem(n) for n in ("ffn_up_done", "ffn_z_ready", "ffn_conv_done", "ffn_silu_ready", "ffn_act_ready",
                             "ffn_acc_zeroed", "ffn_down_done", "ffn_done"))
        lat_final, out_ready, s_out = sem("lat_final"), sem("out_rows_ready"), sem("out_stored")

        def wblock(ap):
            return ap.rearrange("(k p) n -> p k n", p=P)

        ada = io["ada_w"][0]
        stream = {"shift1": ada[:, 0:D], "scale1": ada[:, D:2 * D], "gate1": ada[:, 2 * D:3 * D],
                  "shift2": ada[:, 3 * D:4 * D], "scale2": ada[:, 4 * D:5 * D], "gate2": ada[:, 5 * D:6 * D],
                  "sc_b": io["sc_w_in"][0][:, 0:D], "sc_c": io["sc_w_in"][0][:, D:2 * D],
                  "sc_v": io["sc_w_in"][0][:, 2 * D:3 * D], "sc_out": io["sc_w_out"][0],
                  "in_uq": io["w_in"][0][:, 0:D], "in_kv": io["w_in"][0][:, D:2 * D],
                  "mix_out": io["w_out"][0], "xq": io["w_xq"][0], "xo": io["w_xo"][0]}

        block = ctx.enter_context(nc.Block())

        @block.sync
        def _(sp):
            def load_block(name):
                if BEFORE.get(name):
                    block_done(sp, BEFORE[name][-1])
                elif name in POST[:2]:
                    sp.wait_ge((gate_done, up_done)[POST.index(name)], N_EXPERTS)
                elif name in POST:
                    block_done(sp, POST[POST.index(name) - 2])
                sp.dma_start(block_slot(name), wblock(stream[name])).then_inc(landed[SLOT[name]], 16)

            sp.dma_start(x_rows, io["x"][0].rearrange("(i p) d -> p i d", p=P)).then_inc(s_x, 16)
            sp.dma_start(vec[:, :], io["vectors"]).then_inc(s_vec, 16)
            for name in BLOCKS:
                load_block(name)
                if name == "sc_c":
                    sp.dma_start(mem_rows, io["mem"][0].rearrange("(i p) d -> p i d", p=P)).then_inc(s_mem, 16)
            experts = (io["moe_w_gate"], io["moe_w_up"], io["moe_w_down"])
            for j in (1, 2, 0):
                w = experts[j]
                block_done(sp, [b for b in BLOCKS if SLOT[b] == (MOE0 + j) % RING][-1])
                sp.dma_start(ring[(MOE0 + j) % RING][:, :, :], wblock(w[0, 0])).then_inc(landed[(MOE0 + j) % RING], 16)
            with sp.Fori(1, N_EXPERTS) as e:
                for j, (w, done) in enumerate(zip(experts, (gate_done, up_done, down_done))):
                    m = MOE0 + j
                    sp.wait_ge(done, e)
                    sp.dma_start(ring[m % RING][:, :, :],
                                 w[0, bass.ds(e, 1)].rearrange("o (k p) n -> p (o k) n", p=P)) \
                      .then_inc(landed[m % RING], 16)
            for name in POST:
                load_block(name)
            w_up, w_down = io["w_up"][0], io["w_down"][0]

            def load_up(s, slot):
                for g in range(2):
                    sp.dma_start(ffn_up[slot][g],
                                 w_up[:, bass.ds(s * P + g * FC * P, P)].rearrange("(k p) n -> p k n", p=P)) \
                      .then_inc(ffn_up_in[slot], 16)

            def load_down(s, slot):
                sp.dma_start(ffn_down[slot], w_down[bass.ds(s * P, P), :]).then_inc(ffn_down_in[slot], 16)

            block_done(sp, "xq")
            for s in range(FFN_SLOTS):
                load_up(s, s)
                load_down(s, s)
            with sp.Fori(1, FC // FFN_SLOTS) as i:
                for slot in range(FFN_SLOTS):
                    sp.wait_ge(w_lo[1], i * FFN_SLOTS + (slot - FFN_SLOTS + 1))
                    load_up(i * FFN_SLOTS + slot, slot)
                    sp.wait_ge(w_lo[2], i * FFN_SLOTS + (slot - FFN_SLOTS + 1))
                    load_down(i * FFN_SLOTS + slot, slot)
            out_v = io["out"][0].rearrange("(i p) d -> p i d", p=P)
            for f in range(4):
                sp.wait_ge(out_ready, f + 1)
                sp.dma_start(out_v[:, :, f * 256:(f + 1) * 256], out_rows[:, :, f * 256:(f + 1) * 256]) \
                  .then_inc(s_out, 16)
            sp.wait_ge(s_out, 64)

        @block.gpsimd
        def _(pool):
            nc.gpsimd.memset(ones_d[:, :], 1.0 / D).then_inc(ones_set, 1)
            nc.gpsimd.memset(ones_x[:, :], 1.0 / XHD).then_inc(ones_set, 1)
            nc.gpsimd.memset(eps[:, :], EPS).then_inc(ones_set, 1)
            nc.gpsimd.memset(cv[:, :, 0:1], 0.0).then_inc(cv_zeroed, 1)
            nc.gpsimd.memset(cv[:, :, T + 1:T + 2], 0.0).then_inc(cv_zeroed, 1)
            xkv = io["w_xkv"][0]
            block_wait(pool, "sc_b")
            pool.dma_start(pool_w[:, :, :], io["pool_w"][0].rearrange("g c n -> c g n")).then_inc(s_poolw, 16)
            pool.dma_start(kv_w[:, :, :], wblock(xkv[:, 0:P])).then_inc(kvw_in, 16)
            for f in range(3):
                pair = slice(2 * f, 2 * f + 2)
                pool.wait_ge(conv_summed, f + 1)
                nc.gpsimd.tensor_tensor(conv[:, pair, :], conv[:, pair, :], gate_b[:, pair, :], ALU.mult) \
                    .then_inc(conv_ready, 2)
            for f in range(4):
                cols = slice((f % 2) * 512, (f % 2 + 1) * 512)
                pool.wait_ge(rows_hi, f + 1)
                nc.gpsimd.tensor_tensor(gather_lo[:, f // 2, cols], h2_rows[:, f // 2, cols], gather_hi[:, f // 2, cols],
                                        ALU.subtract).then_inc(rows_ready, 1)
            with pool.Fori(1, N_EXPERTS) as e:
                pool.wait_ge(kvw_used, e)
                pool.dma_start(kv_w[:, :, :], xkv[:, bass.ds(e * P, P)].rearrange("(k p) n -> p k n", p=P)) \
                    .then_inc(kvw_in, 16)
            pool.wait_ge(scat_free, N_EXPERTS + 1)
            nc.gpsimd.memset(u_pad[:, :, 0:PAD], 0.0).then_inc(u_zeroed, 1)
            pool.wait_ge(u_zeroed, 1)
            pool.wait_ge(u_ready, 2)
            n = 0
            src, dst = u_pad, win_a
            for g in range(PG):
                w = 1 << g
                lo = 2 * w - 1
                nc.gpsimd.tensor_tensor(dst[:, g:PG, lo:UP], src[:, g:PG, lo:UP], src[:, g:PG, lo - w:UP - w],
                                        ALU.add).then_inc(poolc, 1)
                n += 1
                pool.wait_ge(poolc, n)
                nc.gpsimd.tensor_scalar(pooled[:, g, :], dst[:, g, PAD:UP], 1.0 / POOL_WINDOWS[g], None,
                                        ALU.mult).then_inc(poolc, 1)
                n += 1
                pool.wait_ge(poolc, n)
                inv = table("invcnt").rearrange("p (g t) -> p g t", g=PG)
                nc.gpsimd.tensor_tensor(pooled[:, g, 0:PAD], dst[:, g, PAD:2 * PAD], inv[:, g, :],
                                        ALU.mult).then_inc(poolc, 1)
                n += 1
                pool.wait_ge(poolc, n)
                nc.gpsimd.tensor_tensor(pooled[:, g, :], pooled[:, g, :], u_pad[:, g, PAD:UP],
                                        ALU.subtract).then_inc(pooled_ready, 1)
                src = dst
                dst = win_b if dst is win_a else win_a

        @block.tensor
        def _(pe):
            mm = nc.tensor.matmul

            def transpose_rows(rows, first):
                for f in range(4):
                    n = first + f
                    fill_free(pe, n)
                    for c in range(2):
                        for i in range(TT):
                            k = 2 * f + c
                            last = nc.tensor.transpose(acc[n % 4][:, c * T + i * P:c * T + (i + 1) * P],
                                                       rows[:, i, k * P:(k + 1) * P], ident)
                    last.then_inc(acc_done[n % 4], 1)

            def norm_mean(n_norm):
                if n_norm:
                    pe.wait_ge(mean_free, n_norm)
                for f in range(4):
                    pe.wait_ge(sq_ready, 4 * n_norm + f + 1)
                    for c in range(2):
                        last = mm(misc[0][:, 0:T], ones_d[:, :], square_slot(n_norm, f)[:, c * T:(c + 1) * T],
                                  start=(f == 0 and c == 0), stop=(f == 3 and c == 1))
                    last.then_inc(sq_used, 1)

            def rows_product(out, w, stationary):
                for k in range(KC):
                    for j in range(4):
                        last = mm(out[CAP * j:CAP * (j + 1), 0:256], stationary(k), w[:, k, 256 * j:256 * (j + 1)],
                                  start=(k == 0), stop=(k == KC - 1))
                return last

            def ada_block(name, j):
                block_wait(pe, name)
                if j >= 2:
                    pe.wait_ge(ada_rows_ready, j - 1)
                rows_product(misc[1 + 2 * (j % 2)], block_slot(name),
                             lambda k: silu_c[:, k:k + 1].to_broadcast([P, CAP])).then_inc(ada_done, 1)

            def ada_columns(j):
                pe.wait_ge(ada_rows_ready, j + 1)
                if j:
                    pe.wait_ge(ada_read, j)
                for c in range(2):
                    last = nc.tensor.transpose(misc[2][:, c * P:(c + 1) * P], ada_rows[:, j % 2, c * P:(c + 1) * P], ident)
                last.then_inc(ada_t_done, 1)

            def split_mm(out, w, x, start, stop, swap=False):
                for i, (a, b) in enumerate(((0, 0), (0, 1), (1, 0))):
                    lhs, rhs = (x[b], w[a]) if swap else (w[a], x[b])
                    last = mm(out, lhs, rhs, start=start and i == 0, stop=stop and i == 2, skip_group_check=True)
                return last

            def parts(q):
                pe.wait_ge(piece_lo_ready, q + 1)
                return piece_part(0, q), piece_part(1, q)

            def split_fill(name, f, x_base=None, between=None, x_lo=x_lo):
                n = FILL[name] + f
                if name != "xq":
                    fill_free(pe, n)
                for i in range(4):
                    if i == 2 and between:
                        between()
                    q = PIECE[name, f] + i
                    hi, lo = parts(q)
                    for kk in range(4):
                        k = 4 * (i % 2) + kk
                        if x_base is not None and i < 2:
                            pe.wait_ge(x_lo_ready, x_base + k + 1)
                        last = split_mm(acc[n % 4][:, (i // 2) * T:(i // 2 + 1) * T], (hi[:, kk, :], lo[:, kk, :]),
                                        (x_hi[:, k, :], x_lo[:, k, :]), k == 0, k == KC - 1)
                    last.then_inc(pieces_used if i < 3 else acc_done[n % 4], 1)

            def split_rows(f, between=None):
                n = FILL["v"] + f
                fill_free(pe, n)
                for t in range(TT):
                    if t and between:
                        between()
                    for i in range(4):
                        q = PIECE["v", f] + i
                        hi, lo = parts(q)
                        for kk in range(2):
                            k = 2 * i + kk
                            x = (x_hi[:, k, t * P:(t + 1) * P], x_lo[:, k, t * P:(t + 1) * P])
                            last = split_mm(acc[n % 4][:, t * T:(t + 1) * T], (hi[:, kk, :], lo[:, kk, :]), x,
                                            k == 0, k == KC - 1, swap=True)
                        if t == TT - 1:
                            last.then_inc(pieces_used if i < 3 else acc_done[n % 4], 1)

            def split_row_chunk(name, k):
                for i in range(2):
                    q = PIECE[name, k] + i
                    hi, lo = parts(q)
                    for c in range(4):
                        n = FILL[name] + 2 * i + c // 2
                        cols = slice(c * P, (c + 1) * P)
                        last = split_mm(acc[n % 4][:, (c % 2) * T:(c % 2 + 1) * T], (hi[:, 0, cols], lo[:, 0, cols]),
                                        (y_hi[:, k, :], y_lo[:, k, :]), False, False)
                        if k == KC - 1 and c % 2:
                            last.then_inc(acc_done[n % 4], 1)
                    if k < KC - 1:
                        last.then_inc(pieces_used, 1)

            pe.wait_ge(s_tab, 16)
            pe.wait_ge(s_x, 16)
            transpose_rows(x_rows, FILL["x_t"])
            pe.wait_ge(ones_set, 3)
            norm_mean(N1)
            pe.wait_ge(silu_c_ready, 1)
            ada_block("shift1", 0)
            ada_block("scale1", 1)
            ada_columns(0)
            ada_columns(1)
            for name in ("conv_b", "conv_c", "conv_v"):
                for f in range(4):
                    split_fill(name, f, 0 if name == "conv_b" and f == 0 else None, x_lo=y_lo)
                if name == "conv_b":
                    ada_block("gate1", 2)
                elif name == "conv_c":
                    ada_columns(2)
            ada_block("shift2", 3)
            for f in range(4):
                split_fill("conv_out", f, None if f else KC, x_lo=y_lo)
                if f == 2:
                    ada_block("scale2", 4)
                    ada_columns(3)
            norm_mean(N2)
            ada_columns(4)
            pe.wait_ge(s_mem, 16)
            transpose_rows(mem_rows, FILL["mem_t"])
            for k in range(KC):
                pe.wait_ge(h_ready[N2], k + 1)
                for i in range(TT):
                    last = mm(logits[i], h[:, k, i * P:(i + 1) * P], router[:, k, :], start=(k == 0), stop=(k == KC - 1))
            last.then_inc(logits_done, 1)

            def h2_transposes(f):
                n = FILL["h2_rows"] + f
                fill_free(pe, n)
                i = f // 2
                for c in range(4):
                    k = 4 * (f % 2) + c
                    last = nc.tensor.transpose(acc[n % 4][:, c * P:(c + 1) * P], h[:, k, i * P:(i + 1) * P], ident)
                last.then_inc(acc_done[n % 4], 1)

            pe.wait_ge(aff_ready, 1)
            for i in range(TT):
                last = nc.tensor.transpose(misc[2][0:N_EXPERTS, i * P:(i + 1) * P], aff[:, i, :], ident)
            last.then_inc(afft_done, 1)
            for f in range(4):
                h2_transposes(f)
            pe.wait_ge(exp_done, 2)
            ada_block("gate2", 5)
            pe.wait_ge(slot_t_ready, 1)
            pe.wait_ge(ada_rows_ready, 6)
            for i in range(TT):
                last = nc.tensor.transpose(misc[3][:, i * N_EXPERTS:(i + 1) * N_EXPERTS],
                                           slot_t[:, i * P:(i + 1) * P], ident[0:N_EXPERTS, 0:N_EXPERTS])
            last.then_inc(slot_done, 1)
            ada_columns(5)
            pe.wait_ge(sel_ready, 1)
            pe.wait_ge(rows_ready, 4)
            for k in range(KC):
                n = FILL["gather"] + k
                fill_free(pe, n)
                for i in range(TT):
                    for j, rows in enumerate((gather_hi, gather_lo)):
                        last = mm(acc[n % 4][:, :], rows[:, i, k * P:(k + 1) * P],
                                  sel[:, i, :, :].rearrange("p e s -> p (e s)"), start=(i == 0 and j == 0),
                                  stop=(i == TT - 1 and j == 1))
                last.then_inc(acc_done[n % 4], 1)

            def scatter_matrices():
                for p in range(N_EXPERTS // 2):
                    pe.wait_ge(selg_ready, p + 1)
                    if p >= 2:
                        pe.wait_ge(scat_ready, p - 1)
                    for j in range(2):
                        for i in range(TT):
                            last = nc.tensor.transpose(
                                misc[2 + p % 2][:, j * T + i * P:j * T + (i + 1) * P],
                                sel_g[:, p % 2, i, j, :, :].rearrange("p j s -> p (j s)"), ident)
                    last.then_inc(scat_t_done, 1)
                pe.wait_ge(scat_ready, N_EXPERTS // 2)
                nc.tensor.nop().then_inc(scat_free, 1)

            gate_w, up_w, down_w = (ring[(MOE0 + j) % RING] for j in range(3))
            uses = [sum(SLOT[b] == (MOE0 + j) % RING for b in BLOCKS) + 1 for j in range(3)]

            def expert_in(e):
                pe.wait_ge(xse_ready, e + 1)
                pe.wait_ge(landed[MOE0 % RING], e * 16 + 16 * uses[0])
                rows_product(misc[0], gate_w, lambda k: xs_e[:, k, :]).then_inc(gate_done, 1)
                pe.wait_ge(landed[(MOE0 + 1) % RING], e * 16 + 16 * uses[1])
                rows_product(misc[1], up_w, lambda k: xs_e[:, k, :]).then_inc(up_done, 1)

            def keys_values(e, values):
                pe.wait_ge(kvw_in, e * 16 + 16)
                pe.wait_ge(silu_ready, e + 1)
                if not values:
                    for k in range(KC):
                        last = mm(misc[0][:, 0:T], kv_w[:, k, :], mem_n[:, k, :], start=(k == 0), stop=(k == KC - 1))
                else:
                    for i in range(TT):
                        for k in range(KC):
                            last = mm(misc[0][:, i * P:(i + 1) * P], mem_n[:, k, i * P:(i + 1) * P], kv_w[:, k, :],
                                      start=(k == 0), stop=(k == KC - 1))
                last.then_inc(kvw_used, 1)

            def expert_down(e):
                pe.wait_ge(hid_ready, e + 1)
                for c in range(2):
                    last = nc.tensor.transpose(misc[2][:, c * P:(c + 1) * P], hid[:, c * P:(c + 1) * P], ident)
                last.then_inc(hidt_done, 1)
                pe.wait_ge(hidt_ready, e + 1)
                pe.wait_ge(landed[(MOE0 + 2) % RING], e * 16 + 16 * uses[2])
                rows_product(misc[3], down_w, lambda k: hid_t[:, k % 2, k // 2, :]).then_inc(down_done, 1)

            def expert_add(e):
                pe.wait_ge(ysr_ready, e + 1)
                pe.wait_ge(scate_ready, e + 1)
                for c in range(2):
                    for j in range(4):
                        g = slice(CAP * j, CAP * (j + 1))
                        last = mm(acc[j][:, c * T:(c + 1) * T], ys_rows[g, c * P:(c + 1) * P], scat_e[g, :],
                                  start=False, stop=False, skip_group_check=True)
                last.then_inc(scat_free, 1)
                pe.wait_ge(kv_read, e + 1)

            def expert(e, values):
                expert_in(e)
                keys_values(e, values)
                expert_down(e)
                expert_add(e)

            expert_in(0)
            pe.wait_ge(silu_ready, 1)
            norm_mean(NMEM)
            scatter_matrices()
            expert_down(0)
            pe.wait_ge(h_ready[NMEM], KC)
            keys_values(0, False)
            pe.wait_ge(y_zeroed, 4)
            expert_add(0)
            with pe.Fori(1, N_EXPERTS // 2) as e:
                expert(e, False)
            for x in range(XHEADS):
                pe.wait_ge(ksq_ready, x + 1)
                if x:
                    pe.wait_ge(kmean_read, x)
                for c in range(2):
                    last = mm(misc[0][:, 0:T], ones_x[:, :], sq[:, x % 2, c * T:(c + 1) * T], start=(c == 0), stop=(c == 1))
                last.then_inc(kmean_done, 1)
            pe.wait_ge(kmean_read, XHEADS)
            with pe.Fori(N_EXPERTS // 2, N_EXPERTS) as e:
                expert(e, True)

            norm_mean(NMIX)
            rot, headmean = table("rot"), table("headmean")

            def qk_mean_rot(j):
                pe.wait_ge(qkg_ready, j + 1)
                if j >= 2:
                    pe.wait_ge(qk_read, j - 1)
                    pe.wait_ge(qk_std, j - 1)
                mm(misc[2 * (j % 2)][:, :], headmean, sq[:, j % 2, :], start=True, stop=True)
                mm(misc[2 * (j % 2) + 1][:, :], rot, qk_gs[j % 2], start=True, stop=True).then_inc(qk_prep, 1)

            split_fill("q", 0, 2 * KC)
            split_fill("q", 1, between=lambda: qk_mean_rot(0))
            split_fill("k", 0, between=lambda: qk_mean_rot(1))
            split_fill("u", 0, between=lambda: qk_mean_rot(2))
            split_fill("u", 1)
            split_fill("k", 1)
            split_rows(0, between=lambda: qk_mean_rot(3))
            pe.wait_ge(s_poolw, 16)
            for f in range(2):
                n = FILL["pool"] + f
                fill_free(pe, n)
                pe.wait_ge(pooled_ready, 2 * f + 2)
                for j in range(2):
                    g = 2 * f + j
                    last = mm(acc[n % 4][:, j * T:(j + 1) * T], pool_w[:, g, :], pooled[:, g, :], start=True, stop=True)
                last.then_inc(acc_done[n % 4], 1)
            split_rows(1)

            def scores(a):
                c, lo = a // 2, HD * (a % 2)
                if a == 0:
                    pe.wait_ge(qk_ready, 4)
                if a >= 2:
                    pe.wait_ge(masked, a - 1)
                b = misc[2 + a % 2]
                mm(b[:, 0:P], q_rot[lo:lo + HD, c, 0:P], k_rot[lo:lo + HD, c, 0:P], start=True, stop=True)
                mm(b[:, P:3 * P], q_rot[lo:lo + HD, c, P:T], k_rot[lo:lo + HD, c, :],
                   start=True, stop=True).then_inc(score_done, 1)

            def transpose_probs(a):
                pe.wait_ge(prob_ready, a + 1)
                if a:
                    pe.wait_ge(probt_ready, a)
                for b in range(3):
                    last = nc.tensor.transpose(misc[0][:, b * P:(b + 1) * P], prob[:, a % 3, b * P:(b + 1) * P], ident)
                last.then_inc(probt_done, 1)

            def weigh(a):
                p, lo = a // 2, HD * (a % 2)
                pe.wait_ge(probt_ready, a + 1)
                if p >= 2:
                    pe.wait_ge(y_lo_ready, 2 + p - 1)
                o = misc[1][lo:lo + HD, (p % 2) * T:(p % 2 + 1) * T]
                mm(o, v_rows[:, 0, a * HD:(a + 1) * HD], prob_t[:, a % 2, 0:T], start=True, stop=False)
                mm(o[:, P:T], v_rows[:, 1, a * HD:(a + 1) * HD], prob_t[:, a % 2, T:T + P],
                   start=False, stop=True).then_inc(pv_done, 1)

            scores(0)
            pe.wait_ge(v_ready, TT)
            for a in range(HEADS + 4):
                if a + 1 < HEADS:
                    scores(a + 1)
                if 1 <= a <= HEADS:
                    transpose_probs(a - 1)
                if 2 <= a <= HEADS + 1:
                    weigh(a - 2)
                if a in MIX_STEP:
                    k = MIX_STEP.index(a)
                    if k == 0:
                        pe.wait_ge(mix_zeroed, 4)
                    pe.wait_ge(y_lo_ready, k // 2 + 1 if k < PG else k - 1)
                    split_row_chunk("mix_out", k)

            norm_mean(NXATT)

            def x_mean(x):
                pe.wait_ge(xsq_ready, x + 1)
                if x:
                    pe.wait_ge(xstd_ready, x)
                for c in range(2):
                    last = mm(misc[0][:, 0:T], ones_x[:, :], sq[:, x % 2, c * T:(c + 1) * T], start=(c == 0), stop=(c == 1))
                last.then_inc(xmean_done, 1)

            def x_scores(x):
                pe.wait_ge(xq_ready, x + 1)
                if x >= 2:
                    pe.wait_ge(xexp, x - 1)
                b = misc[2 + x % 2]
                for i in range(TT):
                    for c in range(2):
                        last = mm(b[:, i * T:(i + 1) * T], q_x[:, 2 * x + c, i * P:(i + 1) * P], k_mem[:, 2 * x + c, :],
                                  start=(c == 0), stop=(c == 1))
                last.then_inc(xscore_done, 1)

            def x_transpose(x):
                pe.wait_ge(xprob_ready, x + 1)
                if x:
                    pe.wait_ge(xprobt_ready, x)
                for j in range(TT):
                    for i in range(TT):
                        last = nc.tensor.transpose(misc[0][:, j * T + i * P:j * T + (i + 1) * P],
                                                   xprob[:, x % 2, i * T + j * P:i * T + (j + 1) * P], ident)
                last.then_inc(xprobt_done, 1)

            def x_weigh(x):
                pe.wait_ge(xprobt_ready, x + 1)
                if x:
                    pe.wait_ge(y_lo_ready, 6 + x)
                for c in range(2):
                    for j in range(TT):
                        at = x * XHD + c * P
                        last = mm(misc[1][:, c * T:(c + 1) * T], v_mem[:, j, at:at + P], xprob_t[:, x % 2, j * T:(j + 1) * T],
                                  start=(j == 0), stop=(j == TT - 1))
                last.then_inc(xpv_done, 1)

            for x in range(XHEADS):
                split_fill("xq", x, None if x else 3 * KC, (lambda: x_mean(x - 1)) if x else None)
            def x_out(k):
                if k == 0:
                    pe.wait_ge(xo_zeroed, 4)
                pe.wait_ge(y_lo_ready, 6 + k // 2 + 1)
                split_row_chunk("xo", k)

            x_scores(0)
            x_mean(XHEADS - 1)
            x_scores(1)
            x_scores(2)
            x_transpose(0)
            x_scores(3)
            x_transpose(1)
            x_weigh(0)
            x_weigh(1)
            x_out(0)
            x_out(1)
            x_transpose(2)
            x_out(2)
            x_transpose(3)
            x_weigh(2)
            x_out(3)
            x_weigh(3)
            for k in range(4, KC):
                x_out(k)

            norm_mean(NFFN)
            pe.wait_ge(ffn_zeroed, 4)

            def ffn_up_step(s, par):
                first = isinstance(s, int) and s == 0
                if not isinstance(s, int) or s >= 2:
                    pe.wait_ge(conv2_done, s - 1)
                for g in range(2):
                    pe.wait_ge(w_lo[g], s + 1)
                    for k in range(KC):
                        if first and g == 0:
                            pe.wait_ge(x_lo_ready, 4 * KC + k + 1)
                        n = slice(k * P, (k + 1) * P)
                        last = split_mm(misc[par][:, g * T:(g + 1) * T], (ffn_hi[par][:, g, n], ffn_lo[par][:, g, n]),
                                        (x_hi[:, k, :], x_lo[:, k, :]), k == 0, k == KC - 1)
                last.then_inc(up2_done, 1)

            def ffn_down_step(s, par, final=False):
                pe.wait_ge(w_lo[2], s + 1)
                pe.wait_ge(act_ready, s + 1)
                for c in range(KC):
                    n = slice(c * P, (c + 1) * P)
                    last = split_mm(acc[c // 2][:, (c % 2) * T:(c % 2 + 1) * T], (ffn_hi[par][:, 2, n], ffn_lo[par][:, 2, n]),
                                    (act_hi[:, par, :], act_lo[:, par, :]), False, False)
                    if final and c % 2:
                        last.then_inc(ffn_done, 1)
                if not final:
                    last.then_inc(down2_done, 1)

            ffn_up_step(0, 0)
            ffn_up_step(1, 1)
            ffn_down_step(0, 0)
            with pe.Fori(1, FC // 2) as i:
                for par in range(2):
                    ffn_up_step(i * 2 + par, par)
                    ffn_down_step(i * 2 + (par - 1), 1 - par)
            ffn_down_step(FC - 1, 1, final=True)

            for f in range(4):
                n = FILL["rows"] + f
                pe.wait_ge(lat_final, max(f, n % 4) + 1)
                for i in range(TT):
                    for c in range(2):
                        last = nc.tensor.transpose(acc[n % 4][:, i * T + c * P:i * T + (c + 1) * P],
                                                   lat[:, 2 * f + c, i * P:(i + 1) * P], ident)
                last.then_inc(acc_done[n % 4], 1)

        @block.scalar
        def _(act):
            A = nc.scalar.activation
            act.dma_start(tab[:, :], io["tables"]).then_inc(s_tab, 16)

            def squares(n_norm, src, before={}):
                for f in range(4):
                    if f in before:
                        before[f]()
                    act.wait_ge(lat_ready[n_norm], f + 1)
                    if n_norm == NMEM and f >= 2:
                        act.wait_ge(sq_used, 4 * n_norm + f - 1)
                    A(square_slot(n_norm, f), src[:, 2 * f:2 * f + 2, :], ACT.Square).then_inc(sq_ready, 1)

            def deviation(n_norm):
                act.wait_ge(sq_used, 4 * (n_norm + 1))
                A(std[:, n_norm % 2, :], misc[0][:, 0:T], ACT.Sqrt, bias=eps[:, :]).then_inc(mean_free, 1)

            def piece_high(q, n=1):
                for q in range(q, q + n):
                    if q % 4 == 0:
                        block_wait(act, PIECES[q][0])
                    if q >= STAGES:
                        piece_used(act, q - STAGES)
                    A(piece_part(0, q), piece_raw(q), ACT.Copy).then_inc(piece_hi_ready, 1)

            def load_table(function):
                A(spare[:, :], eps[:, :], function)

            def input_high(n_norm):
                for k in range(KC):
                    act.wait_ge(h_ready[n_norm], k + 1)
                    A(x_hi[:, k, :], h[:, k, :], ACT.Copy).then_inc(x_hi_ready, 1)

            act.wait_ge(ones_set, 3)
            act.wait_ge(s_vec, 16)
            A(silu_c[:, :], vcol("c"), ACT.Silu).then_inc(silu_c_ready, 1)
            squares(N1, lat)
            deviation(N1)
            def ada_copy(j):
                act.wait_ge(ada_done, j + 1)
                if j >= 2:
                    act.wait_ge(ada_t_done, j - 1)
                A(ada_rows[:, j % 2, :], misc[1 + 2 * (j % 2)][:, 0:256], ACT.Copy).then_inc(ada_rows_ready, 1)

            ada_copy(0)
            ada_copy(1)
            for k in range(KC):
                act.wait_ge(h_scaled, k + 1)
                A(x_hi[:, k, :], h[:, k, :], ACT.Identity, bias=mod[:, k:k + 1]).then_inc(x_hi_ready, 1)
                if k == 3:
                    piece_high(PIECE["conv_b", 0], 2)
            piece_high(PIECE["conv_b", 0] + 2, 2)
            for f in range(12):
                piece_high(PIECE["conv_b", 0] + 4 * (f + 1), 4)
                if f < 8:
                    n = FILL["conv_b"] + f
                    fill_done(act, n)
                    A((gate_b, gate_c)[f // 4][:, 2 * (f % 4):2 * (f % 4) + 2, :], acc[n % 4][:, :], ACT.Copy) \
                        .then_inc(acc_free[n % 4], 1)
                if f == 3:
                    ada_copy(2)
            ada_copy(3)
            fill_done(act, FILL["conv_v"] + 3)
            for f in range(4):
                act.wait_ge(conv_ready, 2 * f + 2)
                A(x_hi[:, 2 * f:2 * f + 2, :], conv[:, 2 * f:2 * f + 2, :], ACT.Copy).then_inc(x_hi_ready, 2)
            piece_high(PIECE["conv_out", 1], 12)
            ada_copy(4)
            squares(N2, lat)
            deviation(N2)
            for k in range(KC):
                act.wait_ge(h_scaled, KC + k + 1)
                A(h[:, k, :], h[:, k, :], ACT.Identity, bias=mod[:, 3 * KC + k:3 * KC + k + 1]).then_inc(h_ready[N2], 1)
            load_table(ACT.Exp)
            act.wait_ge(negmax_r, 1)
            for i in range(TT):
                A(aff_e[:, i, :], logits[i], ACT.Exp, bias=stat[:, i:i + 1],
                  accum_out=stat[:, 2 + i:3 + i]).then_inc(exp_done, 1)
            for f in range(4):
                n = FILL["mem_t"] + f
                fill_done(act, n)
                A(mem_n[:, 2 * f:2 * f + 2, :], acc[n % 4][:, :], ACT.Copy).then_inc(acc_free[n % 4], 1)
            for f in range(4):
                n = FILL["h2_rows"] + f
                fill_done(act, n)
                cols = slice((f % 2) * 512, (f % 2 + 1) * 512)
                A(gather_hi[:, f // 2, cols], acc[n % 4][:, :], ACT.Copy)
                A(h2_rows[:, f // 2, cols], acc[n % 4][:, :], ACT.Copy).then_inc(acc_free[n % 4], 1)
                act.wait_ge(acc_free[n % 4], n // 4 + 1)
                nc.scalar.nop().then_inc(rows_hi, 1)
            ada_copy(5)
            for k in range(0, KC, 2):
                n = FILL["gather"] + k
                fill_done(act, n)
                A(xs[:, k, :], acc[n % 4][:, :], ACT.Copy).then_inc(acc_free[n % 4], 1)

            def expert(e):
                act.wait_ge(gate_done, e + 1)
                A(silu_g, misc[0][:, 0:256], ACT.Silu).then_inc(silu_ready, 1)
                expert_out(e)

            def expert_out(e):
                act.wait_ge(hidt_done, e + 1)
                A(hid_t, misc[2][:, 0:256].rearrange("p (c j s) -> p c j s", c=2, j=4), ACT.Copy).then_inc(hidt_ready, 1)
                if isinstance(e, int):
                    deviation(NMEM)
                act.wait_ge(down_done, e + 1)
                A(ys_rows, misc[3][:, 0:256], ACT.Copy).then_inc(ysr_ready, 1)

            load_table(ACT.Silu)
            for f in range(4):
                act.wait_ge(acc_free[(FILL["mem_t"] + f) % 4], (FILL["mem_t"] + f) // 4 + 1)
            nc.scalar.nop().then_inc(lat_ready[NMEM], 4)
            act.wait_ge(gate_done, 1)
            A(silu_g, misc[0][:, 0:256], ACT.Silu).then_inc(silu_ready, 1)
            squares(NMEM, mem_n)
            for p in range(N_EXPERTS // 2):
                act.wait_ge(scat_t_done, p + 1)
                A(scatter[:, 2 * p:2 * p + 2, :], misc[2 + p % 2][:, :], ACT.Copy).then_inc(scat_ready, 1)
            expert_out(0)
            with act.Fori(1, N_EXPERTS // 2) as e:
                expert(e)
            for x in range(XHEADS):
                act.wait_ge(kv_read, 2 * x + 2)
                if x >= 2:
                    act.wait_ge(kmean_done, x - 1)
                A(sq[:, x % 2, :], k_mem[:, 2 * x:2 * x + 2, :], ACT.Square).then_inc(ksq_ready, 1)
                act.wait_ge(kmean_done, x + 1)
                if x >= 2:
                    act.wait_ge(k_ready, 2 * (x - 1))
                A(std[:, x % 2, :], misc[0][:, 0:T], ACT.Sqrt, bias=eps[:, :]).then_inc(kmean_read, 1)
            with act.Fori(N_EXPERTS // 2, N_EXPERTS) as e:
                expert(e)

            load_table(ACT.Sqrt)
            act.wait_ge(down_done, N_EXPERTS)
            squares(NMIX, lat, {3: lambda: piece_high(PIECE["q", 0], 1)})
            deviation(NMIX)
            piece_high(PIECE["q", 0] + 1, 3)
            input_high(NMIX)
            piece_high(PIECE["q", 1], 4)

            def u_copy(f):
                n = FILL["u"] + f
                fill_done(act, n)
                A(u_pad[:, 2 * f:2 * f + 2, PAD:UP], acc[n % 4][:, :].rearrange("p (g t) -> p g t", g=2), ACT.Copy) \
                    .then_inc(acc_free[n % 4], 1)
                act.wait_ge(acc_free[n % 4], n // 4 + 1)
                nc.scalar.nop().then_inc(u_ready, 1)

            def qk_gain(j):
                n = (FILL["q"], FILL["k"])[j // 2] + j % 2
                fill_done(act, n)
                if j >= 2:
                    act.wait_ge(qk_ready, j - 1)
                A(sq[:, j % 2, :], acc[n % 4][:, :], ACT.Square)
                A(qk_gs[j % 2], acc[n % 4][:, :], ACT.Copy, scale=vcol(("q_norm_g", "k_norm_g")[j // 2])) \
                    .then_inc(acc_free[n % 4], 1)
                act.wait_ge(acc_free[n % 4], n // 4 + 1)
                nc.scalar.nop().then_inc(qkg_ready, 1)

            def qk_deviation(j):
                act.wait_ge(qk_prep, j + 1)
                A(qk_stds[j % 2], misc[2 * (j % 2)][:, :], ACT.Sqrt, bias=eps[:, :]).then_inc(qk_std, 1)

            def v_copy(f):
                n = FILL["v"] + f
                fill_done(act, n)
                A(v_rows[:, :, f * T:(f + 1) * T], acc[n % 4][:, :].rearrange("p (i n) -> p i n", i=TT), ACT.Copy) \
                    .then_inc(acc_free[n % 4], 1)
                act.wait_ge(acc_free[n % 4], n // 4 + 1)
                nc.scalar.nop().then_inc(v_ready, 1)

            for j, fill in ((0, ("k", 0)), (1, ("u", 0)), (2, ("u", 1))):
                qk_gain(j)
                piece_high(PIECE[fill], 2)
                qk_deviation(j)
                piece_high(PIECE[fill] + 2, 2)
            u_copy(0)
            piece_high(PIECE["k", 1], 4)
            u_copy(1)
            piece_high(PIECE["v", 0], 4)
            qk_gain(3)
            qk_deviation(3)
            load_table(ACT.Exp)
            piece_high(PIECE["v", 1], 4)
            for f in range(2):
                n = FILL["pool"] + f
                fill_done(act, n)
                for j in range(2):
                    g = 2 * f + j
                    last = A(y_hi[:, g, :], acc[n % 4][:, j * T:(j + 1) * T], ACT.Copy, scale=vcol("pool_scale", g, 1))
                last.then_inc(y_hi_ready, 1)
            v_copy(0)
            v_copy(1)
            for a in range(HEADS + 4):
                if 2 <= a < HEADS + 2:
                    act.wait_ge(probt_done, a - 1)
                    if a >= 4:
                        act.wait_ge(pv_done, a - 3)
                    A(prob_t[:, a % 2, :], misc[0][:, 0:3 * P], ACT.Copy).then_inc(probt_ready, 1)
                if a < HEADS:
                    act.wait_ge(negmax, a + 1)
                    at = 4 * (a % 2)
                    for i, (lo, hi) in enumerate(((0, P), (P, 3 * P))):
                        A(prob[:, a % 3, lo:hi], prob[:, a % 3, lo:hi], ACT.Exp, scale=HD ** -0.5,
                          bias=stat[:, at + i:at + i + 1], accum_out=stat[:, at + 2 + i:at + 3 + i]).then_inc(prob_exp, 1)
                if a + 1 in MIX_STEP:
                    piece_high(PIECE["mix_out", MIX_STEP.index(a + 1)], 2)
                if a % 2 and 3 <= a < HEADS + 2:
                    p = (a - 3) // 2
                    act.wait_ge(pv_done, 2 * p + 2)
                    A(y_hi[:, PG + p, :], misc[1][:, (p % 2) * T:(p % 2 + 1) * T], ACT.Copy).then_inc(y_hi_ready, 1)
            load_table(ACT.Sqrt)
            piece_high(PIECE["xq", 0], 2)
            squares(NXATT, lat, {2: lambda: piece_high(PIECE["xq", 0] + 2, 1)})
            piece_high(PIECE["xq", 0] + 3, 1)
            deviation(NXATT)
            input_high(NXATT)
            piece_high(PIECE["xq", 1], 4)
            for x in range(XHEADS):
                n = FILL["xq"] + x
                fill_done(act, n)
                if x >= 2:
                    act.wait_ge(xmean_done, x - 1)
                A(sq[:, x % 2, :], acc[n % 4][:, :], ACT.Square).then_inc(xsq_ready, 1)
                if x + 2 < XHEADS:
                    piece_high(PIECE["xq", x + 2], 4)
                act.wait_ge(xmean_done, x + 1)
                if x >= 2:
                    act.wait_ge(xq_ready, x - 1)
                A(std[:, x % 2, :], misc[0][:, 0:T], ACT.Sqrt, bias=eps[:, :]).then_inc(xstd_ready, 1)
            load_table(ACT.Exp)

            def o_high(x):
                act.wait_ge(xpv_done, x + 1)
                A(y_hi[:, 2 * x:2 * x + 2, :], misc[1][:, :], ACT.Copy).then_inc(y_hi_ready, 1)

            for x in range(XHEADS):
                act.wait_ge(xnegmax, x + 1)
                at = 4 * (x % 2)
                if x >= 2:
                    act.wait_ge(xprobt_done, x - 1)
                for i in range(TT):
                    A(xprob[:, x % 2, i * T:(i + 1) * T], misc[2 + x % 2][:, i * T:(i + 1) * T], ACT.Exp,
                      scale=XHD ** -0.5, bias=stat[:, at + i:at + i + 1], accum_out=stat[:, at + 2 + i:at + 3 + i])
                act.drain().then_inc(xexp, 1)
                if x == 0:
                    piece_high(PIECE["xo", 0], 4)
                if x >= 2:
                    o_high(x - 2)
            piece_high(PIECE["xo", 2], 4)
            piece_high(PIECE["xo", 4], 2)
            o_high(2)
            piece_high(PIECE["xo", 5], 2)
            o_high(3)
            piece_high(PIECE["xo", 6], 4)

            def ffn_high(par, part, loads):
                if part < 2:
                    act.wait_ge(ffn_up_in[par], loads * 32)
                else:
                    act.wait_ge(ffn_down_in[par], loads * 16)
                A(ffn_hi[par][:, part, :], ffn_raw(par, part), ACT.Copy).then_inc(w_hi[part], 1)

            act.wait_ge(piece_lo_ready, len(PIECES))
            ffn_high(0, 0, 1)
            ffn_high(0, 1, 1)
            load_table(ACT.Sqrt)
            squares(NFFN, lat)
            deviation(NFFN)
            input_high(NFFN)
            ffn_high(0, 2, 1)
            ffn_high(1, 0, 1)
            ffn_high(1, 1, 1)

            def ffn_step(s, par, loads, last=0):
                act.wait_ge(up2_done, s + 1)
                for g in range(2):
                    w = vec[:, bass.ds(s + (VEC["conv_w"][0] + 2 * 2 * FC + g * FC), 1)]
                    b = vec[:, bass.ds(s + (VEC["conv_b"][0] + g * FC), 1)]
                    z = A(up_z[:, par, g, :], misc[par][:, g * T:(g + 1) * T], ACT.Identity, scale=w, bias=b)
                z.then_inc(z_ready, 1)
                if last < 1:
                    ffn_high(par, 0, loads + 1)
                act.wait_ge(conv2_done, s + 1)
                A(up_s[:, par, :], up_z[:, par, 0, :], ACT.Silu).then_inc(silu2_ready, 1)
                if last < 1:
                    ffn_high(par, 1, loads + 1)
                if last < 2:
                    if not isinstance(s, int) or s:
                        act.wait_ge(down2_done, s)
                    ffn_high(1 - par, 2, loads + par)

            ffn_step(0, 0, 1)
            ffn_step(1, 1, 1)
            with act.Fori(1, FC // 2 - 1) as i:
                ffn_step(i * 2, 0, i + 1)
                ffn_step(i * 2 + 1, 1, i + 1)
            ffn_step(FC - 2, 0, FC // 2, last=1)
            ffn_step(FC - 1, 1, FC // 2, last=2)

        @block.vector
        def _(ve):
            V = nc.vector
            n_chain = [0]

            def then(ins):
                ins.then_inc(dve, 1)
                n_chain[0] += 1
                ve.wait_ge(dve, n_chain[0])

            def norm(n_norm, src, dst, gain, scaled, base=0):
                ve.wait_ge(mean_free, n_norm + 1)
                then(V.reciprocal(rstd[:, :], std[:, n_norm % 2, :]))
                for k in range(KC):
                    V.scalar_tensor_tensor(out=dst[:, k, :], in0=src[:, k, :], scalar=gain[:, k:k + 1], in1=rstd[:, :],
                                           op0=ALU.mult, op1=ALU.mult).then_inc(scaled, 1)

            def piece_low(q, n=1):
                for q in range(q, q + n):
                    ve.wait_ge(piece_hi_ready, q + 1)
                    V.tensor_tensor(piece_part(1, q), piece_raw(q), piece_part(0, q), ALU.subtract) \
                        .then_inc(piece_lo_ready, 1)

            def split_norm(n_norm, gain, base, x_lo=x_lo, shift=None, between=None):
                def x_low(k):
                    ve.wait_ge(x_hi_ready, base + k + 1)
                    if shift is None:
                        ins = V.tensor_tensor(x_lo[:, k, :], h[:, k, :], x_hi[:, k, :], ALU.subtract)
                    else:
                        ins = V.scalar_tensor_tensor(out=x_lo[:, k, :], in0=h[:, k, :], scalar=shift[:, k:k + 1],
                                                     in1=x_hi[:, k, :], op0=ALU.add, op1=ALU.subtract)
                    ins.then_inc(x_lo_ready, 1)

                for k in range(KC):
                    V.scalar_tensor_tensor(out=h[:, k, :], in0=lat[:, k, :], scalar=gain[:, k:k + 1], in1=rstd[:, :],
                                           op0=ALU.mult, op1=ALU.mult) \
                        .then_inc(h_ready[n_norm] if shift is None else h_scaled, 1)
                    if k:
                        x_low(k - 1)
                    if k == 4 and between:
                        between()
                x_low(KC - 1)

            def inverse_deviation(n_norm):
                ve.wait_ge(mean_free, n_norm + 1)
                then(V.reciprocal(rstd[:, :], std[:, n_norm % 2, :]))

            def ada_read_block(j):
                ve.wait_ge(ada_t_done, j + 1)
                first_copy = misc[2][:, 0:256].rearrange("p (c j s) -> p j c s", c=2, j=4)[:, :, :, 0]
                at = j * KC
                V.tensor_tensor(mod[:, at:at + KC].rearrange("p (j c) -> p j c", c=2), first_copy,
                                vcol("ada_b", at, KC).rearrange("p (j c) -> p j c", c=2), ALU.add) \
                    .then_inc(ada_read, 1)
                ve.wait_ge(ada_read, j + 1)

            ve.wait_ge(s_vec, 16)
            for f in range(4):
                n = FILL["x_t"] + f
                fill_done(ve, n)
                V.tensor_copy(lat[:, 2 * f:2 * f + 2, :], acc[n % 4][:, :].rearrange("p (c t) -> p c t", c=2)) \
                    .then_inc(acc_free[n % 4], 1)
                ve.wait_ge(acc_free[n % 4], n // 4 + 1)
                V.engine_nop().then_inc(lat_ready[N1], 1)
            ve.wait_ge(mean_free, 1)
            then(V.reciprocal(rstd[:, :], std[:, 0, :]))
            ada_read_block(0)
            ada_read_block(1)
            then(V.scalar_tensor_tensor(out=gain1[:, :], in0=mod[:, KC:2 * KC], scalar=1.0, in1=vcol("norm_g", 0, KC),
                                        op0=ALU.add, op1=ALU.mult))
            split_norm(N1, gain1, 0, y_lo, mod[:, 0:KC], lambda: piece_low(PIECE["conv_b", 0], 2))
            piece_low(PIECE["conv_b", 0] + 2, 4 * 9 - 2)
            ada_read_block(2)
            ve.wait_ge(cv_zeroed, 2)
            cw = vcol("sc_conv").rearrange("p (w k) -> p w k", w=3)
            for f in range(4):
                n = FILL["conv_v"] + f
                pair = slice(2 * f, 2 * f + 2)
                piece_low(PIECE["conv_v", 0] + 4 * (f + 1), 4)
                ve.wait_ge(acc_free[(FILL["conv_c"] + f) % 4], (FILL["conv_c"] + f) // 4 + 1)
                fill_done(ve, n)
                V.tensor_tensor(cv[:, pair, 1:T + 1], acc[n % 4][:, :].rearrange("p (c t) -> p c t", c=2),
                                gate_c[:, pair, :], ALU.mult).then_inc(acc_free[n % 4], 1)
                ve.wait_ge(acc_free[n % 4], n // 4 + 1)
                for k in range(2 * f, 2 * f + 2):
                    ins = V.tensor_scalar(conv[:, k, :], cv[:, k, 0:T], cw[:, 0, k:k + 1], None, ALU.mult)
                    if k % 2:
                        then(ins)
                for w in (1, 2):
                    for k in range(2 * f, 2 * f + 2):
                        ins = V.scalar_tensor_tensor(out=conv[:, k, :], in0=cv[:, k, w:w + T], scalar=cw[:, w, k:k + 1],
                                                     in1=conv[:, k, :], op0=ALU.mult, op1=ALU.add)
                        if k % 2 and (w == 1 or f == 3):
                            then(ins)
                        elif k % 2:
                            ins.then_inc(conv_summed, 1)
                if f == 3:
                    ve.wait_ge(conv_ready, 6)
                    V.tensor_tensor(conv[:, pair, :], conv[:, pair, :], gate_b[:, pair, :], ALU.mult).then_inc(conv_ready, 2)
            for f in range(4):
                pair = slice(2 * f, 2 * f + 2)
                ve.wait_ge(x_hi_ready, KC + 2 * f + 2)
                V.tensor_tensor(y_lo[:, pair, :], conv[:, pair, :], x_hi[:, pair, :], ALU.subtract).then_inc(x_lo_ready, 2)
            piece_low(PIECE["conv_out", 1], 4)
            for f in range(4):
                if f < 2:
                    piece_low(PIECE["conv_out", f + 2], 4)
                n = FILL["conv_out"] + f
                fill_done(ve, n)
                for c in range(2):
                    k = 2 * f + c
                    last = V.scalar_tensor_tensor(out=lat[:, k, :], in0=acc[n % 4][:, c * T:(c + 1) * T],
                                                  scalar=mod[:, 2 * KC + k:2 * KC + k + 1], in1=lat[:, k, :],
                                                  op0=ALU.mult, op1=ALU.add)
                last.then_inc(acc_free[n % 4], 1)
                ve.wait_ge(acc_free[n % 4], n // 4 + 1)
                V.engine_nop().then_inc(lat_ready[N2], 1)
            ada_read_block(3)
            ada_read_block(4)
            then(V.scalar_tensor_tensor(out=gain2[:, :], in0=mod[:, 4 * KC:5 * KC], scalar=1.0, in1=vcol("norm_g", KC, KC),
                                        op0=ALU.add, op1=ALU.mult))
            norm(N2, lat, h, gain2, h_scaled)
            ve.wait_ge(logits_done, 1)
            V.tensor_reduce(stat[:, 4:5], logits[0], AX, ALU.max)
            then(V.tensor_reduce(stat[:, 5:6], logits[1], AX, ALU.max))
            V.tensor_scalar(stat[:, 0:2], stat[:, 4:6], -1.0, None, ALU.mult).then_inc(negmax_r, 1)
            ve.wait_ge(exp_done, 2)
            then(V.reciprocal(stat[:, 6:8], stat[:, 2:4]))
            for i in range(TT):
                last = V.tensor_scalar(aff[:, i, :], aff_e[:, i, :], stat[:, 6 + i:7 + i], None, ALU.mult)
            last.then_inc(aff_ready, 1)
            V.memset(ones_r, 1.0)
            ve.wait_ge(afft_done, 1)
            then(V.tensor_copy(top_work[:, :], misc[2][0:N_EXPERTS, 0:T]))
            for r in range(CAP // 8):
                then(V.max(top8[:, :], top_work[:, :]))
                then(V.match_replace(top_work[:, :], top8[:, :], top_work[:, :], -1.0))
            then(V.tensor_scalar(chosen[:, :], top_work[:, :], 0.0, None, ALU.is_lt))
            then(V.tensor_tensor_scan(count[:, :], ones_r[:, :], chosen[:, :], 0.0, ALU.mult, ALU.add))
            then(V.tensor_tensor(slot_t[:, :], count[:, :], chosen[:, :], ALU.mult))
            V.tensor_scalar(slot_t[:, :], slot_t[:, :], -1.0, None, ALU.add).then_inc(slot_t_ready, 1)
            ve.wait_ge(slot_done, 1)
            then(V.tensor_copy(slot[:, :, :], misc[3][:, 0:TT * N_EXPERTS].rearrange("p (i e) -> p i e", i=TT)))
            ada_read_block(5)
            iota = table("iota")[:, None, :].to_broadcast([P, N_EXPERTS, CAP])
            for i in range(TT):
                last = V.tensor_tensor(sel[:, i, :, :], iota, slot[:, i, :, None].to_broadcast([P, N_EXPERTS, CAP]),
                                       ALU.is_equal)
            last.then_inc(sel_ready, 1)
            ve.wait_ge(sel_ready, 1)

            def gate_pair(p):
                if p >= 2:
                    ve.wait_ge(scat_t_done, p - 1)
                for i in range(TT):
                    for j in range(2):
                        e = 2 * p + j
                        last = V.tensor_scalar(sel_g[:, p % 2, i, j, :, :],
                                               sel[:, i, e, None, :].to_broadcast([P, 4, CAP]),
                                               aff[:, i, e:e + 1], None, ALU.mult)
                last.then_inc(selg_ready, 1)

            gate_pair(0)
            gate_pair(1)
            for k in range(1, KC, 2):
                n = FILL["gather"] + k
                fill_done(ve, n)
                V.tensor_copy(xs[:, k, :], acc[n % 4][:, :]).then_inc(acc_free[n % 4], 1)
            for b in range(4):
                n = FILL["gather"] + 4 + b
                ve.wait_ge(acc_free[n % 4], n // 4 + 1)

            def expert_in(e):
                V.tensor_copy(xs_e[:, :, :], xs[:, :, bass.ds(e * CAP, CAP)]).then_inc(xse_ready, 1)
                if isinstance(e, int):
                    for p in range(2, N_EXPERTS // 2):
                        gate_pair(p)
                ve.wait_ge(silu_ready, e + 1)
                ve.wait_ge(up_done, e + 1)
                V.tensor_tensor(hid, silu_g, misc[1][:, 0:256], ALU.mult).then_inc(hid_ready, 1)

            def expert_out(e, values):
                ve.wait_ge(kvw_used, e + 1)
                if not values:
                    V.tensor_copy(k_mem[:, bass.ds(e, 1), :], misc[0][:, None, 0:T]).then_inc(kv_read, 1)
                else:
                    V.tensor_copy(v_mem[:, :, bass.ds((e - N_EXPERTS // 2) * P, P)],
                                  misc[0][:, 0:T].rearrange("p (i n) -> p i n", i=TT)).then_inc(kv_read, 1)
                ve.wait_ge(scat_free, e + 1)
                V.tensor_copy(scat_e[:, None, :], scatter[:, bass.ds(e, 1), :]).then_inc(scate_ready, 1)

            expert_in(0)
            for b in range(4):
                V.memset(acc[b][:, :], 0.0).then_inc(y_zeroed, 1)
            norm(NMEM, mem_n, mem_n, vcol("norm_mem_g"), h_ready[NMEM])
            expert_out(0, False)

            with ve.Fori(1, N_EXPERTS // 2) as e:
                expert_in(e)
                expert_out(e, False)
            for x in range(XHEADS):
                ve.wait_ge(kmean_read, x + 1)
                then(V.reciprocal(rstd[:, :], std[:, x % 2, :]))
                for c in range(2):
                    k = 2 * x + c
                    V.scalar_tensor_tensor(out=k_mem[:, k, :], in0=k_mem[:, k, :], scalar=vcol("xk_norm_g", c, 1),
                                           in1=rstd[:, :], op0=ALU.mult, op1=ALU.mult).then_inc(k_ready, 1)
                ve.wait_ge(k_ready, 2 * x + 2)
            with ve.Fori(N_EXPERTS // 2, N_EXPERTS) as e:
                expert_in(e)
                expert_out(e, True)
            ve.wait_ge(scat_free, N_EXPERTS + 1)
            for k in range(KC):
                ins = V.scalar_tensor_tensor(out=lat[:, k, :], in0=acc[k // 2][:, (k % 2) * T:(k % 2 + 1) * T],
                                             scalar=mod[:, 5 * KC + k:5 * KC + k + 1], in1=lat[:, k, :],
                                             op0=ALU.mult, op1=ALU.add)
                if k % 2:
                    ins.then_inc(lat_ready[NMIX], 1)
            piece_low(PIECE["q", 0], 1)
            inverse_deviation(NMIX)
            split_norm(NMIX, vcol("norm_mix_g"), 2 * KC, between=lambda: piece_low(PIECE["q", 0] + 1, 1))
            piece_low(PIECE["q", 0] + 2, 2)
            piece_low(PIECE["q", 1], 4)
            piece_low(PIECE["k", 0], 4)

            def two(ap):
                return ap[:, None, :].to_broadcast([P, 2, T])

            for j in range(4):
                dst = (q_rot, k_rot)[j // 2][:, 2 * (j % 2):2 * (j % 2) + 2, :]
                t3 = qk_t.rearrange("p (c t) -> p c t", c=2)
                ve.wait_ge(qk_prep, j + 1)
                V.tensor_tensor(dst, misc[2 * (j % 2) + 1][:, :].rearrange("p (c t) -> p c t", c=2), two(table("sin")),
                                ALU.mult).then_inc(qk_read, 1)
                then(V.tensor_tensor(t3, qk_gs[j % 2].rearrange("p (c t) -> p c t", c=2), two(table("cos")), ALU.mult))
                ve.wait_ge(qk_read, j + 1)
                V.tensor_tensor(dst, dst, t3, ALU.add)
                piece_low(PIECE[(("u", 0), ("u", 1), ("k", 1), ("v", 1))[j]], 4 if j == 3 else 2)
                ve.wait_ge(qk_std, j + 1)
                then(V.reciprocal(region_s[:, 512:1024], qk_stds[j % 2]))
                V.tensor_tensor(dst, dst, region_s[:, 512:1024].rearrange("p (c t) -> p c t", c=2), ALU.mult) \
                    .then_inc(qk_ready, 1)
                ve.wait_ge(qk_ready, j + 1)
                if j < 3:
                    piece_low(PIECE[(("u", 0), ("u", 1), ("k", 1))[j]] + 2, 6 if j == 2 else 2)
            for f in range(2):
                n = FILL["pool"] + f
                ve.wait_ge(y_hi_ready, f + 1)
                for j in range(2):
                    g = 2 * f + j
                    last = V.scalar_tensor_tensor(out=y_lo[:, g, :], in0=acc[n % 4][:, j * T:(j + 1) * T],
                                                  scalar=vcol("pool_scale", g, 1), in1=y_hi[:, g, :],
                                                  op0=ALU.mult, op1=ALU.subtract)
                last.then_inc(y_lo_ready, 1)
            def mix_zero(f):
                n = FILL["mix_out"] + f
                if n - 4 < FILL["pool"]:
                    ve.wait_ge(acc_free[n % 4], n // 4)
                else:
                    ve.wait_ge(y_lo_ready, n - 4 - FILL["pool"] + 1)
                V.memset(acc[n % 4][:, :], 0.0).then_inc(mix_zeroed, 1)

            mix_zero(2)
            mix_zero(3)
            for a in range(HEADS + 4):
                if a < HEADS:
                    s = prob[:, a % 3, :]
                    at = 4 * (a % 2)
                    ve.wait_ge(score_done, a + 1)
                    if a >= 3:
                        ve.wait_ge(probt_done, a - 2)
                    V.tensor_tensor(s, misc[2 + a % 2][:, 0:3 * P], table("causal"), ALU.add).then_inc(masked, 1)
                    ve.wait_ge(masked, a + 1)
                    V.tensor_reduce(stat[:, 16:17], s[:, 0:P], AX, ALU.max)
                    then(V.tensor_reduce(stat[:, 17:18], s[:, P:3 * P], AX, ALU.max))
                    V.tensor_scalar(stat[:, at:at + 2], stat[:, 16:18], -HD ** -0.5, None, ALU.mult).then_inc(negmax, 1)
                if 1 <= a <= HEADS:
                    s = prob[:, (a - 1) % 3, :]
                    at = 4 * ((a - 1) % 2)
                    ve.wait_ge(prob_exp, 2 * a)
                    then(V.reciprocal(stat[:, 18:20], stat[:, at + 2:at + 4]))
                    V.tensor_scalar(s[:, 0:P], s[:, 0:P], stat[:, 18:19], None, ALU.mult)
                    V.tensor_scalar(s[:, P:3 * P], s[:, P:3 * P], stat[:, 19:20], None, ALU.mult).then_inc(prob_ready, 1)
                if a in MIX_STEP:
                    piece_low(PIECE["mix_out", MIX_STEP.index(a)], 2)
                if a == 1:
                    mix_zero(0)
                    mix_zero(1)
                if a % 2 and 3 <= a < HEADS + 2:
                    p = (a - 3) // 2
                    ve.wait_ge(y_hi_ready, 2 + p + 1)
                    V.tensor_tensor(y_lo[:, PG + p, :], misc[1][:, (p % 2) * T:(p % 2 + 1) * T], y_hi[:, PG + p, :],
                                    ALU.subtract).then_inc(y_lo_ready, 1)

            def add_to_lat(name, ready, before={}):
                for f in range(4):
                    if f in before:
                        before[f]()
                    n = FILL[name] + f
                    fill_done(ve, n)
                    V.tensor_tensor(lat[:, 2 * f:2 * f + 2, :], acc[n % 4][:, :].rearrange("p (c t) -> p c t", c=2),
                                    lat[:, 2 * f:2 * f + 2, :], ALU.add).then_inc(ready, 1)
                ve.wait_ge(ready, 4)

            piece_low(PIECE["xq", 0], 2)
            add_to_lat("mix_out", lat_ready[NXATT], {2: lambda: piece_low(PIECE["xq", 0] + 2, 1)})
            piece_low(PIECE["xq", 0] + 3, 1)
            inverse_deviation(NXATT)
            split_norm(NXATT, vcol("norm_xattn_g"), 3 * KC)
            piece_low(PIECE["xq", 1], 4)
            def x_max(x):
                at = 4 * (x % 2)
                ve.wait_ge(xscore_done, x + 1)
                top = stat[:, 20 + 2 * (x % 2):22 + 2 * (x % 2)]
                then(V.tensor_reduce(top, misc[2 + x % 2][:, :].rearrange("p (i m) -> p i m", i=TT), AX, ALU.max))
                V.tensor_scalar(stat[:, at:at + 2], top, -XHD ** -0.5, None, ALU.mult).then_inc(xnegmax, 1)

            def xo_zero(f):
                V.memset(acc[(FILL["xo"] + f) % 4][:, :], 0.0).then_inc(xo_zeroed, 1)

            for x in range(XHEADS):
                n = FILL["xq"] + x
                if x + 2 < XHEADS:
                    piece_low(PIECE["xq", x + 2], 4)
                if x == XHEADS - 1:
                    xo_zero(0)
                    x_max(0)
                ve.wait_ge(xstd_ready, x + 1)
                then(V.reciprocal(rstd[:, :], std[:, x % 2, :]))
                for c in range(2):
                    last = V.scalar_tensor_tensor(out=q_x[:, 2 * x + c, :], in0=acc[n % 4][:, c * T:(c + 1) * T],
                                                  scalar=vcol("xq_norm_g", c, 1), in1=rstd[:, :],
                                                  op0=ALU.mult, op1=ALU.mult)
                last.then_inc(xq_ready, 1)
                ve.wait_ge(xq_ready, x + 1)

            def x_normalize(x):
                s = xprob[:, x % 2, :].rearrange("p (i m) -> p i m", i=TT)
                at = 4 * (x % 2)
                ve.wait_ge(xexp, x + 1)
                then(V.reciprocal(stat[:, 18:20], stat[:, at + 2:at + 4]))
                for i in range(TT):
                    last = V.tensor_scalar(s[:, i, :], s[:, i, :], stat[:, 18 + i:19 + i], None, ALU.mult)
                last.then_inc(xprob_ready, 1)

            def x_copy(x):
                ve.wait_ge(xprobt_done, x + 1)
                if x >= 2:
                    ve.wait_ge(xpv_done, x - 1)
                V.tensor_copy(xprob_t[:, x % 2, :], misc[0][:, :]).then_inc(xprobt_ready, 1)

            def o_low(x):
                ve.wait_ge(y_hi_ready, 6 + x + 1)
                V.tensor_tensor(y_lo[:, 2 * x:2 * x + 2, :], misc[1][:, :].rearrange("p (c t) -> p c t", c=2),
                                y_hi[:, 2 * x:2 * x + 2, :], ALU.subtract).then_inc(y_lo_ready, 1)

            x_max(1)
            x_normalize(0)
            xo_zero(1)
            x_copy(0)
            piece_low(PIECE["xo", 0], 2)
            x_max(2)
            x_normalize(1)
            xo_zero(2)
            x_copy(1)
            xo_zero(3)
            piece_low(PIECE["xo", 1], 2)
            o_low(0)
            x_max(3)
            x_normalize(2)
            o_low(1)
            piece_low(PIECE["xo", 2], 4)
            x_copy(2)
            x_normalize(3)
            piece_low(PIECE["xo", 4], 2)
            x_copy(3)
            o_low(2)
            piece_low(PIECE["xo", 5], 2)
            o_low(3)
            piece_low(PIECE["xo", 6], 4)

            def ffn_low(s, par, part):
                ve.wait_ge(w_hi[part], s + 1)
                V.tensor_tensor(ffn_lo[par][:, part, :], ffn_raw(par, part), ffn_hi[par][:, part, :], ALU.subtract) \
                    .then_inc(w_lo[part], 1)

            ffn_low(0, 0, 0)
            add_to_lat("xo", lat_ready[NFFN])
            for b in range(4):
                V.memset(acc[b][:, :], 0.0).then_inc(ffn_zeroed, 1)
            inverse_deviation(NFFN)
            split_norm(NFFN, vcol("norm_ffn_g"), 4 * KC)
            ffn_low(0, 0, 1)
            ffn_low(0, 0, 2)
            ffn_low(1, 1, 0)
            ffn_low(1, 1, 1)

            def ffn_step(s, par, base, last=0):
                ve.wait_ge(z_ready, s + 1)
                for w in (1, 0):
                    d = 2 - w
                    for g in range(2):
                        tap = vec[:, bass.ds(s + (VEC["conv_w"][0] + w * 2 * FC + g * FC), 1)]
                        ins = V.scalar_tensor_tensor(out=up_z[:, par, g, d:T], in0=misc[par][:, g * T:(g + 1) * T - d],
                                                     scalar=tap, in1=up_z[:, par, g, d:T], op0=ALU.mult, op1=ALU.add)
                    if w:
                        ins.then_inc(dve, 1)
                        ve.wait_ge(dve, s + base)
                ins.then_inc(conv2_done, 1)
                if last < 1:
                    ffn_low(s + 2, par, 0)
                ve.wait_ge(conv2_done, s + 1)
                ve.wait_ge(silu2_ready, s + 1)
                V.tensor_tensor(up_h[:, par, :], up_s[:, par, :], up_z[:, par, 1, :], ALU.mult).then_inc(hid_f, 1)
                if not isinstance(s, int) or s >= 2:
                    ve.wait_ge(down2_done, s - 1)
                V.tensor_tensor(act_hi[:, par, :], up_s[:, par, :], up_z[:, par, 1, :], ALU.mult).then_inc(act_hi_ready, 1)
                ve.wait_ge(hid_f, s + 1)
                ve.wait_ge(act_hi_ready, s + 1)
                V.tensor_tensor(act_lo[:, par, :], up_h[:, par, :], act_hi[:, par, :], ALU.subtract).then_inc(act_ready, 1)
                if last < 1:
                    ffn_low(s + 2, par, 1)
                if last < 2:
                    ffn_low(s + 1, 1 - par, 2)

            base = n_chain[0] + 1
            ffn_step(0, 0, base)
            ffn_step(1, 1, base)
            with ve.Fori(1, FC // 2 - 1) as i:
                ffn_step(i * 2, 0, base)
                ffn_step(i * 2 + 1, 1, base)
            ffn_step(FC - 2, 0, base, last=1)
            ffn_step(FC - 1, 1, base, last=2)
            for f in range(4):
                ve.wait_ge(ffn_done, f + 1)
                V.tensor_tensor(lat[:, 2 * f:2 * f + 2, :], acc[f][:, :].rearrange("p (c t) -> p c t", c=2),
                                lat[:, 2 * f:2 * f + 2, :], ALU.add).then_inc(lat_final, 1)
            for f in range(4):
                n = FILL["rows"] + f
                fill_done(ve, n)
                V.tensor_copy(out_rows[:, :, f * 256:(f + 1) * 256],
                              acc[n % 4][:, :].rearrange("p (i d) -> p i d", i=TT)).then_inc(out_ready, 1)


def _tables(np):
    tab = np.zeros((P, TAB_COLS), np.float32)

    def put(name, value):
        at, n = TAB[name]
        tab[:, at:at + n] = value

    put("ident", np.eye(P))
    put("iota", np.arange(CAP)[None])
    half = HD // 2
    rot = np.zeros((P, P))
    head = np.zeros((P, P))
    for m in range(P):
        base, j = m // HD * HD, m % HD
        if j < half:
            rot[base + j + half, m] = -1.0
        else:
            rot[base + j - half, m] = 1.0
        head[base:base + HD, m] = 1.0 / HD
    put("rot", rot)
    put("headmean", head)
    inv_freq = (np.float32(10000.0) ** (-np.arange(half, dtype=np.float32) / np.float32(half))).astype(np.float32)
    ang = (np.arange(T, dtype=np.float32)[None, :] * inv_freq[np.arange(P) % half][:, None]).astype(np.float32)
    put("cos", np.cos(ang.astype(np.float64)))
    put("sin", np.sin(ang.astype(np.float64)))
    q, k = np.arange(P)[:, None], np.arange(P)[None, :]
    diag = np.where(k <= q, 0.0, -1e30)
    put("causal", np.concatenate([diag, np.zeros((P, P)), diag], 1))
    put("invcnt", np.concatenate([1.0 / np.minimum(np.arange(PAD) + 1, w) for w in POOL_WINDOWS])[None])
    return tab


def kernel(**inputs):
    import numpy as np
    import concourse.bacc as bacc
    from concourse.bass_utils import run_bass_kernel_spmd

    a = {n: np.asarray(v) for n, v in inputs.items()}

    def cols(v):
        return v.reshape(-1, P).T

    vectors = np.concatenate([
        cols(a["c"]), cols(a["ada_b"]), cols(a["norm_g"]), cols(a["sc_conv"]), cols(a["norm_mem_g_2"]),
        a["moe_router"][0].reshape(KC, P, N_EXPERTS).transpose(1, 0, 2).reshape(P, -1),
        cols(a["norm_mix_g_2"]), cols(a["pool_scale_2"]),
        np.concatenate([a["q_norm_g_2"][0]] * 2)[:, None], np.concatenate([a["k_norm_g_2"][0]] * 2)[:, None],
        cols(a["norm_xattn_g_2"]), cols(a["xq_norm_g_2"]), cols(a["xk_norm_g_2"]), cols(a["norm_ffn_g_2"]),
        cols(a["conv_w_2"]), cols(a["conv_b_2"])], axis=1)
    arrays = {"vectors": vectors, "tables": _tables(np), "x": a["x"], "mem": a["mem_2"], "pool_w": a["pool_w_2"],
              "ada_w": a["ada_w"], "sc_w_in": a["sc_w_in"], "sc_w_out": a["sc_w_out"], "moe_w_gate": a["moe_w_gate"],
              "moe_w_up": a["moe_w_up"], "moe_w_down": a["moe_w_down"], "w_in": a["w_in_2"], "w_out": a["w_out_2"],
              "w_xq": a["w_xq_2"], "w_xkv": a["w_xkv_2"], "w_xo": a["w_xo_2"], "w_up": a["w_up_2"],
              "w_down": a["w_down_2"]}
    nc = bacc.Bacc("TRN2", target_bir_lowering=False, num_devices=1)
    feeds, io = {}, {}
    for name, v in arrays.items():
        v = np.ascontiguousarray(v)
        feeds[f"in_{name}"] = v
        io[name] = nc.dram_tensor(f"in_{name}", v.shape, F32, kind="ExternalInput").ap()
    io["out"] = nc.dram_tensor("out", (1, T, D), F32, kind="ExternalOutput").ap()
    program(nc, io)
    r = run_bass_kernel_spmd(nc, [feeds], core_ids=[0])
    return r.results[0]["out"]
```
